# Optimizing a Trainium2 kernel written in Bass

```python
import jax, jax.numpy as jnp
from jax import lax
import numpy as np

D_MODEL = 1024
BATCH = 1
SEQ = 128
DEPTH = 1
DEC_BATCH = 1
DEC_SEQ = 512
PAST_LEN = 128

GRID_W = 64
D_CONV = D_MODEL // 2
CONV_GROUPS = 8
CONV_WIDTH = 3
GLA_HEADS = 4
GLA_DV = (D_MODEL - D_CONV) // GLA_HEADS
GLA_DK = GLA_DV // 2
GLA_DK_TOT = GLA_HEADS * GLA_DK
GLA_DV_TOT = GLA_HEADS * GLA_DV
GLA_LOW_RANK = 16
GLA_TAU = 16.0
GLA_CHUNK = 64
N_EXPERTS = 16
EC_CAPACITY_FACTOR = 2
D_EXPERT = 1024
N_MOD = 6
EPS = 1e-6
SPLIT_SIZES = (D_CONV, D_CONV, D_CONV, GLA_DK_TOT, GLA_DK_TOT, GLA_DV_TOT, GLA_DV_TOT, 2 * GLA_LOW_RANK)
P_TOT = 3 * D_CONV + 2 * GLA_DK_TOT + 2 * GLA_DV_TOT + 2 * GLA_LOW_RANK

kernel_name = "hybrid_conv_gla_ec_moe_diffusion_step"

def _rmsnorm(x, g):
    xf = x.astype(jnp.float32)
    r = lax.rsqrt(jnp.mean(xf * xf, axis=-1, keepdims=True) + EPS)
    return (xf * r).astype(x.dtype) * g

def _centred_conv3(u, w, bias):
    pad = [(0, 0)] * (u.ndim - 2) + [(1, 1), (0, 0)]
    up = jnp.pad(u, pad)
    L = u.shape[-2]
    return up[..., :L, :] * w[0] + up[..., 1:L + 1, :] * w[1] + up[..., 2:, :] * w[2] + bias

def _gla_chunked(q, k, v, log_a, s0):
    Bn, H, T, DK = q.shape
    DV = v.shape[-1]
    C = GLA_CHUNK
    N = T // C
    f32 = jnp.float32
    q = q.astype(f32).reshape(Bn, H, N, C, DK) * (DK ** -0.5)
    k = k.astype(f32).reshape(Bn, H, N, C, DK)
    v = v.astype(f32).reshape(Bn, H, N, C, DV)
    b = jnp.cumsum(log_a.astype(f32).reshape(Bn, H, N, C, DK), axis=3)
    b_last = b[:, :, :, -1:, :]
    q_d = q * jnp.exp(b)
    k_d = k * jnp.exp(-b)
    k_s = k * jnp.exp(b_last - b)
    mask = jnp.tril(jnp.ones((C, C), dtype=bool))
    att = jnp.where(mask, jnp.einsum('bhncd,bhnsd->bhncs', q_d, k_d), 0.0)
    o_intra = jnp.einsum('bhncs,bhnsv->bhncv', att, v)
    kv = jnp.einsum('bhncd,bhncv->bhndv', k_s, v)
    decay = jnp.exp(b_last[:, :, :, 0, :])

    def step(s, inp):
        q_n, dec_n, kv_n = inp
        o = jnp.einsum('bhcd,bhdv->bhcv', q_n, s)
        s = dec_n[..., None] * s + kv_n
        return s, o

    s_fin, o_inter = lax.scan(step, s0.astype(f32),
                              (jnp.moveaxis(q_d, 2, 0), jnp.moveaxis(decay, 2, 0), jnp.moveaxis(kv, 2, 0)))
    o = o_intra + jnp.moveaxis(o_inter, 0, 2)
    return o.reshape(Bn, H, T, DV), s_fin

def _gla_bidir(q, k, v, la_f, la_b, s_f, s_b):
    o_f, sf = _gla_chunked(q, k, v, la_f, s_f)
    fl = lambda t: jnp.flip(t, axis=2)
    o_b, sb = _gla_chunked(fl(q), fl(k), fl(v), fl(la_b), s_b)
    return o_f + fl(o_b), sf, sb

def _mixer(h, s_f, s_b, grid, w_in, w_conv, b_conv, w_a_up_f, b_a_f, w_a_up_b, b_a_b, g_gla_norm, w_out):
    Bn, T, _ = h.shape
    p = h @ w_in
    offs = []
    acc = 0
    for s in SPLIT_SIZES[:-1]:
        acc += s
        offs.append(acc)
    xb, xc, xv, q, k, v, og, a_low = jnp.split(p, offs, axis=-1)
    u = xc * xv
    if grid:
        rows = T // GRID_W
        y_a = _centred_conv3(u.reshape(Bn, rows, GRID_W, D_CONV), w_conv, b_conv).reshape(Bn, T, D_CONV)
    else:
        y_a = _centred_conv3(u, w_conv, b_conv)
    y_a = xb * y_a
    heads = lambda t, d: jnp.transpose(t.reshape(Bn, T, GLA_HEADS, d), (0, 2, 1, 3))
    la_f = jax.nn.log_sigmoid((a_low[..., :GLA_LOW_RANK] @ w_a_up_f + b_a_f).astype(jnp.float32)) / GLA_TAU
    la_b = jax.nn.log_sigmoid((a_low[..., GLA_LOW_RANK:] @ w_a_up_b + b_a_b).astype(jnp.float32)) / GLA_TAU
    o, sf, sb = _gla_bidir(heads(q, GLA_DK), heads(k, GLA_DK), heads(v, GLA_DV),
                           heads(la_f, GLA_DK), heads(la_b, GLA_DK), s_f, s_b)
    o = o * lax.rsqrt(jnp.mean(o * o, axis=-1, keepdims=True) + EPS) * g_gla_norm[None, :, None, :].astype(jnp.float32)
    o = jnp.transpose(o, (0, 2, 1, 3)).reshape(Bn, T, GLA_DV_TOT).astype(h.dtype)
    y_b = o * jax.nn.silu(og)
    return jnp.concatenate([y_a, y_b], axis=-1) @ w_out, sf, sb

def _ec_moe(h, w_router, w_gate, w_up, w_down):
    Bn, T, _ = h.shape
    cap = EC_CAPACITY_FACTOR * T // N_EXPERTS
    probs = jax.nn.softmax((h @ w_router).astype(jnp.float32), axis=-1)
    gates, idx = lax.top_k(jnp.swapaxes(probs, 1, 2), cap)
    bidx = jnp.arange(Bn)[:, None, None]
    xs = h[bidx, idx]
    a = jax.nn.silu(jnp.einsum('becd,edf->becf', xs, w_gate)) * jnp.einsum('becd,edf->becf', xs, w_up)
    y = jnp.einsum('becf,efd->becd', a, w_down) * gates[..., None].astype(h.dtype)
    return jnp.zeros_like(h).at[bidx, idx].add(y)

def _layer(x, mod, s_f, s_b, grid, g_norm1, g_norm2, w_in, w_conv, b_conv, w_a_up_f, b_a_f,
           w_a_up_b, b_a_b, g_gla_norm, w_out, w_router, w_gate, w_up, w_down):
    shift1, scale1, gate1, shift2, scale2, gate2 = jnp.split(mod, N_MOD, axis=-1)
    h = _rmsnorm(x, g_norm1) * (1.0 + scale1) + shift1
    m, sf, sb = _mixer(h, s_f, s_b, grid, w_in, w_conv, b_conv, w_a_up_f, b_a_f, w_a_up_b, b_a_b, g_gla_norm, w_out)
    x = x + gate1 * m
    h = _rmsnorm(x, g_norm2) * (1.0 + scale2) + shift2
    x = x + gate2 * _ec_moe(h, w_router, w_gate, w_up, w_down)
    return x, sf, sb

def setup_inputs(seed: int = 0) -> dict:
    key = jax.random.key(seed)
    ks = jax.random.split(key, 24)
    nrm = lambda k, shape, s: jax.random.normal(k, shape, jnp.float32) * s
    D = D_MODEL
    return {
        "x_prompt": nrm(ks[0], (BATCH, SEQ, D), 1.0),
        "x_sample": nrm(ks[1], (DEC_BATCH, DEC_SEQ, D), 1.0),
        "state_gla_fwd": nrm(ks[2], (DEC_BATCH, DEPTH, GLA_HEADS, GLA_DK, GLA_DV), 0.5),
        "state_gla_bwd": nrm(ks[3], (DEC_BATCH, DEPTH, GLA_HEADS, GLA_DK, GLA_DV), 0.5),
        "c": nrm(ks[4], (DEC_BATCH, D), 1.0),
        "c_ctx": nrm(ks[5], (D,), 1.0),
        "w_mod": nrm(ks[6], (DEPTH, D, N_MOD * D), 0.5 * D ** -0.5),
        "b_mod": nrm(ks[7], (DEPTH, N_MOD * D), 0.02),
        "g_norm1": 1.0 + nrm(ks[8], (DEPTH, D), 0.02),
        "g_norm2": 1.0 + nrm(ks[9], (DEPTH, D), 0.02),
        "w_in": nrm(ks[10], (DEPTH, D, P_TOT), D ** -0.5),
        "w_conv": nrm(ks[11], (DEPTH, CONV_WIDTH, D_CONV), CONV_WIDTH ** -0.5),
        "b_conv": nrm(ks[12], (DEPTH, D_CONV), 0.02),
        "w_a_up_f": nrm(ks[13], (DEPTH, GLA_LOW_RANK, GLA_DK_TOT), GLA_LOW_RANK ** -0.5),
        "b_a_f": 1.0 + nrm(ks[14], (DEPTH, GLA_DK_TOT), 0.5),
        "w_a_up_b": nrm(ks[15], (DEPTH, GLA_LOW_RANK, GLA_DK_TOT), GLA_LOW_RANK ** -0.5),
        "b_a_b": 1.0 + nrm(ks[16], (DEPTH, GLA_DK_TOT), 0.5),
        "g_gla_norm": 1.0 + nrm(ks[17], (DEPTH, GLA_HEADS, GLA_DV), 0.02),
        "w_out": nrm(ks[18], (DEPTH, D, D), D ** -0.5),
        "w_router": nrm(ks[19], (DEPTH, D, N_EXPERTS), D ** -0.5),
        "w_gate": nrm(ks[20], (DEPTH, N_EXPERTS, D, D_EXPERT), D ** -0.5),
        "w_up": nrm(ks[21], (DEPTH, N_EXPERTS, D, D_EXPERT), D ** -0.5),
        "w_down": nrm(ks[22], (DEPTH, N_EXPERTS, D_EXPERT, D), D_EXPERT ** -0.5),
        "g_final": 1.0 + nrm(ks[23], (D,), 0.02),
    }

def reference(x_prompt, x_sample, state_gla_fwd, state_gla_bwd, c, c_ctx, w_mod, b_mod, g_norm1, g_norm2,
              w_in, w_conv, b_conv, w_a_up_f, b_a_f, w_a_up_b, b_a_b, g_gla_norm, w_out, w_router,
              w_gate, w_up, w_down, g_final):
    n_ctx = x_prompt.shape[0]
    zero_state = jnp.zeros((n_ctx, GLA_HEADS, GLA_DK, GLA_DV), jnp.float32)
    xp = x_prompt
    xs = x_sample
    new_f, new_b = [], []
    for l in range(DEPTH):
        lw = (g_norm1[l], g_norm2[l], w_in[l], w_conv[l], b_conv[l], w_a_up_f[l], b_a_f[l],
              w_a_up_b[l], b_a_b[l], g_gla_norm[l], w_out[l], w_router[l], w_gate[l], w_up[l], w_down[l])
        mod_ctx = (jax.nn.silu(c_ctx) @ w_mod[l] + b_mod[l])[None, None, :]
        xp, sf, sb = _layer(xp, mod_ctx, zero_state, zero_state, False, *lw)
        new_f.append(sf)
        new_b.append(sb)
        mod_lat = (jax.nn.silu(c) @ w_mod[l] + b_mod[l])[:, None, :]
        xs, _, _ = _layer(xs, mod_lat, state_gla_fwd[:, l], state_gla_bwd[:, l], True, *lw)
    y_prompt = _rmsnorm(xp, g_final)
    y_sample = _rmsnorm(xs, g_final)
    new_state_gla_fwd = jnp.stack(new_f, axis=1)
    new_state_gla_bwd = jnp.stack(new_b, axis=1)
    return (y_prompt, y_sample, new_state_gla_fwd, new_state_gla_bwd)


_drawn_inputs = setup_inputs


def setup_inputs(seed=0):
    import zlib

    import numpy as np

    out = dict(_drawn_inputs(seed))
    spreads = {}
    factors = {'state_gla_fwd': 8.0,
     'state_gla_bwd': 8.0,
     'g_norm2': 7.779,
     'b_conv': 8.0,
     'g_gla_norm': 8.0,
     'g_final': 2.898}
    for name, (base, spread) in spreads.items():
        noise = np.random.default_rng([zlib.crc32(name.encode()), seed]).standard_normal(out[name].shape)
        drawn = base * np.exp(spread * noise) if base else spread * noise
        out[name] = __import__('jax').numpy.asarray(drawn.astype(out[name].dtype))
    for name, factor in factors.items():
        out[name] = (out[name] * factor).astype(out[name].dtype)
    return out
```

```python
from contextlib import ExitStack

import concourse.bass as bass
from concourse import mybir

F32 = mybir.dt.float32
F32R = mybir.dt.float32r
U32 = mybir.dt.uint32
I32 = mybir.dt.int32
ALU = mybir.AluOpType
ACT = mybir.ActivationFunctionType
AX = mybir.AxisListType

P = 128
D = 1024
KC = D // P
T_LAT, T_CTX = 512, 128
T = T_LAT + T_CTX
NT = T // P
HALF = T // 2
GRID_W = 64
CH = D // 2 // P
H, DK, DV = 4, 64, 128
C = 64
NCH, NCH_LAT = T // C, T_LAT // C
LR = 16
TAU = 16.0
E = 16
CAP_L, CAP_C = 2 * T_LAT // E, 2 * T_CTX // E
SLOTS = CAP_L + CAP_C
NMOD = 6
EPS = 1e-6
P_TOT = 3 * 512 + 2 * H * DK + 2 * H * DV + 2 * LR

R_BMOD, R_G1, R_G2, R_C, R_CONV, R_BCONV, R_GLA, R_BA = 0, 48, 56, 64, 80, 92, 96, 100
R_ALL = 104

WORK = 16512
RING_SLOTS = 8
SLOT = 4 * D * 4
RING = 229368 // 32 * 32 - RING_SLOTS * SLOT
A_X = WORK
A_CONST = A_X + 20480
A_G2B = A_CONST + 3680
A_GFIN = A_G2B + 8192
A_P2 = A_GFIN + 4096
R_HT = RING
R_U = R_HT + 20480
R_QD = R_U + 10240
R_KD = R_QD + 10240
R_KST = R_KD + 10240
R_V = R_KST + 10240
R_ATT = R_V + 10240
R_FIN = R_ATT + 8192
P1_SLOT0 = 5
W_YT = A_P2
W_QK = W_YT + 10240
W_G1B = W_YT + 20480
W_XR = W_G1B + 8192
W_H2T1 = W_XR + 8192
B_XS = A_P2
B_XT = B_XS + 8192
B_G = B_XT + 6144
B_GC = B_G + 2048
B_AT = B_GC + 2048
B_ATC = B_AT + 2048
B_Y = B_ATC + 1024
B_YH = B_Y + 8192
B_OH = B_YH + 8192
B_IOTA = B_OH + 5120
assert B_IOTA + 2048 <= RING and W_H2T1 + 4096 <= RING


def first_phase_jobs():
    jobs = ["prm", "mod0", "mod1", "modT0", "mod2", "modT1", "mod3", "modT2", "modT3"]
    jobs += [f"xT{t}" for t in range(NT)]
    jobs += ["alow", "q0", "k0", "la0", "la1"]
    jobs += [f"v{t}" for t in range(NT)]
    jobs += ["ks0", "ks1", "q1", "k1", "la2", "la3"]
    jobs += [f"xc{j}" for j in range(CH)] + ["ks2", "ks3"]
    jobs += [f"xv{j}" for j in range(CH)] + [f"xb{j}" for j in range(CH)] + [f"og{j}" for j in range(H)]
    jobs += [f"kv{n}" for n in KV_ORDER]
    jobs += ["att0", "att1", "mod4", "mod5", "modT4", "mod6", "modT5", "mod7", "modT6", "mod8", "modT7", "mod9",
             "modT8", "modT9"]
    jobs += ["o0", "att2", "o1", "oT0", "att3", "o2", "oT1", "att4", "o3", "oT2", "g1_0", "o4", "oT3", "g1_1", "oT4"]
    jobs += ["wo0", "wo1", "x2T0", "wo2", "lg0", "x2T1", "wo3", "lg1", "x2T2", "wo4", "lg2", "x2T3", "mod10", "lg3",
             "modT10", "x2T4", "lg4", "mod11", "modT11", "pT", "g2_0", "g2_1", "ixT"]
    return jobs


KV_ORDER = [0, 7, 1, 6, 2, 5, 3, 4, 8, 9]
JOBS = first_phase_jobs()
UNITS = (["mod0", "mod1", "mod2", "mod3", "qk", "v", "xc", "xv", "xb", "og"]
         + [f"mod{u}" for u in range(4, 10)] + ["wo0", "wo1", "mod10", "mod11"])
IN_COLS = {"xb": 0, "xc": 512, "xv": 1024, "qk": 1536, "v": 2048, "og": 2560}


def job(name):
    return JOBS.index(name)


def build(nc, x_prompt, x_sample, s_fwd, s_bwd, c, c_ctx, w_mod, b_mod, g_norm1, g_norm2, w_in, w_conv, b_conv,
          w_a_up_f, b_a_f, w_a_up_b, b_a_b, g_gla_norm, w_out, w_router, w_gate, w_up, w_down, g_final,
          y_prompt, y_sample, new_f, new_b):
    ctx = ExitStack()
    with ctx:
        def at(name, offset, shape, dt=F32):
            return nc.alloc_sbuf_tensor_at(name, shape, dt, offset=offset)

        def sem(name):
            return ctx.enter_context(nc.semaphore(name))

        const_next = [A_CONST]

        def small(name, shape, dt=F32):
            n = 4
            for s in shape[1:]:
                n *= s
            t = at(name, const_next[0], shape, dt)
            const_next[0] += (n + 31) // 32 * 32
            assert const_next[0] <= A_G2B
            return t

        x_sb = at("x_sb", A_X, [P, NT, D])
        ident = small("ident", [P, P])
        param = small("param", [P, R_ALL])
        mod = small("mod", [P, NMOD * KC, 2])
        scale1 = small("scale1", [P, KC, 2])
        scale2 = small("scale2", [P, KC, 2])
        eps_col = small("eps_col", [P, 1])
        one_col = small("one_col", [P, 1])
        rms = small("rms", [P, 6, NT])
        hrms = small("hrms", [P, 6, H])
        dec = small("dec", [P, H, NCH])
        smax = small("smax", [P, 3, NT])
        gather_idx = small("gather_idx", [P, E], U32)
        pair_cols = small("pair_cols", [P, 8, E // 2])
        logits = small("logits", [P, NT, E])
        w_router_sb = small("w_router_sb", [P, KC, E])

        gate2b = at("gate2b", A_G2B, [P, 2, D])
        gfin = at("gfin", A_GFIN, [P, D])

        hT = at("hT", R_HT, [P, KC, T])
        states = at("states", R_HT, [P, NCH, H, DV])
        u_sb = at("u_sb", R_U, [P, CH, T])
        og_sb = at("og_sb", R_U, [P, H, T])
        qd = at("qd", R_QD, [P, H, T])
        kd = at("kd", R_KD, [P, H, T])
        ksT = at("ksT", R_KST, [P, NT, H, P])
        v_sb = at("v_sb", R_V, [P, NT, H * DV])
        att_sb = at("att_sb", R_ATT, [P, 2, 2, H, P])
        final_state = at("final_state", R_FIN, [P, H, DV])
        p1w = [at(f"p1w{i}", RING + (P1_SLOT0 + i) * SLOT, [P, KC, 512]) for i in range(3)]
        yT = at("yT", W_YT, [P, KC, T])
        qk_rep = at("qk_rep", W_QK, [P, 2, 2, T])
        gate1b = at("gate1b", W_G1B, [P, 2, D])
        work_d = at("work_d", W_G1B, [P, T])
        scan_mask = at("scan_mask", W_G1B + 2560, [P, T])
        a_lowT = at("a_lowT", W_G1B + 5120, [P, T])
        xr = at("xr", W_XR, [P, 2, D])
        work_a = at("work_a", W_H2T1, [P, T])
        norm_r = at("norm_r", W_H2T1, [P, H * P])
        keep_f = at("keep_f", W_H2T1 + 2560, [P, P])
        keep_b = at("keep_b", W_H2T1 + 3072, [P, P])
        param_rows = at("param_rows", W_H2T1 + 3584, [R_ALL, P])
        w_tail = at("w_tail", A_GFIN, [P, KC, 2 * LR])
        work_b = at("work_b", A_GFIN + 1024, [P, T])
        silu_c = at("silu_c", A_G2B + 6144 , [P, KC, 32])
        w_decay = at("w_decay", A_G2B, [P, H, P])
        mod_rows = at("mod_rows", A_G2B + 2048, [P, 2, 512])
        norm_sq = at("norm_sq", A_GFIN + 1024, [P, H * P])
        h2T = [at("h2T_0", A_GFIN, [P, KC, P]), at("h2T_1", W_H2T1, [P, KC, P])]

        ring = [at(f"ring{i}", RING + i * SLOT, [P, 4, D]) for i in range(RING_SLOTS)]
        xs = at("xs", B_XS, [SLOTS, 2, D])
        xT = at("xT", B_XT, [P, 2, KC, 96])
        act_l = at("act_l", B_G, [P, 512])
        act_c = at("act_c", B_GC, [P, 512])
        aT = at("aT", B_AT, [P, 4, P])
        aTc = at("aTc", B_ATC, [P, 4, 64])
        y_f = at("y_f", B_Y, [P, 2, 2, 512])
        y_lo = at("y_lo", B_Y, [P, 2, 2, 512], F32R)
        y_hi = at("y_hi", B_YH, [P, 2, 2, 512], F32R)
        oh_l = at("oh_l", B_OH, [P, 2, 512], F32R)
        oh_c = at("oh_c", B_OH + 4096, [P, 2, P], F32R)
        iota_f = at("iota_f", B_IOTA, [P, 512])
        RTK = RING + (P1_SLOT0 + 2) * SLOT
        probs = at("probs", RTK, [P, NT, E])
        probsT = at("probsT", RTK + 512, [E, T])
        topv_l = at("topv_l", RTK + 3072, [E, P])
        topv_c = at("topv_c", RTK + 3584, [E, P])
        topi_l = at("topi_l", RTK + 4096, [E, P], U32)
        topi_c = at("topi_c", RTK + 4608, [E, P], U32)
        selr = at("selr", RTK + 5120, [E, 5, P])

        hn = nc.dram_tensor("hn", [T, D], F32, kind="Internal").ap()

        square_out = at("square_out", RING, [P, 2, D])

        pairs = [ctx.enter_context(nc.psum_tensor(f"pair{i}", [P, 2 * 512], F32)) for i in range(4)]

        names = """job_done prm_in tail_in st_in p1_used const_ready mask_ready param_ready silu_ready o_sum o_mean o_root
            silu_zero decay_zero modrow_ready mod_sum mod_ready scale_ready ss_ready mean_ready root_ready
            xr_ready hT_low hT_high alow_ready qk_first qk_second abs_ready min_ready softplus_ready cum_ready
            exp_b_ready exp_mb_ready dec_ready diff_ready exp_d_ready ks_ready ksT_ready v_sb_ready xc_ready
            u_ready conv_mid conv_ready ya_ready og_act og_ready kv_ready state_step att_ready o_sq o_norm
            yb_ready g1_ready g2_ready wo_read x2_ready h2_low h2_high lg_ready exp_ready
            smax_ready probs_ready probsT_ready selr_ready idx_ready state_out fin_state dve_chain act_chain
            pool_chain gu_used dl_done d_used xTp_done xT_lat xT_ctx xT_zero gul_done silu_lat silu_ctx act_l_ready
            act_c_ready aTp_l aTp_c aT_ready aTc_ready y_read yhi_ready ylo_ready oh_ready sc_done sc_added
            fss_ready fmean_ready froot_ready gfin_in fin_ready fin_out iota_ready""".split()
        (job_done, prm_in, tail_in, st_in, p1_used, const_ready, mask_ready, param_ready, silu_ready, o_sum, o_mean, o_root,
         silu_zero, decay_zero, modrow_ready, mod_sum, mod_ready, scale_ready, ss_ready, mean_ready, root_ready,
         xr_ready, hT_low, hT_high, alow_ready, qk_first, qk_second, abs_ready, min_ready, softplus_ready, cum_ready,
         exp_b_ready, exp_mb_ready, dec_ready, diff_ready, exp_d_ready, ks_ready, ksT_ready, v_sb_ready, xc_ready,
         u_ready, conv_mid, conv_ready, ya_ready, og_act, og_ready, kv_ready, state_step, att_ready, o_sq,
         o_norm, yb_ready, g1_ready, g2_ready, wo_read, x2_ready, h2_low, h2_high, lg_ready,
         exp_ready, smax_ready, probs_ready, probsT_ready, selr_ready, idx_ready, state_out, fin_state, dve_chain,
         act_chain, pool_chain, gu_used, dl_done, d_used, xTp_done, xT_lat, xT_ctx, xT_zero, gul_done, silu_lat, silu_ctx,
         act_l_ready, act_c_ready, aTp_l, aTp_c, aT_ready, aTc_ready, y_read, yhi_ready, ylo_ready, oh_ready,
         sc_done, sc_added, fss_ready, fmean_ready, froot_ready, gfin_in, fin_ready, fin_out,
         iota_ready) = [sem(n) for n in names]
        x_in = [sem(f"x_in{t}") for t in range(NT)]
        p1_full = [sem(f"p1_full{i}") for i in range(3)]
        w_full = [sem(f"w_full{i}") for i in range(RING_SLOTS)]
        xs_full = [sem(f"xs_full{i}") for i in range(2)]
        hn_out = [sem(f"hn_out{i}") for i in range(2)]

        read_by = {"prm": [(param_ready, 1)], "alow": [(alow_ready, 1)], "pT": [(probsT_ready, 1)]}
        for u in range(12):
            read_by[f"mod{u}"] = [(modrow_ready, u + 1)]
            read_by[f"modT{u}"] = [(mod_sum, u + 1)]
        for t in range(NT):
            read_by[f"xT{t}"] = [(hT_low, t + 1), (hT_high, t + 1)]
            read_by[f"v{t}"] = [(v_sb_ready, t + 1)]
            read_by[f"att{t}"] = [(att_ready, 2 * (t + 1))]
            read_by[f"o{t}"] = [(o_sq, t + 1), (o_norm, t + 1)]
            read_by[f"oT{t}"] = [(yb_ready, t + 1)]
            read_by[f"wo{t}"] = [(wo_read, t + 1)]
            read_by[f"x2T{t}"] = [(h2_low, t + 1), (h2_high, t + 1)]
            read_by[f"lg{t}"] = [(lg_ready, t + 1)]
        for i, n in enumerate(("q0", "k0", "q1", "k1")):
            read_by[n] = [(qk_first, i + 1), (qk_second, i + 1)]
        for h in range(H):
            read_by[f"la{h}"] = [(abs_ready, h + 1), (min_ready, h + 1)]
            read_by[f"ks{h}"] = [(ksT_ready, h + 1)]
            read_by[f"og{h}"] = [(og_act, h + 1)]
        for j in range(CH):
            read_by[f"xc{j}"] = [(xc_ready, j + 1)]
            read_by[f"xv{j}"] = [(u_ready, j + 1)]
            read_by[f"xb{j}"] = [(ya_ready, j + 1)]
        for i, n in enumerate(KV_ORDER):
            read_by[f"kv{n}"] = [(kv_ready, i + 1)]
        for v in range(2):
            read_by[f"g1_{v}"] = [(g1_ready, v + 1)]
            read_by[f"g2_{v}"] = [(g2_ready, v + 1)]

        def vec(t):
            return 0 if t < NT - 1 else 1

        def tile(t):
            return slice(t * P, (t + 1) * P)

        def claim(pe, name):
            n = job(name)
            if n >= 4:
                for signal, value in read_by[JOBS[n - 4]]:
                    pe.wait_ge(signal, value)
            return pairs[n % 4]

        def result(eng, name):
            eng.wait_ge(job_done, job(name) + 1)
            return pairs[job(name) % 4]

        def halves(ap):
            return ap.rearrange("p (s n) -> p s n", s=2)[:, :, 0:HALF]

        def split(ap):
            return ap.rearrange("p (s n) -> p s n", s=2)

        def body_loop(eng, expert):
            expert(0, 0)
            expert(1, 1)
            with eng.Fori(0, 3) as i:
                for j in range(2, 6):
                    expert(4 * i + j, j)
            expert(14, 14)
            expert(15, 15)

        gate_ps, up_ps = pairs[0][:, 0:512], pairs[0][:, 512:1024]
        ctx_ps, sc_ps = pairs[1][:, 0:512], pairs[1][:, 512:1024]
        y_ps = [pairs[3][:, 0:512], pairs[3][:, 512:1024]]
        sc_banks = [sc_ps, y_ps[0], y_ps[1]]
        SC = 2 * NT

        def xT_ps(kk):
            o = kk // 4 * 512 + kk % 4 * SLOTS
            return pairs[2][:, o:o + SLOTS]

        block = ctx.enter_context(nc.Block())

        @block.sync
        def _(sp):

            def load_unit(n):
                name = UNITS[n]
                if n >= 3:
                    sp.wait_ge(p1_used, n - 2)
                if name.startswith("mod"):
                    src = w_mod[0, :, 512 * int(name[3:]):512 * (int(name[3:]) + 1)]
                elif name.startswith("wo"):
                    src = w_out[0, :, 512 * int(name[2:]):512 * (int(name[2:]) + 1)]
                else:
                    src = w_in[0, :, IN_COLS[name]:IN_COLS[name] + 512]
                sp.dma_start(p1w[n % 3][:, :, :], src.rearrange("(k p) n -> p k n", p=P)).then_inc(p1_full[n % 3], 16)

            load_unit(0)
            load_unit(1)
            for t in range(NT):
                src = x_sample[0, tile(t), :] if t < NT - 1 else x_prompt[0]
                sp.dma_start(x_sb[:, t, :], src).then_inc(x_in[t], 16)
            load_unit(2)
            sp.dma_start(w_tail[:, :, :], w_in[0, :, P_TOT - 2 * LR:].rearrange("(k p) n -> p k n", p=P)
                         ).then_inc(tail_in, 16)
            sp.dma_start(w_router_sb[:, :, :], w_router[0].rearrange("(k p) n -> p k n", p=P)).then_inc(tail_in, 16)
            load_unit(3)
            sp.wait_ge(decay_zero, 1)
            sp.dma_start(w_decay[0:LR, :, 0:DK], w_a_up_f[0].rearrange("r (h d) -> r h d", d=DK)).then_inc(tail_in, 16)
            sp.dma_start(w_decay[LR:2 * LR, :, DK:P], w_a_up_b[0].rearrange("r (h d) -> r h d", d=DK)
                         ).then_inc(tail_in, 16)
            for n in range(4, 13):
                load_unit(n)
            sp.wait_ge(job_done, job("og3") + 1)
            sp.dma_start(states[0:DK, 0, :, :], s_fwd[0, 0].rearrange("h d v -> d h v")).then_inc(st_in, 16)
            sp.dma_start(states[DK:P, NCH_LAT - 1, :, :], s_bwd[0, 0].rearrange("h d v -> d h v")).then_inc(st_in, 16)
            for n in range(13, len(UNITS) - 1):
                load_unit(n)
            sp.wait_ge(fin_state, 1)
            sp.dma_start(new_f[0, 0].rearrange("h d v -> d h v"), final_state[0:DK, :, :]).then_inc(state_out, 16)
            sp.dma_start(new_b[0, 0].rearrange("h d v -> d h v"), final_state[DK:P, :, :]).then_inc(state_out, 16)

            def load_expert(e, k):
                for u in range(6):
                    half = u // 2 if u < 4 else u - 4
                    w = (w_gate, w_up)[u % 2] if u < 4 else w_down
                    n = 6 * k + u
                    if n >= RING_SLOTS:
                        if u < 2:
                            sp.wait_ge(d_used, 2 * e - 3 + u)
                        else:
                            sp.wait_ge(gu_used, 2 * e - 1 + (u - 2) // 2)
                    elif n == 0:
                        sp.wait_ge(yb_ready, NT)
                        sp.wait_ge(state_out, 32)
                    elif n == P1_SLOT0:
                        load_unit(len(UNITS) - 1)
                        sp.wait_ge(p1_used, len(UNITS))
                    elif n == P1_SLOT0 + 2:
                        sp.wait_ge(idx_ready, 2)
                    rows = slice(half * 512, (half + 1) * 512)
                    src = w[0, e, rows, :] if isinstance(e, int) else \
                        w[0, bass.ds(e, 1), rows, :].rearrange("o r n -> (o r) n")
                    sp.dma_start(ring[n % RING_SLOTS][:, :, :], src.rearrange("(k p) n -> p k n", p=P)
                                 ).then_inc(w_full[n % RING_SLOTS], 16)

            body_loop(sp, load_expert)
            sp.dma_start(gfin[:, :], g_final.partition_broadcast(P)).then_inc(gfin_in, 16)
            sp.wait_ge(fin_out, 16 * NT)

        @block.gpsimd
        def _(pool):
            g = nc.gpsimd
            steps = [0]

            def link(ins):
                steps[0] += 1
                ins.then_inc(pool_chain, 1)
                pool.wait_ge(pool_chain, steps[0])

            g.memset(silu_c[:, :, :], 0.0).then_inc(silu_zero, 1)
            g.memset(eps_col[:, :], EPS)
            g.memset(one_col[:, :], 1.0)
            link(g.memset(ident[:, :], 0.0))
            g.affine_select(out=ident[:, :], in_=ident[:, :], compare_op=ALU.not_equal, fill=1.0, base=0,
                            pattern=[[-1, P]], channel_multiplier=1).then_inc(const_ready, 1)
            g.memset(w_decay[:, :, :], 0.0).then_inc(decay_zero, 1)
            g.memset(a_lowT[:, :], 0.0).then_inc(decay_zero, 1)
            link(g.memset(scan_mask[:, :], 1.0))
            g.memset(scan_mask[0:DK, 0:T:C], 0.0).then_inc(mask_ready, 1)
            g.memset(scan_mask[DK:P, C - 1:T:C], 0.0).then_inc(mask_ready, 1)
            pool.wait_ge(mask_ready, 2)
            link(g.memset(keep_f[:, :], 1.0))
            link(g.affine_select(out=keep_f[:, :], in_=keep_f[:, :], compare_op=ALU.is_ge, fill=0.0, base=0,
                                 pattern=[[1, P]], channel_multiplier=-1))
            g.memset(keep_f[0:C, C:P], 0.0).then_inc(mask_ready, 1)
            pool.wait_ge(mask_ready, 3)
            link(g.memset(keep_b[:, :], 1.0))
            link(g.affine_select(out=keep_b[:, :], in_=keep_b[:, :], compare_op=ALU.is_ge, fill=0.0, base=0,
                                 pattern=[[-1, P]], channel_multiplier=1))
            g.memset(keep_b[C:P, 0:C], 0.0).then_inc(mask_ready, 1)
            pool.wait_ge(mask_ready, 4)
            g.memset(att_sb[:, :, :, :, :], 0.0).then_inc(mask_ready, 1)

            pool.wait_ge(mask_ready, 5)
            pool.wait_ge(idx_ready, 2)
            g.iota(iota_f[:, :], pattern=[[1, 512]], base=0, channel_multiplier=0,
                   allow_small_or_imprecise_dtypes=True).then_inc(iota_ready, 1)
            pool.wait_ge(hn_out[0], 48)
            pool.wait_ge(hn_out[1], 32)
            for e in range(E):
                if e >= 2:
                    pool.wait_ge(xTp_done, e - 1)
                g.indirect_dma_start(xs[:, e % 2, :], None, hn[:, :],
                                     bass.IndirectOffsetOnAxis(ap=gather_idx[0:SLOTS, e:e + 1], axis=0)
                                     ).then_inc(xs_full[e % 2], 16)

        @block.scalar
        def _(act):
            a = nc.scalar
            steps = [0]

            def link(ins):
                steps[0] += 1
                ins.then_inc(act_chain, 1)
                act.wait_ge(act_chain, steps[0])

            for r0, src in (
                (R_BMOD, b_mod[0].rearrange("(r p) -> r p", p=P)),
                (R_G1, g_norm1[0].rearrange("(r p) -> r p", p=P)),
                (R_G2, g_norm2[0].rearrange("(r p) -> r p", p=P)),
                (R_C, c[0].rearrange("(r p) -> r p", p=P)),
                (R_C + KC, c_ctx.rearrange("(r p) -> r p", p=P)),
                (R_CONV, w_conv[0].rearrange("w (r p) -> (w r) p", p=P)),
                (R_BCONV, b_conv[0].rearrange("(r p) -> r p", p=P)),
                (R_GLA, g_gla_norm[0]),
            ):
                act.dma_start(param_rows[r0:r0 + src.shape[0], :], src).then_inc(prm_in, 16)
            act.dma_start(param_rows[R_BA:R_BA + H, 0:DK], b_a_f[0].rearrange("(h d) -> h d", d=DK)
                          ).then_inc(prm_in, 16)
            act.dma_start(param_rows[R_BA:R_BA + H, DK:P], b_a_b[0].rearrange("(h d) -> h d", d=DK)
                          ).then_inc(prm_in, 16)
            act.wait_ge(param_ready, 1)
            act.wait_ge(silu_zero, 1)
            a.activation(silu_c[:, :, 0:2].rearrange("p k v -> p v k"),
                         param[:, R_C:R_C + 2 * KC].rearrange("p (v k) -> p v k", v=2), ACT.Silu
                         ).then_inc(silu_ready, 1)

            def mod_row(u):
                pp = result(act, f"mod{u}")
                if u >= 2:
                    act.wait_ge(job_done, job(f"modT{u - 2}") + 1)
                a.activation(mod_rows[:, u % 2, :], pp[:, 0:512], ACT.Copy).then_inc(modrow_ready, 1)

            def square_sum(t):
                a.activation(xr[:, t % 2, :], x_sb[:, t, :], ACT.Square, accum_out=rms[:, 0, t:t + 1]
                             ).then_inc(ss_ready, 1)

            mod_row(0)
            mod_row(1)
            for t in range(NT):
                act.wait_ge(x_in[t], 16)
                if t >= 2:
                    act.wait_ge(ss_ready, t - 1)
                square_sum(t)
            act.wait_ge(mean_ready, 1)
            a.activation(rms[:, 2, :], rms[:, 1, :], ACT.Sqrt).then_inc(root_ready, 1)
            for u in range(2, 4):
                mod_row(u)

            act.wait_ge(scale_ready, 1)
            for t in range(NT):
                pp = result(act, f"xT{t}")
                for k in range(KC // 2):
                    ins = a.activation(hT[:, k, tile(t)], pp[:, k * P:(k + 1) * P], ACT.Identity,
                                       bias=mod[:, k, vec(t):vec(t) + 1], scale=scale1[:, k, vec(t):vec(t) + 1])
                ins.then_inc(hT_low, 1)

            def q_k(name, kind):
                pp = result(act, name)
                for d in range(2):
                    ins = a.activation(split(qk_rep[d * DK:(d + 1) * DK, kind, 0, :]), halves(pp[0:DK, :]), ACT.Copy)
                ins.then_inc(qk_first, 1)

            def decay(h):
                pp = result(act, f"la{h}")
                if h:
                    act.wait_ge(ks_ready, h)
                a.activation(split(work_b[:, :]), halves(pp), ACT.Abs, bias=param[:, R_BA + h:R_BA + h + 1]
                             ).then_inc(abs_ready, 1)
                act.wait_ge(abs_ready, h + 1)
                link(a.activation(work_b[:, :], work_b[:, :], ACT.Exp, scale=-1.0))
                a.activation(work_b[:, :], work_b[:, :], ACT.Ln, bias=one_col[:, 0:1]).then_inc(softplus_ready, 1)
                act.wait_ge(cum_ready, 2 * (h + 1))
                a.activation(work_a[:, :], work_b[:, :], ACT.Exp, scale=1.0 / TAU).then_inc(exp_b_ready, 1)
                a.activation(work_d[:, :], work_b[:, :], ACT.Exp, scale=-1.0 / TAU).then_inc(exp_mb_ready, 1)
                a.activation(dec[0:DK, h, :], work_b[0:DK, C - 1:T:C], ACT.Exp, scale=1.0 / TAU)
                a.activation(dec[DK:P, h, :], work_b[DK:P, 0:T:C], ACT.Exp, scale=1.0 / TAU).then_inc(dec_ready, 1)
                act.wait_ge(diff_ready, h + 1)
                a.activation(work_a[:, :], work_a[:, :], ACT.Exp, scale=1.0 / TAU).then_inc(exp_d_ready, 1)

            def ks_turn(h):
                pp = result(act, f"ks{h}")
                a.activation(ksT[:, :, h, :], pp[:, 0:T].rearrange("p (t n) -> p t n", n=P), ACT.Copy
                             ).then_inc(ksT_ready, 1)

            q_k("q0", 0)
            q_k("k0", 1)
            decay(0)
            decay(1)
            for t in range(NT):
                pp = result(act, f"v{t}")
                a.activation(v_sb[:, t, :], pp[:, 0:512], ACT.Copy).then_inc(v_sb_ready, 1)
            ks_turn(0)
            ks_turn(1)
            q_k("q1", 0)
            q_k("k1", 1)
            decay(2)
            decay(3)
            for j in range(CH):
                pp = result(act, f"xc{j}")
                a.activation(split(u_sb[:, j, :]), halves(pp), ACT.Copy).then_inc(xc_ready, 1)
            ks_turn(2)
            ks_turn(3)
            for j in range(CH):
                act.wait_ge(u_ready, j + 1)
                a.activation(yT[:, j, :], u_sb[:, j, :], ACT.Identity,
                             scale=param[:, R_CONV + CH + j:R_CONV + CH + j + 1],
                             bias=param[:, R_BCONV + j:R_BCONV + j + 1]).then_inc(conv_mid, 1)
            act.wait_ge(conv_ready, CH)
            for j in range(H):
                pp = result(act, f"og{j}")
                a.activation(split(og_sb[:, j, :]), halves(pp), ACT.Silu).then_inc(og_act, 1)

            for n in KV_ORDER:
                pp = result(act, f"kv{n}")
                f_dst = final_state[0:DK] if n == NCH - 1 else None if n == NCH_LAT - 1 else states[0:DK, n + 1]
                b_dst = final_state[DK:P] if n == NCH_LAT else None if n == 0 else states[DK:P, n - 1]
                src = pp[:, 0:512].rearrange("p (h n) -> p h n", h=H)
                if f_dst is not None:
                    ins = a.activation(f_dst, src[0:DK], ACT.Copy)
                if b_dst is not None:
                    ins = a.activation(b_dst, src[DK:P], ACT.Copy)
                ins.then_inc(kv_ready, 1)

            for u in range(4, 10):
                mod_row(u)

            def o_square(t):
                pp = result(act, f"o{t}")
                if t:
                    act.wait_ge(o_sum, t)
                a.activation(norm_sq[:, :], pp[:, 0:512], ACT.Square).then_inc(o_sq, 1)
                act.wait_ge(o_mean, t + 1)
                a.activation(hrms[:, 2, :], hrms[:, 1, :], ACT.Sqrt).then_inc(o_root, 1)

            def gate_row(name, v, dst, ready):
                pp = result(act, name)
                a.activation(dst[:, v, :], pp[:, :], ACT.Copy).then_inc(ready, 1)

            for t in range(NT):
                o_square(t)
                if t >= 3:
                    gate_row(f"g1_{t - 3}", t - 3, gate1b, g1_ready)

            def second_norm(t):
                act.wait_ge(x2_ready, t + 1)
                square_sum(t)
                act.wait_ge(mean_ready, t + 2)
                a.activation(rms[:, 2, t:t + 1], rms[:, 1, t:t + 1], ACT.Sqrt).then_inc(root_ready, 1)
                act.wait_ge(xr_ready, NT + t + 1)
                act.dma_start(hn[tile(t), :], xr[:, t % 2, :]).then_inc(hn_out[t % 2], 16)

            def h2_turn(t):
                pp = result(act, f"x2T{t}")
                if t >= 2:
                    act.wait_ge(job_done, job(f"lg{t - 2}") + 1)
                for k in range(KC // 2):
                    ins = a.activation(h2T[t % 2][:, k, :], pp[:, k * P:(k + 1) * P], ACT.Identity,
                                       bias=mod[:, 3 * KC + k, vec(t):vec(t) + 1],
                                       scale=scale2[:, k, vec(t):vec(t) + 1])
                ins.then_inc(h2_low, 1)

            act.wait_ge(scale_ready, 2)
            for t in range(NT):
                second_norm(t)
                if t >= 1:
                    h2_turn(t - 1)
            mod_row(10)
            h2_turn(NT - 1)
            act.wait_ge(smax_ready, 1)
            a.activation(probs[:, :, :], probs[:, :, :], ACT.Exp).then_inc(exp_ready, 1)
            mod_row(11)
            for v in range(2):
                gate_row(f"g2_{v}", v, gate2b, g2_ready)

            def tokens(e, k):
                act.wait_ge(xTp_done, e + 1)
                for kk in range(KC):
                    ins = a.activation(xT[:, k % 2, kk, 0:CAP_L], xT_ps(kk)[:, 0:CAP_L], ACT.Identity,
                                       bias=mod[:, 3 * KC + kk, 0:1], scale=scale2[:, kk, 0:1])
                ins.then_inc(xT_lat, 1)

            def expert(e, k):
                act.wait_ge(gul_done, e + 1)
                a.activation(act_l[:, :], gate_ps, ACT.Silu).then_inc(silu_lat, 1)
                act.wait_ge(gu_used, 2 * e + 2)
                a.activation(act_c[64:P, :], ctx_ps[0:64, :], ACT.Silu).then_inc(silu_ctx, 1)
                if k < E - 1:
                    tokens(e + 1, k + 1)
                if k % 2 == 1:
                    for kind in range(2):
                        act.wait_ge(y_read, 4 * e + 2 + 2 * kind)
                        a.activation(y_hi[:, kind, :, :], y_f[:, kind, :, :], ACT.Copy).then_inc(yhi_ready, 1)

            tokens(0, 0)
            body_loop(act, expert)

            for t in range(NT):
                act.wait_ge(sc_added, SC * (E // 2 - 1) + 2 * t + 2)
                if t >= 2:
                    act.wait_ge(fss_ready, t - 1)
                a.activation(square_out[:, t % 2, :], x_sb[:, t, :], ACT.Square, accum_out=rms[:, 0, t:t + 1]
                             ).then_inc(fss_ready, 1)
                act.wait_ge(fmean_ready, t + 1)
                a.activation(rms[:, 2, t:t + 1], rms[:, 1, t:t + 1], ACT.Sqrt).then_inc(froot_ready, 1)
            for t in range(NT):
                act.wait_ge(fin_ready, t + 1)
                dst = y_sample[0, tile(t), :] if t < NT - 1 else y_prompt[0]
                act.dma_start(dst, x_sb[:, t, :]).then_inc(fin_out, 16)

        @block.vector
        def _(dve):
            v = nc.vector
            steps = [0]

            def link(ins):
                steps[0] += 1
                ins.then_inc(dve_chain, 1)
                dve.wait_ge(dve_chain, steps[0])

            pp = result(dve, "prm")
            v.tensor_copy(param[:, :], pp[:, 0:R_ALL]).then_inc(param_ready, 1)

            def mean_square(cols, ready):
                v.tensor_scalar(rms[:, 1, cols], rms[:, 0, cols], 1.0 / D, EPS, ALU.mult, ALU.add).then_inc(ready, 1)

            def inverse_root(r, cols):
                link(v.reciprocal(r[:, 3, cols], r[:, 2, cols]))
                link(v.tensor_tensor(r[:, 4, cols], r[:, 3, cols], r[:, 3, cols], ALU.mult))
                link(v.tensor_tensor(r[:, 4, cols], r[:, 4, cols], r[:, 1, cols], ALU.mult))
                link(v.tensor_scalar(r[:, 4, cols], r[:, 4, cols], -0.5, 1.5, ALU.mult, ALU.add))
                link(v.tensor_tensor(r[:, 5, cols], r[:, 3, cols], r[:, 4, cols], ALU.mult))

            def normalise(t):
                v.tensor_scalar(xr[:, t % 2, :], x_sb[:, t, :], rms[:, 5, t:t + 1], None, ALU.mult
                                ).then_inc(xr_ready, 1)

            def modulation(u):
                pp = result(dve, f"modT{u}")
                src = pp[:, 0:512].rearrange("p (j g r) -> p j r g", j=4, g=4)[:, :, 0:2, :]
                cols = slice(4 * u, 4 * u + 4)
                v.tensor_reduce(mod[:, cols, :], src, AX.X, ALU.add).then_inc(mod_sum, 1)
                dve.wait_ge(mod_sum, u + 1)
                v.tensor_tensor(mod[:, cols, :], mod[:, cols, :],
                                param[:, R_BMOD + 4 * u:R_BMOD + 4 * u + 4].unsqueeze(2).to_broadcast([P, 4, 2]),
                                ALU.add).then_inc(mod_ready, 1)

            def scales(dst, chunk, g_row, u):
                dve.wait_ge(mod_ready, u)
                v.scalar_tensor_tensor(out=dst[:, :, :], in0=mod[:, chunk:chunk + KC, :], scalar=1.0,
                                       in1=param[:, g_row:g_row + KC].unsqueeze(2).to_broadcast([P, KC, 2]),
                                       op0=ALU.add, op1=ALU.mult).then_inc(scale_ready, 1)

            dve.wait_ge(ss_ready, NT)
            mean_square(slice(0, NT), mean_ready)
            dve.wait_ge(root_ready, 1)
            inverse_root(rms, slice(0, NT))
            normalise(0)
            normalise(1)
            dve.wait_ge(param_ready, 1)
            for u in range(4):
                modulation(u)
            scales(scale1, KC, R_G1, 4)
            dve.wait_ge(scale_ready, 1)
            for t in range(NT):
                pp = result(dve, f"xT{t}")
                for k in range(KC // 2, KC):
                    ins = v.tensor_scalar(hT[:, k, tile(t)], pp[:, k * P:(k + 1) * P],
                                          scale1[:, k, vec(t):vec(t) + 1], mod[:, k, vec(t):vec(t) + 1],
                                          ALU.mult, ALU.add)
                ins.then_inc(hT_high, 1)
                if t + 2 < NT:
                    normalise(t + 2)

            pp = result(dve, "alow")
            dve.wait_ge(decay_zero, 2)
            v.tensor_copy(split(a_lowT[0:2 * LR, :]), halves(pp[0:2 * LR, :])).then_inc(alow_ready, 1)

            def q_k(name, kind):
                pp = result(dve, name)
                for d in range(2):
                    ins = v.tensor_copy(split(qk_rep[d * DK:(d + 1) * DK, kind, 1, :]), halves(pp[DK:P, :]))
                ins.then_inc(qk_second, 1)

            def decay(h):
                hh = h % 2
                pp = result(dve, f"la{h}")
                dve.wait_ge(abs_ready, h + 1)
                v.tensor_scalar(split(work_a[:, :]), halves(pp), param[:, R_BA + h:R_BA + h + 1], 0.0,
                                ALU.add, ALU.min).then_inc(min_ready, 1)
                dve.wait_ge(min_ready, h + 1)
                dve.wait_ge(softplus_ready, h + 1)
                link(v.tensor_tensor(work_a[:, :], work_a[:, :], work_b[:, :], ALU.subtract))
                v.tensor_tensor_scan(work_b[0:DK, :], scan_mask[0:DK, :], work_a[0:DK, :], 0.0,
                                     ALU.mult, ALU.add).then_inc(cum_ready, 1)
                v.tensor_tensor_scan(work_b[DK:P, ::-1], scan_mask[DK:P, ::-1], work_a[DK:P, ::-1], 0.0,
                                     ALU.mult, ALU.add).then_inc(cum_ready, 1)
                dve.wait_ge(exp_b_ready, h + 1)
                dve.wait_ge(qk_first, 2 * (h // 2) + 2)
                dve.wait_ge(qk_second, 2 * (h // 2) + 2)
                link(v.scalar_tensor_tensor(out=qd[:, h, :], in0=qk_rep[:, 0, hh, :], scalar=float(DK) ** -0.5,
                                            in1=work_a[:, :], op0=ALU.mult, op1=ALU.mult))
                chunks = lambda ap: ap.rearrange("p (n c) -> p n c", c=C)
                v.tensor_tensor(chunks(work_a[0:DK, :]),
                                work_b[0:DK, C - 1:T:C].unsqueeze(2).to_broadcast([DK, NCH, C]),
                                chunks(work_b[0:DK, :]), ALU.subtract)
                v.tensor_tensor(chunks(work_a[DK:P, :]),
                                work_b[DK:P, 0:T:C].unsqueeze(2).to_broadcast([DK, NCH, C]),
                                chunks(work_b[DK:P, :]), ALU.subtract).then_inc(diff_ready, 1)
                dve.wait_ge(exp_mb_ready, h + 1)
                v.tensor_tensor(kd[:, h, :], qk_rep[:, 1, hh, :], work_d[:, :], ALU.mult)
                dve.wait_ge(exp_d_ready, h + 1)
                v.tensor_tensor(qk_rep[:, 1, hh, :], qk_rep[:, 1, hh, :], work_a[:, :], ALU.mult
                                ).then_inc(ks_ready, 1)

            q_k("q0", 0)
            q_k("k0", 1)
            dve.wait_ge(mask_ready, 5)
            decay(0)
            decay(1)
            q_k("q1", 0)
            q_k("k1", 1)
            decay(2)
            decay(3)

            for j in range(CH):
                pp = result(dve, f"xv{j}")
                dve.wait_ge(xc_ready, j + 1)
                v.tensor_tensor(split(u_sb[:, j, :]), split(u_sb[:, j, :]), halves(pp), ALU.mult
                                ).then_inc(u_ready, 1)
            for j in range(CH):
                dve.wait_ge(conv_mid, j + 1)
                w0 = param[:, R_CONV + j:R_CONV + j + 1]
                w2 = param[:, R_CONV + 2 * CH + j:R_CONV + 2 * CH + j + 1]
                for lo, hi, width in ((0, T_LAT, GRID_W), (T_LAT, T, T_CTX)):
                    y = yT[:, j, lo:hi].rearrange("p (r w) -> p r w", w=width)
                    x = u_sb[:, j, lo:hi].rearrange("p (r w) -> p r w", w=width)
                    link(v.scalar_tensor_tensor(out=y[:, :, 1:], in0=x[:, :, :width - 1], scalar=w0,
                                                in1=y[:, :, 1:], op0=ALU.mult, op1=ALU.add))
                    ins = v.scalar_tensor_tensor(out=y[:, :, :width - 1], in0=x[:, :, 1:], scalar=w2,
                                                 in1=y[:, :, :width - 1], op0=ALU.mult, op1=ALU.add)
                ins.then_inc(conv_ready, 1)
            for j in range(CH):
                pp = result(dve, f"xb{j}")
                dve.wait_ge(conv_ready, j + 1)
                v.tensor_tensor(split(yT[:, j, :]), split(yT[:, j, :]), halves(pp), ALU.mult).then_inc(ya_ready, 1)
            for j in range(H):
                dve.wait_ge(og_act, j + 1)
                v.tensor_scalar(og_sb[:, j, :], og_sb[:, j, :], param[:, R_GLA + j:R_GLA + j + 1], None, ALU.mult
                                ).then_inc(og_ready, 1)

            dve.wait_ge(job_done, job("og3") + 1)
            v.memset(states[0:DK, NCH_LAT, :, :], 0.0).then_inc(state_step, 1)
            v.memset(states[DK:P, NCH - 1, :, :], 0.0).then_inc(state_step, 1)

            def state(n, d):
                rows = slice(0, DK) if d == 0 else slice(DK, P)
                m = n + 1 if d == 0 else n - 1
                last = (n == NCH - 1 and d == 0) or (n == NCH_LAT and d == 1)
                dst = final_state[rows] if last else states[rows, m]
                for h in range(H):
                    ins = v.scalar_tensor_tensor(out=dst[:, h, :], in0=states[rows, n, h, :],
                                                 scalar=dec[rows, h, n:n + 1], in1=dst[:, h, :],
                                                 op0=ALU.mult, op1=ALU.add)
                return ins

            dve.wait_ge(st_in, 32)
            dve.wait_ge(dec_ready, H)
            for i in range(NCH_LAT - 1):
                for d in range(2):
                    n = i if d == 0 else NCH_LAT - 1 - i
                    dve.wait_ge(kv_ready, KV_ORDER.index(n) + 1)
                    if i:
                        dve.wait_ge(state_step, 2 * i + d + 1)
                    state(n, d).then_inc(state_step, 1)
            STEPS = 2 * NCH_LAT
            dve.wait_ge(kv_ready, len(KV_ORDER))
            dve.wait_ge(state_step, 2)
            state(NCH_LAT, 0).then_inc(state_step, 1)
            state(NCH - 1, 1).then_inc(state_step, 1)
            dve.wait_ge(state_step, STEPS + 2)
            state(NCH - 1, 0)
            state(NCH_LAT, 1).then_inc(fin_state, 1)

            def att_mask(t):
                pp = result(dve, f"att{t}")
                if t >= 2:
                    dve.wait_ge(job_done, job(f"o{t - 2}") + 1)
                for d, keep in enumerate((keep_f, keep_b)):
                    v.copy_predicated(att_sb[:, t % 2, d, :, :],
                                      keep[:, :].bitcast(I32).unsqueeze(1).to_broadcast([P, H, P]),
                                      pp[:, d * 512:(d + 1) * 512].rearrange("p (h n) -> p h n", h=H)
                                      ).then_inc(att_ready, 1)

            att_mask(0)
            att_mask(1)
            for u in range(4, 10):
                modulation(u)
            scales(scale2, 4 * KC, R_G2, 10)
            heads = lambda ap: ap.rearrange("p (h n) -> p h n", h=H)

            def head_norm(t):
                dve.wait_ge(o_sq, t + 1)
                v.tensor_reduce(hrms[:, 0, :], heads(norm_sq[:, :]), AX.X, ALU.add).then_inc(o_sum, 1)
                dve.wait_ge(o_sum, t + 1)
                v.tensor_scalar(hrms[:, 1, :], hrms[:, 0, :], 1.0 / DV, EPS, ALU.mult, ALU.add).then_inc(o_mean, 1)
                dve.wait_ge(o_root, t + 1)
                inverse_root(hrms, slice(0, H))
                pp = result(dve, f"o{t}")
                if t:
                    dve.wait_ge(job_done, job(f"oT{t - 1}") + 1)
                v.tensor_tensor(heads(norm_r[:, :]), heads(pp[:, 0:512]),
                                hrms[:, 5, :].unsqueeze(2).to_broadcast([P, H, DV]), ALU.mult).then_inc(o_norm, 1)

            def gated(t):
                pp = result(dve, f"oT{t}")
                dve.wait_ge(og_ready, H)
                v.tensor_tensor(yT[:, CH:KC, tile(t)], heads(pp[:, 0:512]), og_sb[:, :, tile(t)], ALU.mult
                                ).then_inc(yb_ready, 1)

            for t in range(NT):
                if t + 2 < NT:
                    att_mask(t + 2)
                head_norm(t)
                gated(t)

            dve.wait_ge(g1_ready, 2)

            def high_chunks(t):
                pp = result(dve, f"x2T{t}")
                if t >= 2:
                    dve.wait_ge(job_done, job(f"lg{t - 2}") + 1)
                for k in range(KC // 2, KC):
                    ins = v.tensor_scalar(h2T[t % 2][:, k, :], pp[:, k * P:(k + 1) * P],
                                          scale2[:, k, vec(t):vec(t) + 1], mod[:, 3 * KC + k, vec(t):vec(t) + 1],
                                          ALU.mult, ALU.add)
                ins.then_inc(h2_high, 1)

            def router_row(t):
                pp = result(dve, f"lg{t}")
                v.tensor_copy(logits[:, t, :], pp[:, 0:E]).then_inc(lg_ready, 1)

            dve.wait_ge(scale_ready, 2)
            for t in range(NT):
                pp = result(dve, f"wo{t}")
                if t >= 2:
                    dve.wait_ge(hn_out[t % 2], 16 * (t // 2))
                    dve.wait_ge(job_done, job(f"x2T{t - 2}") + 1)
                v.tensor_tensor(xr[:, t % 2, :], pp[:, :], gate1b[:, vec(t), :], ALU.mult).then_inc(wo_read, 1)
                dve.wait_ge(wo_read, t + 1)
                v.tensor_tensor(x_sb[:, t, :], x_sb[:, t, :], xr[:, t % 2, :], ALU.add).then_inc(x2_ready, 1)
                dve.wait_ge(ss_ready, NT + t + 1)
                mean_square(slice(t, t + 1), mean_ready)
                dve.wait_ge(root_ready, t + 2)
                inverse_root(rms, slice(t, t + 1))
                normalise(t)
                if t >= 1:
                    high_chunks(t - 1)
                if t >= 2:
                    router_row(t - 2)
            router_row(NT - 2)
            modulation(10)
            high_chunks(NT - 1)
            router_row(NT - 1)

            dve.wait_ge(lg_ready, NT)
            dve.wait_ge(job_done, job("wo4") + 1)
            link(v.tensor_reduce(smax[:, 0, :], logits[:, :, :], AX.X, ALU.max))
            v.tensor_tensor(probs[:, :, :], logits[:, :, :], smax[:, 0, :].unsqueeze(2).to_broadcast([P, NT, E]),
                            ALU.subtract).then_inc(smax_ready, 1)
            dve.wait_ge(exp_ready, 1)
            link(v.tensor_reduce(smax[:, 1, :], probs[:, :, :], AX.X, ALU.add))
            link(v.reciprocal(smax[:, 2, :], smax[:, 1, :]))
            v.tensor_tensor(probs[:, :, :], probs[:, :, :], smax[:, 2, :].unsqueeze(2).to_broadcast([P, NT, E]),
                            ALU.mult).then_inc(probs_ready, 1)
            modulation(11)
            pp = result(dve, "pT")
            v.tensor_copy(probsT[:, :], pp[0:E, 0:T]).then_inc(probsT_ready, 1)
            dve.wait_ge(probsT_ready, 1)

            for lo, hi, cap, top_v, top_i in ((0, T_LAT, CAP_L, topv_l, topi_l), (T_LAT, T, CAP_C, topv_c, topi_c)):
                for r in range(cap // 8):
                    eight = slice(8 * r, 8 * r + 8)
                    link(v.max(top_v[:, eight], probsT[:, lo:hi]))
                    v.max_index(top_i[:, eight], top_v[:, eight], probsT[:, lo:hi])
                    if r < cap // 8 - 1:
                        link(v.match_replace(probsT[:, lo:hi], top_v[:, eight], probsT[:, lo:hi], -1.0))

            four = lambda ap: ap.rearrange("e (b s) -> e b s", s=32)
            v.memset(selr[:, 0:2, :], 0.0)
            v.memset(selr[:, 2, :], -1.0)
            link(v.memset(selr[:, 3:5, :], 0.0))
            for b in range(2):
                v.tensor_copy(selr[:, 0, b * CAP_L:(b + 1) * CAP_L], topi_l[:, 0:CAP_L])
                v.tensor_copy(selr[:, 1, b * CAP_L:(b + 1) * CAP_L], topv_l[:, 0:CAP_L])
            v.tensor_copy(four(selr[:, 2, :])[:, :, 0:CAP_C],
                          topi_c[:, 0:CAP_C].unsqueeze(1).to_broadcast([E, 4, CAP_C]))
            v.tensor_copy(four(selr[:, 3, :])[:, :, 0:CAP_C],
                          topv_c[:, 0:CAP_C].unsqueeze(1).to_broadcast([E, 4, CAP_C]))
            v.tensor_copy(selr[:, 4, 0:CAP_L], topi_l[:, 0:CAP_L])
            v.tensor_scalar(selr[:, 4, CAP_L:SLOTS], topi_c[:, 0:CAP_C], float(T_LAT), None, ALU.add
                            ).then_inc(selr_ready, 1)
            pp = result(dve, "ixT")
            v.tensor_copy(gather_idx[0:SLOTS, :], pp[0:SLOTS, 4 * E:5 * E]).then_inc(idx_ready, 1)
            src = pp[:, 0:4 * E].rearrange("p (q n two) -> p q n two", q=4, two=2)
            dst = pair_cols[:, :, :].rearrange("p (q o) n -> p q o n", o=2)
            v.tensor_copy(dst[0:64, :, 0, :], src[0:64, :, :, 0])
            v.tensor_copy(dst[0:64, :, 1, :], src[0:64, :, :, 1])
            v.tensor_copy(dst[64:P, :, 0, :], src[64:P, :, :, 1])
            v.tensor_copy(dst[64:P, :, 1, :], src[64:P, :, :, 0]).then_inc(idx_ready, 1)

            def col(q, o, pair):
                return pair_cols[:, 2 * q + o, pair:pair + 1] if isinstance(pair, int) else \
                    pair_cols[:, 2 * q + o, bass.ds(pair, 1)]

            def tokens(e, k):
                dve.wait_ge(xT_lat, e + 1)
                src = pairs[2][:, :].rearrange("p (b n) -> p b n", b=2)[:, :, 0:4 * SLOTS].rearrange(
                    "p b (k s) -> p b k s", s=SLOTS)[:, :, :, CAP_L:SLOTS]
                dst = xT[:, k % 2, :, CAP_L:SLOTS].rearrange("p (b k) s -> p b k s", b=2)
                by = lambda ap: ap.rearrange("p (b k) v -> p b k v", b=2).to_broadcast([P, 2, 4, CAP_C])
                v.tensor_tensor(dst, src, by(scale2[:, :, 1:2]), ALU.mult).then_inc(xT_ctx, 1)
                dve.wait_ge(xT_ctx, 2 * e + 1)
                v.tensor_tensor(dst, dst, by(mod[:, 3 * KC:4 * KC, 1:2]), ALU.add).then_inc(xT_ctx, 1)

            def add_back(base, n):
                t, half = n // 2, n % 2
                cols = slice(half * 512, (half + 1) * 512)
                dve.wait_ge(sc_done, base + n + 1)
                v.tensor_tensor(x_sb[:, t, cols], x_sb[:, t, cols], sc_banks[n % 3], ALU.add).then_inc(sc_added, 1)

            def expert(e, k):
                q = k % 2
                if q == 0 and k > 0:
                    for n in range(6):
                        add_back(5 * e - SC, n)
                dve.wait_ge(silu_lat, e + 1)
                v.tensor_tensor(act_l[:, :], act_l[:, :], up_ps, ALU.mult).then_inc(act_l_ready, 1)
                if q == 0 and k > 0:
                    for n in range(6, 8):
                        add_back(5 * e - SC, n)
                dve.wait_ge(aTp_l, e + 1)
                v.tensor_copy(aT[:, :, :], gate_ps.rearrange("p (j n) -> p j n", j=4)).then_inc(aT_ready, 1)
                dve.wait_ge(silu_ctx, e + 1)
                v.tensor_tensor(act_c[0:64, :], act_c[64:P, :], ctx_ps[64:P, :], ALU.mult).then_inc(act_c_ready, 1)
                if q == 0 and k > 0:
                    for n in range(8, SC):
                        add_back(5 * e - SC, n)
                dve.wait_ge(aTp_c, e + 1)
                v.tensor_copy(aTc[:, :, :], ctx_ps.rearrange("p (j n) -> p j n", j=4)[:, :, 0:64]).then_inc(aTc_ready, 1)
                if k < E - 1:
                    tokens(e + 1, k + 1)
                pair = k // 2 if isinstance(e, int) else pair_of[0]
                if q == 0:
                    dve.wait_ge(iota_ready, 1)
                    for o in range(2):
                        v.tensor_scalar(oh_l[:, o, :], iota_f[:, :], col(0, o, pair), None, ALU.is_equal)
                        ins = v.tensor_scalar(oh_c[:, o, :], iota_f[:, 0:P], col(2, o, pair), None, ALU.is_equal)
                    ins.then_inc(oh_ready, 1)
                for kind in range(2):
                    dve.wait_ge(*((dl_done, e + 1) if kind == 0 else (d_used, 2 * e + 2)))
                    for half in range(2):
                        r = 64 * (half ^ q)
                        v.scalar_tensor_tensor(out=y_f[r:r + 64, kind, half, :], in0=y_ps[kind][r:r + 64, :],
                                               scalar=col(2 * kind + 1, half, pair)[r:r + 64],
                                               in1=gate2b[r:r + 64, kind, half * 512:(half + 1) * 512],
                                               op0=ALU.mult, op1=ALU.mult).then_inc(y_read, 1)
                    if q == 1:
                        dve.wait_ge(yhi_ready, 2 * pair + kind + 1)
                        v.tensor_tensor(y_lo[:, kind, :, :], y_f[:, kind, :, :], y_hi[:, kind, :, :].bitcast(F32),
                                        ALU.subtract).then_inc(ylo_ready, 1)

            pair_of = [0]

            def dve_loop():
                expert(0, 0)
                expert(1, 1)
                with dve.Fori(0, 3) as i:
                    for j in range(2, 6):
                        pair_of[0] = 2 * i + j // 2
                        expert(4 * i + j, j)
                expert(14, 14)
                expert(15, 15)

            dve.wait_ge(g2_ready, 2)
            v.memset(xT[:, :, :, SLOTS:96], 0.0).then_inc(xT_zero, 1)
            tokens(0, 0)
            dve_loop()
            for n in range(SC):
                add_back(SC * (E // 2 - 1), n)
            dve.wait_ge(gfin_in, 16)
            for t in range(NT):
                dve.wait_ge(fss_ready, t + 1)
                mean_square(slice(t, t + 1), fmean_ready)
                dve.wait_ge(froot_ready, t + 1)
                inverse_root(rms, slice(t, t + 1))
                v.scalar_tensor_tensor(out=x_sb[:, t, :], in0=x_sb[:, t, :], scalar=rms[:, 5, t:t + 1],
                                       in1=gfin[:, :], op0=ALU.mult, op1=ALU.mult).then_inc(fin_ready, 1)

        @block.tensor
        def _(pe):
            mm, turn = nc.tensor.matmul, nc.tensor.transpose
            units_used = [0]

            def unit_wait(name):
                n = UNITS.index(name)
                pe.wait_ge(p1_full[n % 3], 16 * (n // 3 + 1))
                return p1w[n % 3]

            def use_signal():
                pe.wait_ge(job_done, done[0])
                pe.sem_inc(p1_used, 1)

            done = [0]

            def end(ins, name):
                assert JOBS[done[0]] == name, (JOBS[done[0]], name)
                done[0] += 1
                ins.then_inc(job_done, 1)

            def turn_params():
                pe.wait_ge(prm_in, 160)
                pe.wait_ge(const_ready, 1)
                pp = claim(pe, "prm")
                end(turn(pp[:, 0:R_ALL], param_rows[:, :], ident[0:R_ALL, 0:R_ALL]), "prm")

            def mod_products(u):
                w = unit_wait(f"mod{u}")
                pe.wait_ge(silu_ready, 1)
                pp = claim(pe, f"mod{u}")
                for k in range(KC):
                    g = 32 * (k % 4)
                    ins = mm(pp[g:g + 32, 0:512], silu_c[:, k, :], w[:, k, :], start=k < 4, stop=k >= 4)
                end(ins, f"mod{u}")
                use_signal()

            def mod_turn(u):
                pe.wait_ge(modrow_ready, u + 1)
                pp = claim(pe, f"modT{u}")
                for j in range(4):
                    ins = turn(pp[:, tile(j)], mod_rows[:, u % 2, tile(j)], ident[:, :])
                end(ins, f"modT{u}")

            def turn_rows(name, ready, t):
                pe.wait_ge(xr_ready, ready)
                pp = claim(pe, name)
                for k in range(KC):
                    ins = turn(pp[:, tile(k)], xr[:, t % 2, tile(k)], ident[:, :])
                end(ins, name)

            def project(name, w, cols):
                pp = claim(pe, name)
                m = cols.stop - cols.start
                for s in range(2):
                    for k in range(KC):
                        ins = mm(pp[0:m, s * 512:s * 512 + HALF], w[:, k, cols], hT[:, k, s * HALF:(s + 1) * HALF],
                                 start=k == 0, stop=k == KC - 1)
                end(ins, name)

            def log_decay(h):
                pe.wait_ge(alow_ready, 1)
                pe.wait_ge(tail_in, 64)
                pp = claim(pe, f"la{h}")
                for s in range(2):
                    ins = mm(pp[:, s * 512:s * 512 + HALF], w_decay[:, h, :], a_lowT[:, s * HALF:(s + 1) * HALF],
                             start=True, stop=True)
                end(ins, f"la{h}")

            def values(t):
                w = unit_wait("v")
                pp = claim(pe, f"v{t}")
                for k in range(KC):
                    ins = mm(pp[:, 0:512], hT[:, k, tile(t)], w[:, k, :], start=k == 0, stop=k == KC - 1)
                end(ins, f"v{t}")

            def turn_ks(h):
                pe.wait_ge(ks_ready, h + 1)
                pp = claim(pe, f"ks{h}")
                for t in range(NT):
                    ins = turn(pp[:, tile(t)], qk_rep[:, 1, h % 2, tile(t)], ident[:, :])
                end(ins, f"ks{h}")

            turn_params()
            mod_products(0)
            mod_products(1)
            mod_turn(0)
            mod_products(2)
            mod_turn(1)
            mod_products(3)
            mod_turn(2)
            mod_turn(3)
            for t in range(NT):
                turn_rows(f"xT{t}", t + 1, t)
            pe.wait_ge(hT_low, NT)
            pe.wait_ge(hT_high, NT)
            pe.wait_ge(tail_in, 32)
            project("alow", w_tail, slice(0, 2 * LR))
            w = unit_wait("qk")
            project("q0", w, tile(0))
            project("k0", w, tile(2))
            log_decay(0)
            log_decay(1)
            for t in range(NT):
                values(t)
            turn_ks(0)
            turn_ks(1)
            project("q1", w, tile(1))
            project("k1", w, tile(3))
            use_signal()
            use_signal()
            log_decay(2)
            log_decay(3)
            for name in ("xc", "xv", "xb", "og"):
                w = unit_wait(name)
                for j in range(4):
                    project(f"{name}{j}", w, tile(j))
                use_signal()
                if name == "xc":
                    turn_ks(2)
                    turn_ks(3)

            pe.wait_ge(ksT_ready, H)
            pe.wait_ge(v_sb_ready, NT)
            for n in KV_ORDER:
                pp = claim(pe, f"kv{n}")
                r = slice(n % 2 * C, n % 2 * C + C)
                for h in range(H):
                    ins = mm(pp[:, tile(h)], ksT[r, n // 2, h, :], v_sb[r, n // 2, tile(h)], start=True, stop=True)
                end(ins, f"kv{n}")

            def attention(t):
                pp = claim(pe, f"att{t}")
                for d in range(2):
                    r = slice(d * DK, (d + 1) * DK)
                    for h in range(H):
                        ins = mm(pp[:, d * 512 + h * P:d * 512 + (h + 1) * P], kd[r, h, tile(t)], qd[r, h, tile(t)],
                                 start=True, stop=True)
                end(ins, f"att{t}")

            def head_outputs(t):
                pe.wait_ge(att_ready, 2 * (t + 1))
                pp = claim(pe, f"o{t}")
                for h in range(H):
                    for d in range(2):
                        mm(pp[:, tile(h)], att_sb[:, t % 2, d, h, :], v_sb[:, t, tile(h)], start=d == 0, stop=False)
                    for j in range(2):
                        n = 2 * t + j
                        ins = mm(pp[j * C:(j + 1) * C, tile(h)], qd[:, h, n * C:(n + 1) * C], states[:, n, h, :],
                                 start=False, stop=True)
                end(ins, f"o{t}")

            def turn_heads(t):
                pe.wait_ge(o_norm, t + 1)
                pp = claim(pe, f"oT{t}")
                for h in range(H):
                    ins = turn(pp[:, tile(h)], norm_r[:, tile(h)], ident[:, :])
                end(ins, f"oT{t}")

            def gate_rows(which, chunk, v):
                pp = claim(pe, f"g{which}_{v}")
                for k in range(KC):
                    ins = mm(pp[:, tile(k)], mod[:, chunk + k, v:v + 1].to_broadcast([P, P]), ident[:, :],
                             start=True, stop=True)
                end(ins, f"g{which}_{v}")

            attention(0)
            attention(1)
            mod_products(4)
            for u in range(5, 10):
                mod_products(u)
                mod_turn(u - 1)
            mod_turn(9)
            pe.wait_ge(state_step, 2 * NCH_LAT + 2)
            pe.wait_ge(mod_ready, 10)
            head_outputs(0)
            attention(2)
            head_outputs(1)
            turn_heads(0)
            attention(3)
            head_outputs(2)
            turn_heads(1)
            attention(4)
            head_outputs(3)
            turn_heads(2)
            gate_rows(1, 2 * KC, 0)
            head_outputs(4)
            turn_heads(3)
            gate_rows(1, 2 * KC, 1)
            turn_heads(4)

            def output_projection(t):
                pe.wait_ge(yb_ready, t + 1)
                ws = [unit_wait("wo0"), unit_wait("wo1")]
                pp = claim(pe, f"wo{t}")
                for half in range(2):
                    for k in range(KC):
                        ins = mm(pp[:, half * 512:(half + 1) * 512], yT[:, k, tile(t)], ws[half][:, k, :],
                                 start=k == 0, stop=k == KC - 1)
                end(ins, f"wo{t}")

            def router(t):
                pe.wait_ge(h2_low, t + 1)
                pe.wait_ge(h2_high, t + 1)
                pp = claim(pe, f"lg{t}")
                for k in range(KC):
                    ins = mm(pp[:, 0:E], h2T[t % 2][:, k, :], w_router_sb[:, k, :], start=k == 0, stop=k == KC - 1)
                end(ins, f"lg{t}")

            pe.wait_ge(ya_ready, CH)
            output_projection(0)
            output_projection(1)
            turn_rows("x2T0", NT + 1, 0)
            output_projection(2)
            router(0)
            turn_rows("x2T1", NT + 2, 1)
            output_projection(3)
            router(1)
            turn_rows("x2T2", NT + 3, 2)
            output_projection(4)
            use_signal()
            use_signal()
            router(2)
            turn_rows("x2T3", NT + 4, 3)
            mod_products(10)
            router(3)
            mod_turn(10)
            turn_rows("x2T4", NT + 5, 4)
            router(4)
            mod_products(11)
            mod_turn(11)

            pe.wait_ge(probs_ready, 1)
            pp = claim(pe, "pT")
            for t in range(NT):
                ins = turn(pp[0:E, tile(t)], probs[:, t, :], ident[:, :])
            end(ins, "pT")
            pe.wait_ge(mod_ready, 12)
            gate_rows(2, 5 * KC, 0)
            gate_rows(2, 5 * KC, 1)
            pe.wait_ge(selr_ready, 1)
            pp = claim(pe, "ixT")
            for q in range(5):
                ins = turn(pp[:, q * E:(q + 1) * E], selr[:, q, :], ident[0:E, 0:E])
            end(ins, "ixT")

            def turn_tokens(e, k):
                pe.wait_ge(xs_full[k % 2], 16 * (e // 2 + 1) if isinstance(e, int) else 8 * e + (16 if k % 2 == 0 else 8))
                if k > 0:
                    pe.wait_ge(xT_lat, e)
                    pe.wait_ge(xT_ctx, 2 * e)
                for kk in range(KC):
                    ins = turn(xT_ps(kk), xs[:, k % 2, tile(kk)], ident[0:SLOTS, 0:SLOTS])
                ins.then_inc(xTp_done, 1)

            def scatter(base, n):
                t, half = n // 2, n % 2
                kind = vec(t)
                if n >= 3:
                    pe.wait_ge(sc_added, base + n - 2)
                else:
                    pe.wait_ge(sc_added, base)
                oh = oh_l[:, half, tile(t)] if kind == 0 else oh_c[:, half, :]
                mm(sc_banks[n % 3], oh, y_hi[:, kind, half, :], start=True, stop=False)
                mm(sc_banks[n % 3], oh, y_lo[:, kind, half, :], start=False, stop=True).then_inc(sc_done, 1)

            def weights(e, k, u):
                n = 6 * k + u
                slot = n % RING_SLOTS
                count = 16 * (n // RING_SLOTS + 1)
                pe.wait_ge(w_full[slot], count if isinstance(e, int) else 12 * (e - k) + count)
                return ring[slot]

            def expert(e, k):
                q = k % 2
                add = q == 0 and k > 0
                base = 5 * e - SC
                xt = xT[:, k % 2]
                pe.wait_ge(xT_lat, e + 1)
                pe.wait_ge(xT_ctx, 2 * e + 2)
                if k > 0:
                    pe.wait_ge(aT_ready, e)
                    pe.wait_ge(aTc_ready, e)
                for half in range(2):
                    wg, wu = weights(e, k, 2 * half), weights(e, k, 2 * half + 1)
                    for j in range(4):
                        kk = 4 * half + j
                        for ps, w in ((gate_ps, wg), (up_ps, wu)):
                            for n in range(2):
                                ins = mm(ps[64 * n:64 * n + 64, :], xt[:, kk, 0:CAP_L], w[:, j, n * 512:(n + 1) * 512],
                                         start=kk == 0, stop=kk == KC - 1)
                    if half == 1:
                        ins.then_inc(gul_done, 1)
                    if add:
                        if half == 0:
                            pe.wait_ge(ylo_ready, e if isinstance(e, int) else 2 * pair_of[0])
                            pe.wait_ge(oh_ready, base // SC + 1 if isinstance(e, int) else pair_of[0])
                            pe.wait_ge(y_read, 4 * e)
                        for n in ((0, 1, 2), (6, 7))[half]:
                            scatter(base, n)
                    for j in range(4):
                        kk = 4 * half + j
                        for g in range(4):
                            n, w = g % 2, (wg, wu)[g // 2]
                            ins = mm(ctx_ps[32 * g:32 * g + 32, :], xt[:, kk, CAP_L:96], w[:, j, n * 512:(n + 1) * 512],
                                     start=kk == 0, stop=kk == KC - 1)
                        if half == 1 and j == 2:
                            pe.wait_ge(act_l_ready, e + 1)
                            for jl in range(4):
                                turned = turn(gate_ps[:, tile(jl)], act_l[:, tile(jl)], ident[:, :])
                            turned.then_inc(aTp_l, 1)
                    ins.then_inc(gu_used, 1)
                    if add:
                        for n in ((3, 4, 5), (8, 9))[half]:
                            scatter(base, n)
                if k < E - 1:
                    turn_tokens(e + 1, k + 1)
                pe.wait_ge(aT_ready, e + 1)
                if k > 0:
                    pe.wait_ge(y_read, 4 * e)
                if add:
                    pe.wait_ge(sc_added, base + 8)
                for fh in range(2):
                    wd = weights(e, k, 4 + fh)
                    for j in range(4):
                        for n in range(2):
                            r = 64 * (n ^ q)
                            ins = mm(y_ps[0][r:r + 64, :], aT[:, j, 64 * fh:64 * fh + 64], wd[:, j, n * 512:(n + 1) * 512],
                                     start=fh == 0 and j == 0, stop=fh == 1 and j == 3)
                            if fh == 1 and j == 3 and n == 1:
                                ins.then_inc(dl_done, 1)
                        if fh == 0 and j == 1:
                            pe.wait_ge(act_c_ready, e + 1)
                            for jc in range(4):
                                ins = turn(ctx_ps[:, tile(jc)], act_c[:, tile(jc)], ident[:, :])
                            ins.then_inc(aTp_c, 1)
                    if fh == 0:
                        pe.wait_ge(aTc_ready, e + 1)
                        if add:
                            pe.wait_ge(sc_added, base + 9)
                    for j in range(4):
                        for n in range(2):
                            r = 64 * (n ^ q) + 32 * (j % 2)
                            ins = mm(y_ps[1][r:r + 32, :], aTc[:, j, 32 * fh:32 * fh + 32],
                                     wd[:, j, n * 512:(n + 1) * 512], start=fh == 0 and j < 2, stop=fh == 1 and j >= 2)
                    ins.then_inc(d_used, 1)

            pair_of = [0]
            pe.wait_ge(xT_zero, 1)
            turn_tokens(0, 0)
            expert(0, 0)
            expert(1, 1)
            with pe.Fori(0, 3) as i:
                for j in range(2, 6):
                    pair_of[0] = 2 * i + j // 2
                    expert(4 * i + j, j)
            expert(14, 14)
            expert(15, 15)
            pe.wait_ge(ylo_ready, E)
            pe.wait_ge(y_read, 4 * E)
            for n in range(SC):
                scatter(SC * (E // 2 - 1), n)


_INS = ["x_prompt", "x_sample", "state_gla_fwd", "state_gla_bwd", "c", "c_ctx", "w_mod", "b_mod", "g_norm1", "g_norm2",
        "w_in", "w_conv", "b_conv", "w_a_up_f", "b_a_f", "w_a_up_b", "b_a_b", "g_gla_norm", "w_out", "w_router",
        "w_gate", "w_up", "w_down", "g_final"]
_OUTS = [(1, T_CTX, D), (1, T_LAT, D), (1, 1, H, DK, DV), (1, 1, H, DK, DV)]


def kernel(**inputs):
    import numpy as np
    import concourse.bacc as bacc
    from concourse.bass_utils import run_bass_kernel_spmd

    nc = bacc.Bacc("TRN2", target_bir_lowering=False, num_devices=1)
    arrays, args = {}, []
    for name in _INS:
        a = np.ascontiguousarray(inputs[name])
        arrays[f"in_{name}"] = a
        args.append(nc.dram_tensor(f"in_{name}", a.shape, mybir.dt.from_np(a.dtype), kind="ExternalInput").ap())
    for i, shape in enumerate(_OUTS):
        args.append(nc.dram_tensor(f"out_{i}", shape, F32, kind="ExternalOutput").ap())
    build(nc, *args)
    r = run_bass_kernel_spmd(nc, [arrays], core_ids=[0])
    return tuple(r.results[0][f"out_{i}"] for i in range(len(_OUTS)))
```

```python
from contextlib import ExitStack

import concourse.bass as bass
from concourse import mybir

F32 = mybir.dt.float32
F32R = mybir.dt.float32r
U32 = mybir.dt.uint32
I32 = mybir.dt.int32
ALU = mybir.AluOpType
ACT = mybir.ActivationFunctionType
AX = mybir.AxisListType

P = 128
D = 1024
KC = D // P
T_LAT, T_CTX = 512, 128
T = T_LAT + T_CTX
NT = T // P
HALF = T // 2
GRID_W = 64
CH = D // 2 // P
H, DK, DV = 4, 64, 128
C = 64
NCH, NCH_LAT = T // C, T_LAT // C
LR = 16
TAU = 16.0
E = 16
CAP_L, CAP_C = 2 * T_LAT // E, 2 * T_CTX // E
SLOTS = CAP_L + CAP_C
NMOD = 6
EPS = 1e-6
P_TOT = 3 * 512 + 2 * H * DK + 2 * H * DV + 2 * LR

R_BMOD, R_G1, R_G2, R_C, R_CONV, R_BCONV, R_GLA, R_BA = 0, 48, 56, 64, 80, 92, 96, 100
R_ALL = 104

WORK = 16512
RING_SLOTS = 8
SLOT = 4 * D * 4
RING = 229368 // 32 * 32 - RING_SLOTS * SLOT
A_X = WORK
A_CONST = A_X + 20480
A_G2B = A_CONST + 3680
A_GFIN = A_G2B + 8192
A_P2 = A_GFIN + 4096
R_HT = RING
R_HLO = R_HT + 20480
R_U = R_HLO + 20480
R_QD = R_U + 10240
R_KD = R_QD + 10240
R_KST = R_KD + 10240
R_V = RING + 7 * SLOT
R_FIN = R_V + 10240
R_ALOW = R_FIN + 2048
P1_SLOTS = (5, 6, 4, 3)
W_YT = A_P2
W_KS = W_YT + 10240
W_HI = W_YT + 20480
W_XR = W_HI + 16384
B_XS = A_P2
B_XT = B_XS + 8192
B_G = B_XT + 6144
B_GC = B_G + 2048
B_AT = B_GC + 2048
B_ATC = B_AT + 2048
B_Y = B_ATC + 1024
B_YH = B_Y + 8192
B_OH = B_YH + 8192
B_IOTA = B_OH + 5120
assert B_IOTA + 2048 <= RING and W_XR + 8192 <= RING


def first_phase_jobs():
    jobs = ["prm", "mod0", "mod1", "modT0", "mod2", "modT1", "modT2", "xT0", "xT1", "mod3", "modT3"]
    jobs += [f"xT{t}" for t in range(2, NT)]
    jobs += ["q0", "q1", "alow", "k0", "k1", "la0", "la1"]
    jobs += ["v0", "v1", "v2", "mod4", "v3", "v4", "ks0", "ks1", "modT4", "la2"]
    jobs += ["xc0", "xc1", "mod5", "xc2", "modT5", "xc3", "ks2"]
    jobs += ["xv0", "la3", "xv1", "mod6", "xv2", "modT6", "xv3", "ks3"]
    jobs += ["xb0", "xb1", "mod7", "xb2", "modT7", "xb3"]
    jobs += ["og0", "og1", "mod8", "og2", "modT8", "og3"]
    jobs += [f"kv{n}" for n in KV_ORDER]
    jobs += ["att0", "att1", "mod9", "modT9"]
    jobs += ["o0", "att2", "o1", "oT0", "att3", "o2", "oT1", "att4", "o3", "oT2", "g1_0", "o4", "oT3", "g1_1", "oT4"]
    jobs += ["wo0", "wo1", "x2T0", "wo2", "lg0", "x2T1", "wo3", "lg1", "x2T2", "wo4", "lg2", "x2T3", "mod10", "lg3",
             "modT10", "x2T4", "lg4", "mod11", "modT11", "pT", "g2_0", "g2_1", "ixT"]
    return jobs


KV_ORDER = [0, 7, 1, 6, 2, 5, 3, 4, 8, 9]
JOBS = first_phase_jobs()
UNITS = ["mod0", "mod1", "mod2", "mod3", "qk", "v", "mod4", "xc", "mod5", "xv", "mod6", "xb", "mod7", "og", "mod8", "wo0",
         "mod9", "wo1", "mod10", "mod11"]
PLACES = [0, 1, 0, 1, 0, 1, 0, 0, 1, 1, 0, 0, 1, 1, 0, 0, 1, 1, 2, 3]
USES = ["mod0", "mod1", "mod2", "mod3", "qk", "mod4", "v", "mod5", "xc", "mod6", "xv", "mod7", "xb", "mod8", "og", "mod9",
        "wo0", "wo1", "mod10", "mod11"]
IN_COLS = {"xb": 0, "xc": 512, "xv": 1024, "qk": 1536, "v": 2048, "og": 2560}


CHUNK_UNITS = ["qk", "v", "xc", "xv", "xb", "og"]
SPLITS = [(name, j) for name in CHUNK_UNITS for j in range(4)]
CHUNK_JOBS = {"qk": ("q0", "q1", "k0", "k1"), "v": ("v4",) * 4,
              **{name: tuple(f"{name}{j}" for j in range(4)) for name in ("xc", "xv", "xb", "og")}}


def unit_place(name):
    n = UNITS.index(name)
    return PLACES[n], PLACES[:n].count(PLACES[n])


def job(name):
    return JOBS.index(name)


def build(nc, x_prompt, x_sample, s_fwd, s_bwd, c, c_ctx, w_mod, b_mod, g_norm1, g_norm2, w_in, w_conv, b_conv,
          w_a_up_f, b_a_f, w_a_up_b, b_a_b, g_gla_norm, w_out, w_router, w_gate, w_up, w_down, g_final,
          y_prompt, y_sample, new_f, new_b):
    ctx = ExitStack()
    with ctx:
        def at(name, offset, shape, dt=F32):
            return nc.alloc_sbuf_tensor_at(name, shape, dt, offset=offset)

        def sem(name):
            return ctx.enter_context(nc.semaphore(name))

        const_next = [A_CONST]

        def small(name, shape, dt=F32):
            n = 4
            for s in shape[1:]:
                n *= s
            t = at(name, const_next[0], shape, dt)
            const_next[0] += (n + 31) // 32 * 32
            assert const_next[0] <= A_G2B
            return t

        x_sb = at("x_sb", A_X, [P, NT, D])
        ident = small("ident", [P, P])
        param = small("param", [P, R_ALL])
        mod = small("mod", [P, NMOD * KC, 2])
        scale1 = small("scale1", [P, KC, 2])
        scale2 = small("scale2", [P, KC, 2])
        eps_col = small("eps_col", [P, 1])
        one_col = small("one_col", [P, 1])
        rms = small("rms", [P, 6, NT])
        hrms = small("hrms", [P, 6, H])
        dec = small("dec", [P, H, NCH])
        smax = small("smax", [P, 3, NT])
        gather_idx = small("gather_idx", [P, E], U32)
        pair_cols = small("pair_cols", [P, 8, E // 2])
        logits = small("logits", [P, NT, E])
        w_router_sb = small("w_router_sb", [P, KC, E])

        gate2b = at("gate2b", A_G2B, [P, 2, D])
        gfin = at("gfin", A_GFIN, [P, D])

        hT = at("hT", R_HLO, [P, KC, T])
        hT_lo = at("hT_lo", R_HLO, [P, KC, T], F32R)
        hT_hi = at("hT_hi", R_HT, [P, KC, T], F32R)
        states = at("states", R_HT, [P, NCH, H, DV])
        u_sb = at("u_sb", R_U, [P, CH, T])
        og_sb = at("og_sb", R_U, [P, H, T])
        qd = at("qd", R_QD, [P, H, T])
        kd = at("kd", R_KD, [P, H, T])
        ksT = at("ksT", R_KST, [P, NT, H, P])
        v_sb = at("v_sb", R_V, [P, NT, H * DV])
        att_sb = at("att_sb", W_HI + 8192, [P, 2, 2, H, P])
        w_hi = at("w_hi", W_HI, [P, KC, 512], F32R)
        final_state = at("final_state", R_FIN, [P, H, DV])
        p1w = [at(f"p1w{i}", RING + slot * SLOT, [P, KC, 512]) for i, slot in enumerate(P1_SLOTS)]
        w_lo = [at(f"w_lo{i}", RING + P1_SLOTS[i] * SLOT, [P, KC, 512], F32R) for i in range(2)]
        yT = at("yT", W_YT, [P, KC, T])
        ks_row = at("ks_row", W_KS, [P, 2, T])
        scan_mask = at("scan_mask", W_KS + 5120, [P, T])
        work_d = at("work_d", W_KS + 7680, [P, T])
        gate1b = at("gate1b", W_HI, [P, 2, D])
        a_lowT = at("a_lowT", R_ALOW, [P, T])
        xr = at("xr", W_XR, [P, 2, D])
        work_a = at("work_a", W_XR, [P, T])
        work_b = at("work_b", W_XR + 2560, [P, T])
        norm_r = at("norm_r", W_XR, [P, H * P])
        norm_sq = at("norm_sq", W_XR + 2048, [P, H * P])
        w_decay = at("w_decay", A_G2B, [P, H, P])
        mod_rows = at("mod_rows", A_G2B + 2048, [P, 2, 512])
        silu_c = at("silu_c", A_G2B + 6144, [P, KC, 32])
        keep_f = at("keep_f", A_G2B + 7168, [P, P])
        keep_b = at("keep_b", A_G2B + 7680, [P, P])
        w_tail = at("w_tail", A_GFIN, [P, KC, 2 * LR])
        param_rows = at("param_rows", A_GFIN + 1024, [R_ALL, P])
        h2T = [at("h2T_0", A_GFIN, [P, KC, P]), at("h2T_1", W_HI + 8192, [P, KC, P])]

        ring = [at(f"ring{i}", RING + i * SLOT, [P, 4, D]) for i in range(RING_SLOTS)]
        xs = at("xs", B_XS, [SLOTS, 2, D])
        xT = at("xT", B_XT, [P, 2, KC, 96])
        act_l = at("act_l", B_G, [P, 512])
        act_c = at("act_c", B_GC, [P, 512])
        aT = at("aT", B_AT, [P, 4, P])
        aTc = at("aTc", B_ATC, [P, 4, 64])
        y_f = at("y_f", B_Y, [P, 2, 2, 512])
        y_lo = at("y_lo", B_Y, [P, 2, 2, 512], F32R)
        y_hi = at("y_hi", B_YH, [P, 2, 2, 512], F32R)
        oh_l = at("oh_l", B_OH, [P, 2, 512], F32R)
        oh_c = at("oh_c", B_OH + 4096, [P, 2, P], F32R)
        iota_f = at("iota_f", B_IOTA, [P, 512])
        RTK = RING + 7 * SLOT
        probs = at("probs", RTK, [P, NT, E])
        probsT = at("probsT", RTK + 512, [E, T])
        topv_l = at("topv_l", RTK + 3072, [E, P])
        topv_c = at("topv_c", RTK + 3584, [E, P])
        topi_l = at("topi_l", RTK + 4096, [E, P], U32)
        topi_c = at("topi_c", RTK + 4608, [E, P], U32)
        selr = at("selr", RTK + 5120, [E, 5, P])

        hn = nc.dram_tensor("hn", [T, D], F32, kind="Internal").ap()

        square_out = at("square_out", RING, [P, 2, D])

        pairs = [ctx.enter_context(nc.psum_tensor(f"pair{i}", [P, 2 * 512], F32)) for i in range(4)]

        names = """job_done prm_in tail_in st_in p1_used const_ready mask_ready param_ready silu_ready o_sum o_mean o_root
            silu_zero decay_zero modrow_ready mod_sum mod_ready scale_ready ss_ready mean_ready root_ready
            xr_ready hT_low hT_high hT_hi_ready hT_ready whi_ready wlo_ready alow_ready qk_first qk_second abs_ready min_ready softplus_ready cum_ready
            exp_b_ready exp_mb_ready dec_ready diff_ready exp_d_ready ks_ready ksT_ready v_sb_ready xc_ready
            u_ready conv_mid conv_ready ya_ready og_act og_ready kv_ready state_step att_ready o_sq o_norm
            yb_ready g1_ready g2_ready wo_read x2_ready h2_low h2_high lg_ready exp_ready
            smax_ready probs_ready probsT_ready selr_ready idx_ready state_out fin_state dve_chain act_chain
            pool_chain gu_used dl_done d_used xTp_done xT_lat xT_ctx xT_zero gul_done silu_lat silu_ctx act_l_ready
            act_c_ready aTp_l aTp_c aT_ready aTc_ready y_read yhi_ready ylo_ready oh_ready sc_done sc_added
            fss_ready fmean_ready froot_ready gfin_in fin_ready fin_out iota_ready""".split()
        (job_done, prm_in, tail_in, st_in, p1_used, const_ready, mask_ready, param_ready, silu_ready, o_sum, o_mean, o_root,
         silu_zero, decay_zero, modrow_ready, mod_sum, mod_ready, scale_ready, ss_ready, mean_ready, root_ready,
         xr_ready, hT_low, hT_high, hT_hi_ready, hT_ready, whi_ready, wlo_ready, alow_ready, qk_first, qk_second, abs_ready, min_ready, softplus_ready, cum_ready,
         exp_b_ready, exp_mb_ready, dec_ready, diff_ready, exp_d_ready, ks_ready, ksT_ready, v_sb_ready, xc_ready,
         u_ready, conv_mid, conv_ready, ya_ready, og_act, og_ready, kv_ready, state_step, att_ready, o_sq,
         o_norm, yb_ready, g1_ready, g2_ready, wo_read, x2_ready, h2_low, h2_high, lg_ready,
         exp_ready, smax_ready, probs_ready, probsT_ready, selr_ready, idx_ready, state_out, fin_state, dve_chain,
         act_chain, pool_chain, gu_used, dl_done, d_used, xTp_done, xT_lat, xT_ctx, xT_zero, gul_done, silu_lat, silu_ctx,
         act_l_ready, act_c_ready, aTp_l, aTp_c, aT_ready, aTc_ready, y_read, yhi_ready, ylo_ready, oh_ready,
         sc_done, sc_added, fss_ready, fmean_ready, froot_ready, gfin_in, fin_ready, fin_out,
         iota_ready) = [sem(n) for n in names]
        x_in = [sem(f"x_in{t}") for t in range(NT)]
        p1_full = [sem(f"p1_full{i}") for i in range(4)]
        w_full = [sem(f"w_full{i}") for i in range(RING_SLOTS)]
        xs_full = [sem(f"xs_full{i}") for i in range(2)]
        hn_out = [sem(f"hn_out{i}") for i in range(2)]

        read_by = {"prm": [(param_ready, 1)], "alow": [(alow_ready, 1)], "pT": [(probsT_ready, 1)]}
        for u in range(12):
            read_by[f"mod{u}"] = [(modrow_ready, u + 1)]
            read_by[f"modT{u}"] = [(mod_sum, u + 1)]
        for t in range(NT):
            read_by[f"xT{t}"] = [(hT_low, t + 1), (hT_high, t + 1)]
            read_by[f"v{t}"] = [(v_sb_ready, t + 1)]
            read_by[f"att{t}"] = [(att_ready, 2 * (t + 1))]
            read_by[f"o{t}"] = [(o_sq, t + 1), (o_norm, t + 1)]
            read_by[f"oT{t}"] = [(yb_ready, t + 1)]
            read_by[f"wo{t}"] = [(wo_read, t + 1)]
            read_by[f"x2T{t}"] = [(h2_low, t + 1), (h2_high, t + 1)]
            read_by[f"lg{t}"] = [(lg_ready, t + 1)]
        for i, n in enumerate(("q0", "q1", "k0", "k1")):
            read_by[n] = [(qk_first, i + 1), (qk_second, i + 1)]
        for h in range(H):
            read_by[f"la{h}"] = [(abs_ready, h + 1), (min_ready, h + 1)]
            read_by[f"ks{h}"] = [(ksT_ready, h + 1)]
            read_by[f"og{h}"] = [(og_act, h + 1)]
        for j in range(CH):
            read_by[f"xc{j}"] = [(xc_ready, j + 1)]
            read_by[f"xv{j}"] = [(u_ready, j + 1)]
            read_by[f"xb{j}"] = [(ya_ready, j + 1)]
        for i, n in enumerate(KV_ORDER):
            read_by[f"kv{n}"] = [(kv_ready, i + 1)]
        for v in range(2):
            read_by[f"g1_{v}"] = [(g1_ready, v + 1)]
            read_by[f"g2_{v}"] = [(g2_ready, v + 1)]

        def vec(t):
            return 0 if t < NT - 1 else 1

        def tile(t):
            return slice(t * P, (t + 1) * P)

        def claim(pe, name):
            n = job(name)
            if n >= 4:
                for signal, value in read_by[JOBS[n - 4]]:
                    pe.wait_ge(signal, value)
            return pairs[n % 4]

        def result(eng, name):
            eng.wait_ge(job_done, job(name) + 1)
            return pairs[job(name) % 4]

        def halves(ap):
            return ap.rearrange("p (s n) -> p s n", s=2)[:, :, 0:HALF]

        def split(ap):
            return ap.rearrange("p (s n) -> p s n", s=2)

        def body_loop(eng, expert):
            expert(0, 0)
            expert(1, 1)
            with eng.Fori(0, 3) as i:
                for j in range(2, 6):
                    expert(4 * i + j, j)
            expert(14, 14)
            expert(15, 15)

        gate_ps, up_ps = pairs[0][:, 0:512], pairs[0][:, 512:1024]
        ctx_ps, sc_ps = pairs[1][:, 0:512], pairs[1][:, 512:1024]
        y_ps = [pairs[3][:, 0:512], pairs[3][:, 512:1024]]
        sc_banks = [sc_ps, y_ps[0], y_ps[1]]
        SC = 2 * NT

        def xT_ps(kk):
            o = kk // 4 * 512 + kk % 4 * SLOTS
            return pairs[2][:, o:o + SLOTS]

        block = ctx.enter_context(nc.Block())

        @block.sync
        def _(sp):

            def load_unit(n):
                name = UNITS[n]
                place, turns = unit_place(name)
                if turns:
                    last = max(i for i in range(n) if PLACES[i] == place)
                    sp.wait_ge(p1_used, USES.index(UNITS[last]) + 1)
                if name.startswith("mod"):
                    src = w_mod[0, :, 512 * int(name[3:]):512 * (int(name[3:]) + 1)]
                elif name.startswith("wo"):
                    src = w_out[0, :, 512 * int(name[2:]):512 * (int(name[2:]) + 1)]
                else:
                    src = w_in[0, :, IN_COLS[name]:IN_COLS[name] + 512]
                sp.dma_start(p1w[place][:, :, :], src.rearrange("(k p) n -> p k n", p=P)).then_inc(p1_full[place], 16)

            sp.dma_start(param_rows[R_C:R_C + KC, :], c[0].rearrange("(r p) -> r p", p=P)).then_inc(prm_in, 16)
            sp.dma_start(param_rows[R_C + KC:R_C + 2 * KC, :], c_ctx.rearrange("(r p) -> r p", p=P)).then_inc(prm_in, 16)
            sp.dma_start(param_rows[R_GLA:R_GLA + H, :], g_gla_norm[0]).then_inc(prm_in, 16)
            sp.dma_start(param_rows[R_BA:R_BA + H, 0:DK], b_a_f[0].rearrange("(h d) -> h d", d=DK)).then_inc(prm_in, 16)
            sp.dma_start(param_rows[R_BA:R_BA + H, DK:P], b_a_b[0].rearrange("(h d) -> h d", d=DK)).then_inc(prm_in, 16)
            load_unit(0)
            for t in range(NT):
                src = x_sample[0, tile(t), :] if t < NT - 1 else x_prompt[0]
                sp.dma_start(x_sb[:, t, :], src).then_inc(x_in[t], 16)
            for n in range(1, 4):
                load_unit(n)
            sp.dma_start(w_tail[:, :, :], w_in[0, :, P_TOT - 2 * LR:].rearrange("(k p) n -> p k n", p=P)
                         ).then_inc(tail_in, 16)
            load_unit(4)
            sp.wait_ge(decay_zero, 1)
            for r in range(0, P, 2 * LR):
                sp.dma_start(w_decay[r:r + LR, :, 0:DK], w_a_up_f[0].rearrange("r (h d) -> r h d", d=DK)
                             ).then_inc(tail_in, 16)
                sp.dma_start(w_decay[r + LR:r + 2 * LR, :, DK:P], w_a_up_b[0].rearrange("r (h d) -> r h d", d=DK)
                             ).then_inc(tail_in, 16)
            sp.dma_start(w_router_sb[:, :, :], w_router[0].rearrange("(k p) n -> p k n", p=P)).then_inc(tail_in, 16)
            for n in range(5, UNITS.index("wo0")):
                load_unit(n)
            sp.wait_ge(job_done, job("og3") + 1)
            sp.dma_start(states[0:DK, 0, :, :], s_fwd[0, 0].rearrange("h d v -> d h v")).then_inc(st_in, 16)
            sp.dma_start(states[DK:P, NCH_LAT - 1, :, :], s_bwd[0, 0].rearrange("h d v -> d h v")).then_inc(st_in, 16)
            for n in range(UNITS.index("wo0"), len(UNITS) - 2):
                load_unit(n)
            sp.wait_ge(fin_state, 1)
            sp.dma_start(new_f[0, 0].rearrange("h d v -> d h v"), final_state[0:DK, :, :]).then_inc(state_out, 16)
            sp.dma_start(new_b[0, 0].rearrange("h d v -> d h v"), final_state[DK:P, :, :]).then_inc(state_out, 16)

            def load_expert(e, k):
                for u in range(6):
                    half = u // 2 if u < 4 else u - 4
                    w = (w_gate, w_up)[u % 2] if u < 4 else w_down
                    n = 6 * k + u
                    if n >= RING_SLOTS:
                        if u < 2:
                            sp.wait_ge(d_used, 2 * e - 3 + u)
                        else:
                            sp.wait_ge(gu_used, 2 * e - 1 + (u - 2) // 2)
                    elif n == 0:
                        sp.wait_ge(yb_ready, NT)
                        load_unit(len(UNITS) - 2)
                        load_unit(len(UNITS) - 1)
                    elif n == P1_SLOTS[3]:
                        sp.wait_ge(p1_used, len(UNITS))
                    elif n == 7:
                        sp.wait_ge(state_out, 32)
                        sp.wait_ge(idx_ready, 2)
                    rows = slice(half * 512, (half + 1) * 512)
                    src = w[0, e, rows, :] if isinstance(e, int) else \
                        w[0, bass.ds(e, 1), rows, :].rearrange("o r n -> (o r) n")
                    sp.dma_start(ring[n % RING_SLOTS][:, :, :], src.rearrange("(k p) n -> p k n", p=P)
                                 ).then_inc(w_full[n % RING_SLOTS], 16)

            body_loop(sp, load_expert)
            sp.dma_start(gfin[:, :], g_final.partition_broadcast(P)).then_inc(gfin_in, 16)
            sp.wait_ge(fin_out, 16 * NT)

        @block.gpsimd
        def _(pool):
            g = nc.gpsimd
            steps = [0]

            def link(ins):
                steps[0] += 1
                ins.then_inc(pool_chain, 1)
                pool.wait_ge(pool_chain, steps[0])

            g.memset(silu_c[:, :, :], 0.0).then_inc(silu_zero, 1)
            g.memset(eps_col[:, :], EPS)
            g.memset(one_col[:, :], 1.0)
            link(g.memset(ident[:, :], 0.0))
            g.affine_select(out=ident[:, :], in_=ident[:, :], compare_op=ALU.not_equal, fill=1.0, base=0,
                            pattern=[[-1, P]], channel_multiplier=1).then_inc(const_ready, 1)
            g.memset(w_decay[:, :, :], 0.0).then_inc(decay_zero, 1)
            link(g.memset(scan_mask[:, :], 1.0))
            g.memset(scan_mask[0:DK, 0:T:C], 0.0).then_inc(mask_ready, 1)
            g.memset(scan_mask[DK:P, C - 1:T:C], 0.0).then_inc(mask_ready, 1)
            pool.wait_ge(mask_ready, 2)
            link(g.memset(keep_f[:, :], 1.0))
            link(g.affine_select(out=keep_f[:, :], in_=keep_f[:, :], compare_op=ALU.is_ge, fill=0.0, base=0,
                                 pattern=[[1, P]], channel_multiplier=-1))
            g.memset(keep_f[0:C, C:P], 0.0).then_inc(mask_ready, 1)
            pool.wait_ge(mask_ready, 3)
            link(g.memset(keep_b[:, :], 1.0))
            link(g.affine_select(out=keep_b[:, :], in_=keep_b[:, :], compare_op=ALU.is_ge, fill=0.0, base=0,
                                 pattern=[[-1, P]], channel_multiplier=1))
            g.memset(keep_b[C:P, 0:C], 0.0).then_inc(mask_ready, 1)
            pool.wait_ge(mask_ready, 4)
            pool.wait_ge(job_done, job("og3") + 1)
            g.memset(att_sb[:, :, :, :, :], 0.0).then_inc(mask_ready, 1)

            pool.wait_ge(mask_ready, 5)
            pool.wait_ge(idx_ready, 2)
            pool.wait_ge(hn_out[0], 48)
            pool.wait_ge(hn_out[1], 32)
            g.iota(iota_f[:, :], pattern=[[1, 512]], base=0, channel_multiplier=0,
                   allow_small_or_imprecise_dtypes=True).then_inc(iota_ready, 1)
            for e in range(E):
                if e >= 2:
                    pool.wait_ge(xTp_done, e - 1)
                g.indirect_dma_start(xs[:, e % 2, :], None, hn[:, :],
                                     bass.IndirectOffsetOnAxis(ap=gather_idx[0:SLOTS, e:e + 1], axis=0)
                                     ).then_inc(xs_full[e % 2], 16)

        @block.scalar
        def _(act):
            a = nc.scalar
            steps = [0]

            def link(ins):
                steps[0] += 1
                ins.then_inc(act_chain, 1)
                act.wait_ge(act_chain, steps[0])

            for r0, src in (
                (R_BMOD, b_mod[0].rearrange("(r p) -> r p", p=P)),
                (R_G1, g_norm1[0].rearrange("(r p) -> r p", p=P)),
                (R_G2, g_norm2[0].rearrange("(r p) -> r p", p=P)),
                (R_CONV, w_conv[0].rearrange("w (r p) -> (w r) p", p=P)),
                (R_BCONV, b_conv[0].rearrange("(r p) -> r p", p=P)),
            ):
                act.dma_start(param_rows[r0:r0 + src.shape[0], :], src).then_inc(prm_in, 16)
            act.wait_ge(param_ready, 1)
            act.wait_ge(silu_zero, 1)
            a.activation(silu_c[:, :, 0:2].rearrange("p k v -> p v k"),
                         param[:, R_C:R_C + 2 * KC].rearrange("p (v k) -> p v k", v=2), ACT.Silu
                         ).then_inc(silu_ready, 1)

            def mod_row(u):
                pp = result(act, f"mod{u}")
                if u >= 2:
                    act.wait_ge(job_done, job(f"modT{u - 2}") + 1)
                a.activation(mod_rows[:, u % 2, :], pp[:, 0:512], ACT.Copy).then_inc(modrow_ready, 1)

            def square_sum(t):
                a.activation(xr[:, t % 2, :], x_sb[:, t, :], ACT.Square, accum_out=rms[:, 0, t:t + 1]
                             ).then_inc(ss_ready, 1)

            mod_row(0)
            for t in range(NT):
                act.wait_ge(x_in[t], 16)
                if t >= 2:
                    act.wait_ge(ss_ready, t - 1)
                square_sum(t)
            act.wait_ge(mean_ready, 1)
            a.activation(rms[:, 2, :], rms[:, 1, :], ACT.Sqrt).then_inc(root_ready, 1)
            for u in range(1, 4):
                mod_row(u)

            def split_hi(name, j):
                place, turns = unit_place(name)
                act.wait_ge(p1_full[place], 16 * (turns + 1))
                if name != "qk":
                    act.wait_ge(job_done, job(CHUNK_JOBS[CHUNK_UNITS[CHUNK_UNITS.index(name) - 1]][j]) + 1)
                a.activation(w_hi[:, :, tile(j)], p1w[place][:, :, tile(j)], ACT.Copy).then_inc(whi_ready, 1)

            act.wait_ge(scale_ready, 1)

            def tokens_low(t):
                pp = result(act, f"xT{t}")
                for k in range(KC // 2):
                    ins = a.activation(hT[:, k, tile(t)], pp[:, k * P:(k + 1) * P], ACT.Identity,
                                       bias=mod[:, k, vec(t):vec(t) + 1], scale=scale1[:, k, vec(t):vec(t) + 1])
                ins.then_inc(hT_low, 1)

            def tokens_hi(t):
                act.wait_ge(hT_low, t + 1)
                act.wait_ge(hT_high, t + 1)
                a.activation(hT_hi[:, :, tile(t)], hT[:, :, tile(t)], ACT.Copy).then_inc(hT_hi_ready, 1)

            for t in range(NT):
                tokens_low(t)
                tokens_hi(t)
                if t == 2:
                    split_hi("qk", 0)
            for j in range(1, 4):
                split_hi("qk", j)

            def q_k(name, dst):
                pp = result(act, name)
                for d in range(2):
                    ins = a.activation(split(dst[d * DK:(d + 1) * DK, 2 * int(name[1]), :]), halves(pp[0:DK, :]), ACT.Copy)
                ins.then_inc(qk_first, 1)

            def decay(h):
                pp = result(act, f"la{h}")
                if h:
                    act.wait_ge(ks_ready, h)
                a.activation(split(work_b[:, :]), halves(pp), ACT.Abs, bias=param[:, R_BA + h:R_BA + h + 1]
                             ).then_inc(abs_ready, 1)
                act.wait_ge(abs_ready, h + 1)
                link(a.activation(work_b[:, :], work_b[:, :], ACT.Exp, scale=-1.0))
                a.activation(work_b[:, :], work_b[:, :], ACT.Ln, bias=one_col[:, 0:1]).then_inc(softplus_ready, 1)
                act.wait_ge(cum_ready, 2 * (h + 1))
                a.activation(work_a[:, :], work_b[:, :], ACT.Exp, scale=1.0 / TAU).then_inc(exp_b_ready, 1)
                a.activation(work_d[:, :], work_b[:, :], ACT.Exp, scale=-1.0 / TAU).then_inc(exp_mb_ready, 1)
                a.activation(dec[0:DK, h, :], work_b[0:DK, C - 1:T:C], ACT.Exp, scale=1.0 / TAU)
                a.activation(dec[DK:P, h, :], work_b[DK:P, 0:T:C], ACT.Exp, scale=1.0 / TAU).then_inc(dec_ready, 1)
                act.wait_ge(diff_ready, h + 1)
                a.activation(work_a[:, :], work_a[:, :], ACT.Exp, scale=1.0 / TAU).then_inc(exp_d_ready, 1)

            def ks_turn(h):
                pp = result(act, f"ks{h}")
                a.activation(ksT[:, :, h, :], pp[:, 0:T].rearrange("p (t n) -> p t n", n=P), ACT.Copy
                             ).then_inc(ksT_ready, 1)

            def values(t):
                pp = result(act, f"v{t}")
                a.activation(v_sb[:, t, :], pp[:, 0:512], ACT.Copy).then_inc(v_sb_ready, 1)

            def conv_input(j):
                pp = result(act, f"xc{j}")
                a.activation(split(u_sb[:, j, :]), halves(pp), ACT.Copy).then_inc(xc_ready, 1)

            for j, (name, dst) in enumerate((("q0", qd), ("q1", qd), ("k0", kd), ("k1", kd))):
                q_k(name, dst)
                split_hi("v", j)
            decay(0)
            values(0)
            values(1)
            decay(1)
            values(2)
            mod_row(4)
            values(3)
            values(4)
            split_hi("xc", 0)
            split_hi("xc", 1)
            ks_turn(0)
            ks_turn(1)
            split_hi("xc", 2)
            split_hi("xc", 3)
            decay(2)
            conv_input(0)
            conv_input(1)
            mod_row(5)
            conv_input(2)
            split_hi("xv", 0)
            split_hi("xv", 1)
            conv_input(3)
            split_hi("xv", 2)
            split_hi("xv", 3)
            ks_turn(2)

            def centre_tap(j):
                act.wait_ge(u_ready, j + 1)
                a.activation(yT[:, j, :], u_sb[:, j, :], ACT.Identity,
                             scale=param[:, R_CONV + CH + j:R_CONV + CH + j + 1],
                             bias=param[:, R_BCONV + j:R_BCONV + j + 1]).then_inc(conv_mid, 1)

            decay(3)
            mod_row(6)
            centre_tap(0)
            centre_tap(1)
            centre_tap(2)
            split_hi("xb", 0)
            split_hi("xb", 1)
            split_hi("xb", 2)
            split_hi("xb", 3)
            centre_tap(3)
            ks_turn(3)
            mod_row(7)
            for j in range(H):
                split_hi("og", j)
            act.wait_ge(conv_ready, CH)
            for j in range(H):
                pp = result(act, f"og{j}")
                a.activation(split(og_sb[:, j, :]), halves(pp), ACT.Silu).then_inc(og_act, 1)
                if j == 1:
                    mod_row(8)

            for n in KV_ORDER:
                pp = result(act, f"kv{n}")
                f_dst = final_state[0:DK] if n == NCH - 1 else None if n == NCH_LAT - 1 else states[0:DK, n + 1]
                b_dst = final_state[DK:P] if n == NCH_LAT else None if n == 0 else states[DK:P, n - 1]
                src = pp[:, 0:512].rearrange("p (h n) -> p h n", h=H)
                if f_dst is not None:
                    ins = a.activation(f_dst, src[0:DK], ACT.Copy)
                if b_dst is not None:
                    ins = a.activation(b_dst, src[DK:P], ACT.Copy)
                ins.then_inc(kv_ready, 1)

            mod_row(9)

            def o_square(t):
                pp = result(act, f"o{t}")
                if t:
                    act.wait_ge(o_sum, t)
                a.activation(norm_sq[:, :], pp[:, 0:512], ACT.Square).then_inc(o_sq, 1)
                act.wait_ge(o_mean, t + 1)
                a.activation(hrms[:, 2, :], hrms[:, 1, :], ACT.Sqrt).then_inc(o_root, 1)

            def gate_row(name, v, dst, ready):
                pp = result(act, name)
                a.activation(dst[:, v, :], pp[:, :], ACT.Copy).then_inc(ready, 1)

            for t in range(NT):
                o_square(t)
                if t >= 3:
                    gate_row(f"g1_{t - 3}", t - 3, gate1b, g1_ready)

            def second_norm(t):
                act.wait_ge(x2_ready, t + 1)
                square_sum(t)
                act.wait_ge(mean_ready, t + 2)
                a.activation(rms[:, 2, t:t + 1], rms[:, 1, t:t + 1], ACT.Sqrt).then_inc(root_ready, 1)
                act.wait_ge(xr_ready, NT + t + 1)
                act.dma_start(hn[tile(t), :], xr[:, t % 2, :]).then_inc(hn_out[t % 2], 16)

            def h2_turn(t):
                pp = result(act, f"x2T{t}")
                if t >= 2:
                    act.wait_ge(job_done, job(f"lg{t - 2}") + 1)
                for k in range(KC // 2):
                    ins = a.activation(h2T[t % 2][:, k, :], pp[:, k * P:(k + 1) * P], ACT.Identity,
                                       bias=mod[:, 3 * KC + k, vec(t):vec(t) + 1],
                                       scale=scale2[:, k, vec(t):vec(t) + 1])
                ins.then_inc(h2_low, 1)

            act.wait_ge(scale_ready, 2)
            for t in range(NT):
                second_norm(t)
                if t >= 1:
                    h2_turn(t - 1)
            mod_row(10)
            h2_turn(NT - 1)
            act.wait_ge(smax_ready, 1)
            a.activation(probs[:, :, :], probs[:, :, :], ACT.Exp).then_inc(exp_ready, 1)
            mod_row(11)
            for v in range(2):
                gate_row(f"g2_{v}", v, gate2b, g2_ready)

            def tokens(e, k):
                act.wait_ge(xTp_done, e + 1)
                for kk in range(KC):
                    ins = a.activation(xT[:, k % 2, kk, 0:CAP_L], xT_ps(kk)[:, 0:CAP_L], ACT.Identity,
                                       bias=mod[:, 3 * KC + kk, 0:1], scale=scale2[:, kk, 0:1])
                ins.then_inc(xT_lat, 1)

            def expert(e, k):
                act.wait_ge(gul_done, e + 1)
                a.activation(act_l[:, :], gate_ps, ACT.Silu).then_inc(silu_lat, 1)
                act.wait_ge(gu_used, 2 * e + 2)
                a.activation(act_c[64:P, :], ctx_ps[0:64, :], ACT.Silu).then_inc(silu_ctx, 1)
                if k < E - 1:
                    tokens(e + 1, k + 1)
                if k % 2 == 1:
                    for kind in range(2):
                        act.wait_ge(y_read, 4 * e + 2 + 2 * kind)
                        a.activation(y_hi[:, kind, :, :], y_f[:, kind, :, :], ACT.Copy).then_inc(yhi_ready, 1)

            tokens(0, 0)
            body_loop(act, expert)

            for t in range(NT):
                act.wait_ge(sc_added, SC * (E // 2 - 1) + 2 * t + 2)
                if t >= 2:
                    act.wait_ge(fss_ready, t - 1)
                a.activation(square_out[:, t % 2, :], x_sb[:, t, :], ACT.Square, accum_out=rms[:, 0, t:t + 1]
                             ).then_inc(fss_ready, 1)
                act.wait_ge(fmean_ready, t + 1)
                a.activation(rms[:, 2, t:t + 1], rms[:, 1, t:t + 1], ACT.Sqrt).then_inc(froot_ready, 1)
            for t in range(NT):
                act.wait_ge(fin_ready, t + 1)
                dst = y_sample[0, tile(t), :] if t < NT - 1 else y_prompt[0]
                act.dma_start(dst, x_sb[:, t, :]).then_inc(fin_out, 16)

        @block.vector
        def _(dve):
            v = nc.vector
            steps = [0]

            def link(ins):
                steps[0] += 1
                ins.then_inc(dve_chain, 1)
                dve.wait_ge(dve_chain, steps[0])

            pp = result(dve, "prm")
            v.tensor_copy(param[:, :], pp[:, 0:R_ALL]).then_inc(param_ready, 1)

            def mean_square(cols, ready):
                v.tensor_scalar(rms[:, 1, cols], rms[:, 0, cols], 1.0 / D, EPS, ALU.mult, ALU.add).then_inc(ready, 1)

            def inverse_root(r, cols):
                link(v.reciprocal(r[:, 3, cols], r[:, 2, cols]))
                link(v.tensor_tensor(r[:, 4, cols], r[:, 3, cols], r[:, 3, cols], ALU.mult))
                link(v.tensor_tensor(r[:, 4, cols], r[:, 4, cols], r[:, 1, cols], ALU.mult))
                link(v.tensor_scalar(r[:, 4, cols], r[:, 4, cols], -0.5, 1.5, ALU.mult, ALU.add))
                link(v.tensor_tensor(r[:, 5, cols], r[:, 3, cols], r[:, 4, cols], ALU.mult))

            def normalise(t):
                v.tensor_scalar(xr[:, t % 2, :], x_sb[:, t, :], rms[:, 5, t:t + 1], None, ALU.mult
                                ).then_inc(xr_ready, 1)

            def modulation(u):
                pp = result(dve, f"modT{u}")
                src = pp[:, 0:512].rearrange("p (j g r) -> p j r g", j=4, g=4)[:, :, 0:2, :]
                cols = slice(4 * u, 4 * u + 4)
                v.tensor_reduce(mod[:, cols, :], src, AX.X, ALU.add).then_inc(mod_sum, 1)
                dve.wait_ge(mod_sum, u + 1)
                v.tensor_tensor(mod[:, cols, :], mod[:, cols, :],
                                param[:, R_BMOD + 4 * u:R_BMOD + 4 * u + 4].unsqueeze(2).to_broadcast([P, 4, 2]),
                                ALU.add).then_inc(mod_ready, 1)

            def scales(dst, chunk, g_row, u):
                dve.wait_ge(mod_ready, u)
                v.scalar_tensor_tensor(out=dst[:, :, :], in0=mod[:, chunk:chunk + KC, :], scalar=1.0,
                                       in1=param[:, g_row:g_row + KC].unsqueeze(2).to_broadcast([P, KC, 2]),
                                       op0=ALU.add, op1=ALU.mult).then_inc(scale_ready, 1)

            dve.wait_ge(ss_ready, NT)
            mean_square(slice(0, NT), mean_ready)
            dve.wait_ge(root_ready, 1)
            inverse_root(rms, slice(0, NT))
            normalise(0)
            normalise(1)
            dve.wait_ge(param_ready, 1)
            for u in range(4):
                modulation(u)

            splits = [0]

            def split_lo(name, j):
                assert SPLITS[splits[0]] == (name, j)
                splits[0] += 1
                place = unit_place(name)[0]
                dve.wait_ge(whi_ready, splits[0])
                v.tensor_tensor(w_lo[place][:, :, tile(j)], p1w[place][:, :, tile(j)],
                                w_hi[:, :, tile(j)].bitcast(F32), ALU.subtract).then_inc(wlo_ready, 1)

            scales(scale1, KC, R_G1, 4)
            dve.wait_ge(scale_ready, 1)
            for t in range(NT):
                pp = result(dve, f"xT{t}")
                for k in range(KC // 2, KC):
                    ins = v.tensor_scalar(hT[:, k, tile(t)], pp[:, k * P:(k + 1) * P],
                                          scale1[:, k, vec(t):vec(t) + 1], mod[:, k, vec(t):vec(t) + 1],
                                          ALU.mult, ALU.add)
                ins.then_inc(hT_high, 1)
                if t + 2 < NT:
                    normalise(t + 2)
                dve.wait_ge(hT_hi_ready, t + 1)
                v.tensor_tensor(hT_lo[:, :, tile(t)], hT[:, :, tile(t)], hT_hi[:, :, tile(t)].bitcast(F32),
                                ALU.subtract).then_inc(hT_ready, 1)
                if t == 2:
                    split_lo("qk", 0)
            for j in range(1, 4):
                split_lo("qk", j)

            def q_k(name, dst):
                pp = result(dve, name)
                for d in range(2):
                    ins = v.tensor_copy(split(dst[d * DK:(d + 1) * DK, 2 * int(name[1]) + 1, :]), halves(pp[DK:P, :]))
                ins.then_inc(qk_second, 1)

            def decay(h):
                pp = result(dve, f"la{h}")
                dve.wait_ge(abs_ready, h + 1)
                v.tensor_scalar(split(work_a[:, :]), halves(pp), param[:, R_BA + h:R_BA + h + 1], 0.0,
                                ALU.add, ALU.min).then_inc(min_ready, 1)
                dve.wait_ge(min_ready, h + 1)
                dve.wait_ge(softplus_ready, h + 1)
                link(v.tensor_tensor(work_a[:, :], work_a[:, :], work_b[:, :], ALU.subtract))
                v.tensor_tensor_scan(work_b[0:DK, :], scan_mask[0:DK, :], work_a[0:DK, :], 0.0,
                                     ALU.mult, ALU.add).then_inc(cum_ready, 1)
                v.tensor_tensor_scan(work_b[DK:P, ::-1], scan_mask[DK:P, ::-1], work_a[DK:P, ::-1], 0.0,
                                     ALU.mult, ALU.add).then_inc(cum_ready, 1)
                dve.wait_ge(exp_b_ready, h + 1)
                dve.wait_ge(qk_first, 4)
                dve.wait_ge(qk_second, 4)
                link(v.scalar_tensor_tensor(out=qd[:, h, :], in0=qd[:, h, :], scalar=float(DK) ** -0.5,
                                            in1=work_a[:, :], op0=ALU.mult, op1=ALU.mult))
                chunks = lambda ap: ap.rearrange("p (n c) -> p n c", c=C)
                v.tensor_tensor(chunks(work_a[0:DK, :]),
                                work_b[0:DK, C - 1:T:C].unsqueeze(2).to_broadcast([DK, NCH, C]),
                                chunks(work_b[0:DK, :]), ALU.subtract)
                v.tensor_tensor(chunks(work_a[DK:P, :]),
                                work_b[DK:P, 0:T:C].unsqueeze(2).to_broadcast([DK, NCH, C]),
                                chunks(work_b[DK:P, :]), ALU.subtract).then_inc(diff_ready, 1)
                if h >= 2:
                    dve.wait_ge(job_done, job(f"ks{h - 2}") + 1)
                dve.wait_ge(exp_d_ready, h + 1)
                v.tensor_tensor(ks_row[:, h % 2, :], kd[:, h, :], work_a[:, :], ALU.mult)
                dve.wait_ge(exp_mb_ready, h + 1)
                v.tensor_tensor(kd[:, h, :], kd[:, h, :], work_d[:, :], ALU.mult).then_inc(ks_ready, 1)

            q_k("q0", qd)
            split_lo("v", 0)
            q_k("q1", qd)
            split_lo("v", 1)
            pp = result(dve, "alow")
            v.tensor_copy(split(a_lowT[:, :]), halves(pp)).then_inc(alow_ready, 1)
            q_k("k0", kd)
            split_lo("v", 2)
            q_k("k1", kd)
            split_lo("v", 3)
            dve.wait_ge(mask_ready, 4)
            decay(0)
            decay(1)
            for j in range(3):
                split_lo("xc", j)
            modulation(4)
            split_lo("xc", 3)
            decay(2)
            split_lo("xv", 0)
            split_lo("xv", 1)
            modulation(5)
            split_lo("xv", 2)
            split_lo("xv", 3)

            def gated_input(j):
                pp = result(dve, f"xv{j}")
                dve.wait_ge(xc_ready, j + 1)
                v.tensor_tensor(split(u_sb[:, j, :]), split(u_sb[:, j, :]), halves(pp), ALU.mult
                                ).then_inc(u_ready, 1)

            def side_taps(j):
                dve.wait_ge(conv_mid, j + 1)
                w0 = param[:, R_CONV + j:R_CONV + j + 1]
                w2 = param[:, R_CONV + 2 * CH + j:R_CONV + 2 * CH + j + 1]
                for lo, hi, width in ((0, T_LAT, GRID_W), (T_LAT, T, T_CTX)):
                    y = yT[:, j, lo:hi].rearrange("p (r w) -> p r w", w=width)
                    x = u_sb[:, j, lo:hi].rearrange("p (r w) -> p r w", w=width)
                    link(v.scalar_tensor_tensor(out=y[:, :, 1:], in0=x[:, :, :width - 1], scalar=w0,
                                                in1=y[:, :, 1:], op0=ALU.mult, op1=ALU.add))
                    ins = v.scalar_tensor_tensor(out=y[:, :, :width - 1], in0=x[:, :, 1:], scalar=w2,
                                                 in1=y[:, :, :width - 1], op0=ALU.mult, op1=ALU.add)
                ins.then_inc(conv_ready, 1)

            gated_input(0)
            decay(3)
            gated_input(1)
            side_taps(0)
            gated_input(2)
            modulation(6)
            split_lo("xb", 0)
            split_lo("xb", 1)
            side_taps(1)
            gated_input(3)
            split_lo("xb", 2)
            split_lo("xb", 3)
            side_taps(2)
            side_taps(3)

            def gated_conv(j):
                pp = result(dve, f"xb{j}")
                dve.wait_ge(conv_ready, j + 1)
                v.tensor_tensor(split(yT[:, j, :]), split(yT[:, j, :]), halves(pp), ALU.mult).then_inc(ya_ready, 1)

            for j in range(3):
                gated_conv(j)
            modulation(7)
            split_lo("og", 0)
            split_lo("og", 1)
            gated_conv(3)
            split_lo("og", 2)
            split_lo("og", 3)
            for j in range(H):
                dve.wait_ge(og_act, j + 1)
                v.tensor_scalar(og_sb[:, j, :], og_sb[:, j, :], param[:, R_GLA + j:R_GLA + j + 1], None, ALU.mult
                                ).then_inc(og_ready, 1)
                if j == 2:
                    modulation(8)

            dve.wait_ge(job_done, job("og3") + 1)
            v.memset(states[0:DK, NCH_LAT, :, :], 0.0).then_inc(state_step, 1)
            v.memset(states[DK:P, NCH - 1, :, :], 0.0).then_inc(state_step, 1)

            def state(n, d):
                rows = slice(0, DK) if d == 0 else slice(DK, P)
                m = n + 1 if d == 0 else n - 1
                last = (n == NCH - 1 and d == 0) or (n == NCH_LAT and d == 1)
                dst = final_state[rows] if last else states[rows, m]
                for h in range(H):
                    ins = v.scalar_tensor_tensor(out=dst[:, h, :], in0=states[rows, n, h, :],
                                                 scalar=dec[rows, h, n:n + 1], in1=dst[:, h, :],
                                                 op0=ALU.mult, op1=ALU.add)
                return ins

            dve.wait_ge(st_in, 32)
            dve.wait_ge(dec_ready, H)
            for i in range(NCH_LAT - 1):
                for d in range(2):
                    n = i if d == 0 else NCH_LAT - 1 - i
                    dve.wait_ge(kv_ready, KV_ORDER.index(n) + 1)
                    if i:
                        dve.wait_ge(state_step, 2 * i + d + 1)
                    state(n, d).then_inc(state_step, 1)
            STEPS = 2 * NCH_LAT
            dve.wait_ge(kv_ready, len(KV_ORDER))
            dve.wait_ge(state_step, 2)
            state(NCH_LAT, 0).then_inc(state_step, 1)
            state(NCH - 1, 1).then_inc(state_step, 1)
            dve.wait_ge(state_step, STEPS + 2)
            state(NCH - 1, 0)
            state(NCH_LAT, 1).then_inc(fin_state, 1)

            def att_mask(t):
                pp = result(dve, f"att{t}")
                if t >= 2:
                    dve.wait_ge(job_done, job(f"o{t - 2}") + 1)
                for d, keep in enumerate((keep_f, keep_b)):
                    v.copy_predicated(att_sb[:, t % 2, d, :, :],
                                      keep[:, :].bitcast(I32).unsqueeze(1).to_broadcast([P, H, P]),
                                      pp[:, d * 512:(d + 1) * 512].rearrange("p (h n) -> p h n", h=H)
                                      ).then_inc(att_ready, 1)

            dve.wait_ge(mask_ready, 5)
            att_mask(0)
            att_mask(1)
            modulation(9)
            scales(scale2, 4 * KC, R_G2, 10)
            heads = lambda ap: ap.rearrange("p (h n) -> p h n", h=H)

            def head_norm(t):
                dve.wait_ge(o_sq, t + 1)
                v.tensor_reduce(hrms[:, 0, :], heads(norm_sq[:, :]), AX.X, ALU.add).then_inc(o_sum, 1)
                dve.wait_ge(o_sum, t + 1)
                v.tensor_scalar(hrms[:, 1, :], hrms[:, 0, :], 1.0 / DV, EPS, ALU.mult, ALU.add).then_inc(o_mean, 1)
                dve.wait_ge(o_root, t + 1)
                inverse_root(hrms, slice(0, H))
                pp = result(dve, f"o{t}")
                if t:
                    dve.wait_ge(job_done, job(f"oT{t - 1}") + 1)
                v.tensor_tensor(heads(norm_r[:, :]), heads(pp[:, 0:512]),
                                hrms[:, 5, :].unsqueeze(2).to_broadcast([P, H, DV]), ALU.mult).then_inc(o_norm, 1)

            def gated(t):
                pp = result(dve, f"oT{t}")
                dve.wait_ge(og_ready, H)
                v.tensor_tensor(yT[:, CH:KC, tile(t)], heads(pp[:, 0:512]), og_sb[:, :, tile(t)], ALU.mult
                                ).then_inc(yb_ready, 1)

            for t in range(NT):
                if t + 2 < NT:
                    att_mask(t + 2)
                head_norm(t)
                gated(t)

            dve.wait_ge(g1_ready, 2)

            def high_chunks(t):
                pp = result(dve, f"x2T{t}")
                if t >= 2:
                    dve.wait_ge(job_done, job(f"lg{t - 2}") + 1)
                for k in range(KC // 2, KC):
                    ins = v.tensor_scalar(h2T[t % 2][:, k, :], pp[:, k * P:(k + 1) * P],
                                          scale2[:, k, vec(t):vec(t) + 1], mod[:, 3 * KC + k, vec(t):vec(t) + 1],
                                          ALU.mult, ALU.add)
                ins.then_inc(h2_high, 1)

            def router_row(t):
                pp = result(dve, f"lg{t}")
                v.tensor_copy(logits[:, t, :], pp[:, 0:E]).then_inc(lg_ready, 1)

            dve.wait_ge(scale_ready, 2)
            for t in range(NT):
                pp = result(dve, f"wo{t}")
                if t >= 2:
                    dve.wait_ge(hn_out[t % 2], 16 * (t // 2))
                    dve.wait_ge(job_done, job(f"x2T{t - 2}") + 1)
                v.tensor_tensor(xr[:, t % 2, :], pp[:, :], gate1b[:, vec(t), :], ALU.mult).then_inc(wo_read, 1)
                dve.wait_ge(wo_read, t + 1)
                v.tensor_tensor(x_sb[:, t, :], x_sb[:, t, :], xr[:, t % 2, :], ALU.add).then_inc(x2_ready, 1)
                dve.wait_ge(ss_ready, NT + t + 1)
                mean_square(slice(t, t + 1), mean_ready)
                dve.wait_ge(root_ready, t + 2)
                inverse_root(rms, slice(t, t + 1))
                normalise(t)
                if t >= 1:
                    high_chunks(t - 1)
                if t >= 2:
                    router_row(t - 2)
            router_row(NT - 2)
            modulation(10)
            high_chunks(NT - 1)
            router_row(NT - 1)

            dve.wait_ge(lg_ready, NT)
            dve.wait_ge(job_done, job("wo4") + 1)
            link(v.tensor_reduce(smax[:, 0, :], logits[:, :, :], AX.X, ALU.max))
            v.tensor_tensor(probs[:, :, :], logits[:, :, :], smax[:, 0, :].unsqueeze(2).to_broadcast([P, NT, E]),
                            ALU.subtract).then_inc(smax_ready, 1)
            dve.wait_ge(exp_ready, 1)
            link(v.tensor_reduce(smax[:, 1, :], probs[:, :, :], AX.X, ALU.add))
            link(v.reciprocal(smax[:, 2, :], smax[:, 1, :]))
            v.tensor_tensor(probs[:, :, :], probs[:, :, :], smax[:, 2, :].unsqueeze(2).to_broadcast([P, NT, E]),
                            ALU.mult).then_inc(probs_ready, 1)
            modulation(11)
            pp = result(dve, "pT")
            v.tensor_copy(probsT[:, :], pp[0:E, 0:T]).then_inc(probsT_ready, 1)
            dve.wait_ge(probsT_ready, 1)

            for lo, hi, cap, top_v, top_i in ((0, T_LAT, CAP_L, topv_l, topi_l), (T_LAT, T, CAP_C, topv_c, topi_c)):
                for r in range(cap // 8):
                    eight = slice(8 * r, 8 * r + 8)
                    link(v.max(top_v[:, eight], probsT[:, lo:hi]))
                    v.max_index(top_i[:, eight], top_v[:, eight], probsT[:, lo:hi])
                    if r < cap // 8 - 1:
                        link(v.match_replace(probsT[:, lo:hi], top_v[:, eight], probsT[:, lo:hi], -1.0))

            four = lambda ap: ap.rearrange("e (b s) -> e b s", s=32)
            v.memset(selr[:, 0:2, :], 0.0)
            v.memset(selr[:, 2, :], -1.0)
            link(v.memset(selr[:, 3:5, :], 0.0))
            for b in range(2):
                v.tensor_copy(selr[:, 0, b * CAP_L:(b + 1) * CAP_L], topi_l[:, 0:CAP_L])
                v.tensor_copy(selr[:, 1, b * CAP_L:(b + 1) * CAP_L], topv_l[:, 0:CAP_L])
            v.tensor_copy(four(selr[:, 2, :])[:, :, 0:CAP_C],
                          topi_c[:, 0:CAP_C].unsqueeze(1).to_broadcast([E, 4, CAP_C]))
            v.tensor_copy(four(selr[:, 3, :])[:, :, 0:CAP_C],
                          topv_c[:, 0:CAP_C].unsqueeze(1).to_broadcast([E, 4, CAP_C]))
            v.tensor_copy(selr[:, 4, 0:CAP_L], topi_l[:, 0:CAP_L])
            v.tensor_scalar(selr[:, 4, CAP_L:SLOTS], topi_c[:, 0:CAP_C], float(T_LAT), None, ALU.add
                            ).then_inc(selr_ready, 1)
            pp = result(dve, "ixT")
            v.tensor_copy(gather_idx[0:SLOTS, :], pp[0:SLOTS, 4 * E:5 * E]).then_inc(idx_ready, 1)
            src = pp[:, 0:4 * E].rearrange("p (q n two) -> p q n two", q=4, two=2)
            dst = pair_cols[:, :, :].rearrange("p (q o) n -> p q o n", o=2)
            v.tensor_copy(dst[0:64, :, 0, :], src[0:64, :, :, 0])
            v.tensor_copy(dst[0:64, :, 1, :], src[0:64, :, :, 1])
            v.tensor_copy(dst[64:P, :, 0, :], src[64:P, :, :, 1])
            v.tensor_copy(dst[64:P, :, 1, :], src[64:P, :, :, 0]).then_inc(idx_ready, 1)

            def col(q, o, pair):
                return pair_cols[:, 2 * q + o, pair:pair + 1] if isinstance(pair, int) else \
                    pair_cols[:, 2 * q + o, bass.ds(pair, 1)]

            def tokens(e, k):
                dve.wait_ge(xT_lat, e + 1)
                src = pairs[2][:, :].rearrange("p (b n) -> p b n", b=2)[:, :, 0:4 * SLOTS].rearrange(
                    "p b (k s) -> p b k s", s=SLOTS)[:, :, :, CAP_L:SLOTS]
                dst = xT[:, k % 2, :, CAP_L:SLOTS].rearrange("p (b k) s -> p b k s", b=2)
                by = lambda ap: ap.rearrange("p (b k) v -> p b k v", b=2).to_broadcast([P, 2, 4, CAP_C])
                v.tensor_tensor(dst, src, by(scale2[:, :, 1:2]), ALU.mult).then_inc(xT_ctx, 1)
                dve.wait_ge(xT_ctx, 2 * e + 1)
                v.tensor_tensor(dst, dst, by(mod[:, 3 * KC:4 * KC, 1:2]), ALU.add).then_inc(xT_ctx, 1)

            def add_back(base, n):
                t, half = n // 2, n % 2
                cols = slice(half * 512, (half + 1) * 512)
                dve.wait_ge(sc_done, base + n + 1)
                v.tensor_tensor(x_sb[:, t, cols], x_sb[:, t, cols], sc_banks[n % 3], ALU.add).then_inc(sc_added, 1)

            def expert(e, k):
                q = k % 2
                if q == 0 and k > 0:
                    for n in range(6):
                        add_back(5 * e - SC, n)
                dve.wait_ge(silu_lat, e + 1)
                v.tensor_tensor(act_l[:, :], act_l[:, :], up_ps, ALU.mult).then_inc(act_l_ready, 1)
                if q == 0 and k > 0:
                    for n in range(6, 8):
                        add_back(5 * e - SC, n)
                dve.wait_ge(aTp_l, e + 1)
                v.tensor_copy(aT[:, :, :], gate_ps.rearrange("p (j n) -> p j n", j=4)).then_inc(aT_ready, 1)
                dve.wait_ge(silu_ctx, e + 1)
                v.tensor_tensor(act_c[0:64, :], act_c[64:P, :], ctx_ps[64:P, :], ALU.mult).then_inc(act_c_ready, 1)
                if q == 0 and k > 0:
                    for n in range(8, SC):
                        add_back(5 * e - SC, n)
                dve.wait_ge(aTp_c, e + 1)
                v.tensor_copy(aTc[:, :, :], ctx_ps.rearrange("p (j n) -> p j n", j=4)[:, :, 0:64]).then_inc(aTc_ready, 1)
                if k < E - 1:
                    tokens(e + 1, k + 1)
                pair = k // 2 if isinstance(e, int) else pair_of[0]
                if q == 0:
                    dve.wait_ge(iota_ready, 1)
                    for o in range(2):
                        v.tensor_scalar(oh_l[:, o, :], iota_f[:, :], col(0, o, pair), None, ALU.is_equal)
                        ins = v.tensor_scalar(oh_c[:, o, :], iota_f[:, 0:P], col(2, o, pair), None, ALU.is_equal)
                    ins.then_inc(oh_ready, 1)
                for kind in range(2):
                    dve.wait_ge(*((dl_done, e + 1) if kind == 0 else (d_used, 2 * e + 2)))
                    for half in range(2):
                        r = 64 * (half ^ q)
                        v.scalar_tensor_tensor(out=y_f[r:r + 64, kind, half, :], in0=y_ps[kind][r:r + 64, :],
                                               scalar=col(2 * kind + 1, half, pair)[r:r + 64],
                                               in1=gate2b[r:r + 64, kind, half * 512:(half + 1) * 512],
                                               op0=ALU.mult, op1=ALU.mult).then_inc(y_read, 1)
                    if q == 1:
                        dve.wait_ge(yhi_ready, 2 * pair + kind + 1)
                        v.tensor_tensor(y_lo[:, kind, :, :], y_f[:, kind, :, :], y_hi[:, kind, :, :].bitcast(F32),
                                        ALU.subtract).then_inc(ylo_ready, 1)

            pair_of = [0]

            def dve_loop():
                expert(0, 0)
                expert(1, 1)
                with dve.Fori(0, 3) as i:
                    for j in range(2, 6):
                        pair_of[0] = 2 * i + j // 2
                        expert(4 * i + j, j)
                expert(14, 14)
                expert(15, 15)

            dve.wait_ge(g2_ready, 2)
            v.memset(xT[:, :, :, SLOTS:96], 0.0).then_inc(xT_zero, 1)
            tokens(0, 0)
            dve_loop()
            for n in range(SC):
                add_back(SC * (E // 2 - 1), n)
            dve.wait_ge(gfin_in, 16)
            for t in range(NT):
                dve.wait_ge(fss_ready, t + 1)
                mean_square(slice(t, t + 1), fmean_ready)
                dve.wait_ge(froot_ready, t + 1)
                inverse_root(rms, slice(t, t + 1))
                v.scalar_tensor_tensor(out=x_sb[:, t, :], in0=x_sb[:, t, :], scalar=rms[:, 5, t:t + 1],
                                       in1=gfin[:, :], op0=ALU.mult, op1=ALU.mult).then_inc(fin_ready, 1)

        @block.tensor
        def _(pe):
            mm, turn = nc.tensor.matmul, nc.tensor.transpose
            units_used = [0]

            def unit_wait(name):
                place, turns = unit_place(name)
                pe.wait_ge(p1_full[place], 16 * (turns + 1))
                return p1w[place]

            def use_signal(name):
                assert USES[units_used[0]] == name
                units_used[0] += 1
                pe.wait_ge(job_done, done[0])
                pe.sem_inc(p1_used, 1)

            done = [0]

            def end(ins, name):
                assert JOBS[done[0]] == name, (JOBS[done[0]], name)
                done[0] += 1
                ins.then_inc(job_done, 1)

            def turn_params():
                pe.wait_ge(prm_in, 160)
                pe.wait_ge(const_ready, 1)
                pp = claim(pe, "prm")
                end(turn(pp[:, 0:R_ALL], param_rows[:, :], ident[0:R_ALL, 0:R_ALL]), "prm")

            def mod_products(u):
                w = unit_wait(f"mod{u}")
                pe.wait_ge(silu_ready, 1)
                pp = claim(pe, f"mod{u}")
                for k in range(KC):
                    g = 32 * (k % 4)
                    ins = mm(pp[g:g + 32, 0:512], silu_c[:, k, :], w[:, k, :], start=k < 4, stop=k >= 4)
                end(ins, f"mod{u}")
                use_signal(f"mod{u}")

            def mod_turn(u):
                pe.wait_ge(modrow_ready, u + 1)
                pp = claim(pe, f"modT{u}")
                for j in range(4):
                    ins = turn(pp[:, tile(j)], mod_rows[:, u % 2, tile(j)], ident[:, :])
                end(ins, f"modT{u}")

            def turn_rows(name, ready, t):
                pe.wait_ge(xr_ready, ready)
                pp = claim(pe, name)
                for k in range(KC):
                    ins = turn(pp[:, tile(k)], xr[:, t % 2, tile(k)], ident[:, :])
                end(ins, name)

            def passes(w_hi_part, w_lo_part, tokens_hi_part, tokens_lo_part):
                return ((w_hi_part, tokens_hi_part), (w_hi_part, tokens_lo_part), (w_lo_part, tokens_hi_part))

            def project(name, unit, j):
                pe.wait_ge(wlo_ready, SPLITS.index((unit, j)) + 1)
                lo = w_lo[unit_place(unit)[0]]
                pp = claim(pe, name)
                for s in range(2):
                    pe.wait_ge(hT_ready, 3 if s == 0 else NT)
                    tok = slice(s * HALF, (s + 1) * HALF)
                    for k in range(KC):
                        for i, (w, h) in enumerate(passes(w_hi[:, k, tile(j)], lo[:, k, tile(j)],
                                                          hT_hi[:, k, tok], hT_lo[:, k, tok])):
                            ins = mm(pp[:, s * 512:s * 512 + HALF], w, h, start=k == 0 and i == 0,
                                     stop=k == KC - 1 and i == 2)
                end(ins, name)

            def low_rank():
                pe.wait_ge(tail_in, 16)
                pp = claim(pe, "alow")
                for s in range(2):
                    tok = slice(s * HALF, (s + 1) * HALF)
                    for k in range(KC):
                        g = 32 * (k % 4)
                        for i, h in enumerate((hT_hi, hT_lo)):
                            ins = mm(pp[g:g + 32, s * 512:s * 512 + HALF], w_tail[:, k, :],
                                     h[:, k, tok].bitcast(F32), start=k < 4 and i == 0, stop=k >= 4 and i == 1)
                end(ins, "alow")

            def log_decay(h):
                pe.wait_ge(alow_ready, 1)
                pe.wait_ge(tail_in, 144)
                pp = claim(pe, f"la{h}")
                for s in range(2):
                    ins = mm(pp[:, s * 512:s * 512 + HALF], w_decay[:, h, :], a_lowT[:, s * HALF:(s + 1) * HALF],
                             start=True, stop=True)
                end(ins, f"la{h}")

            def values(t):
                lo = w_lo[unit_place("v")[0]]
                pp = claim(pe, f"v{t}")
                for s in range(2):
                    pe.wait_ge(wlo_ready, SPLITS.index(("v", 2 * s + 1)) + 1)
                    cols = slice(256 * s, 256 * s + 256)
                    for k in range(KC):
                        for i, (w, h) in enumerate(passes(w_hi[:, k, cols], lo[:, k, cols],
                                                          hT_hi[:, k, tile(t)], hT_lo[:, k, tile(t)])):
                            ins = mm(pp[:, cols], h, w, start=k == 0 and i == 0, stop=k == KC - 1 and i == 2)
                end(ins, f"v{t}")

            def turn_ks(h):
                pe.wait_ge(ks_ready, h + 1)
                pp = claim(pe, f"ks{h}")
                for t in range(NT):
                    ins = turn(pp[:, tile(t)], ks_row[:, h % 2, tile(t)], ident[:, :])
                end(ins, f"ks{h}")

            turn_params()
            mod_products(0)
            mod_products(1)
            mod_turn(0)
            mod_products(2)
            mod_turn(1)
            mod_turn(2)
            turn_rows("xT0", 1, 0)
            turn_rows("xT1", 2, 1)
            mod_products(3)
            mod_turn(3)
            for t in range(2, NT):
                turn_rows(f"xT{t}", t + 1, t)
            project("q0", "qk", 0)
            project("q1", "qk", 1)
            low_rank()
            project("k0", "qk", 2)
            project("k1", "qk", 3)
            use_signal("qk")
            log_decay(0)
            log_decay(1)
            values(0)
            values(1)
            values(2)
            mod_products(4)
            values(3)
            values(4)
            use_signal("v")
            turn_ks(0)
            turn_ks(1)
            mod_turn(4)
            log_decay(2)
            for name, u in (("xc", 5), ("xv", 6), ("xb", 7), ("og", 8)):
                project(f"{name}0", name, 0)
                if name == "xv":
                    log_decay(3)
                project(f"{name}1", name, 1)
                mod_products(u)
                project(f"{name}2", name, 2)
                mod_turn(u)
                project(f"{name}3", name, 3)
                use_signal(name)
                if name == "xc":
                    turn_ks(2)
                elif name == "xv":
                    turn_ks(3)

            pe.wait_ge(ksT_ready, H)
            pe.wait_ge(v_sb_ready, NT)
            for n in KV_ORDER:
                pp = claim(pe, f"kv{n}")
                r = slice(n % 2 * C, n % 2 * C + C)
                for h in range(H):
                    ins = mm(pp[:, tile(h)], ksT[r, n // 2, h, :], v_sb[r, n // 2, tile(h)], start=True, stop=True)
                end(ins, f"kv{n}")

            def attention(t):
                pp = claim(pe, f"att{t}")
                for d in range(2):
                    r = slice(d * DK, (d + 1) * DK)
                    for h in range(H):
                        ins = mm(pp[:, d * 512 + h * P:d * 512 + (h + 1) * P], kd[r, h, tile(t)], qd[r, h, tile(t)],
                                 start=True, stop=True)
                end(ins, f"att{t}")

            def head_outputs(t):
                pe.wait_ge(att_ready, 2 * (t + 1))
                pp = claim(pe, f"o{t}")
                for h in range(H):
                    for d in range(2):
                        mm(pp[:, tile(h)], att_sb[:, t % 2, d, h, :], v_sb[:, t, tile(h)], start=d == 0, stop=False)
                    for j in range(2):
                        n = 2 * t + j
                        ins = mm(pp[j * C:(j + 1) * C, tile(h)], qd[:, h, n * C:(n + 1) * C], states[:, n, h, :],
                                 start=False, stop=True)
                end(ins, f"o{t}")

            def turn_heads(t):
                pe.wait_ge(o_norm, t + 1)
                pp = claim(pe, f"oT{t}")
                for h in range(H):
                    ins = turn(pp[:, tile(h)], norm_r[:, tile(h)], ident[:, :])
                end(ins, f"oT{t}")

            def gate_rows(which, chunk, v):
                pp = claim(pe, f"g{which}_{v}")
                for k in range(KC):
                    ins = mm(pp[:, tile(k)], mod[:, chunk + k, v:v + 1].to_broadcast([P, P]), ident[:, :],
                             start=True, stop=True)
                end(ins, f"g{which}_{v}")

            attention(0)
            attention(1)
            mod_products(9)
            mod_turn(9)
            pe.wait_ge(state_step, 2 * NCH_LAT + 2)
            pe.wait_ge(mod_ready, 10)
            head_outputs(0)
            attention(2)
            head_outputs(1)
            turn_heads(0)
            attention(3)
            head_outputs(2)
            turn_heads(1)
            attention(4)
            head_outputs(3)
            turn_heads(2)
            gate_rows(1, 2 * KC, 0)
            head_outputs(4)
            turn_heads(3)
            gate_rows(1, 2 * KC, 1)
            turn_heads(4)

            def output_projection(t):
                pe.wait_ge(yb_ready, t + 1)
                ws = [unit_wait("wo0"), unit_wait("wo1")]
                pp = claim(pe, f"wo{t}")
                for half in range(2):
                    for k in range(KC):
                        ins = mm(pp[:, half * 512:(half + 1) * 512], yT[:, k, tile(t)], ws[half][:, k, :],
                                 start=k == 0, stop=k == KC - 1)
                end(ins, f"wo{t}")

            def router(t):
                pe.wait_ge(h2_low, t + 1)
                pe.wait_ge(h2_high, t + 1)
                pp = claim(pe, f"lg{t}")
                for k in range(KC):
                    ins = mm(pp[:, 0:E], h2T[t % 2][:, k, :], w_router_sb[:, k, :], start=k == 0, stop=k == KC - 1)
                end(ins, f"lg{t}")

            pe.wait_ge(ya_ready, CH)
            output_projection(0)
            output_projection(1)
            turn_rows("x2T0", NT + 1, 0)
            output_projection(2)
            router(0)
            turn_rows("x2T1", NT + 2, 1)
            output_projection(3)
            router(1)
            turn_rows("x2T2", NT + 3, 2)
            output_projection(4)
            use_signal("wo0")
            use_signal("wo1")
            router(2)
            turn_rows("x2T3", NT + 4, 3)
            mod_products(10)
            router(3)
            mod_turn(10)
            turn_rows("x2T4", NT + 5, 4)
            router(4)
            mod_products(11)
            mod_turn(11)

            pe.wait_ge(probs_ready, 1)
            pp = claim(pe, "pT")
            for t in range(NT):
                ins = turn(pp[0:E, tile(t)], probs[:, t, :], ident[:, :])
            end(ins, "pT")
            pe.wait_ge(mod_ready, 12)
            gate_rows(2, 5 * KC, 0)
            gate_rows(2, 5 * KC, 1)
            pe.wait_ge(selr_ready, 1)
            pp = claim(pe, "ixT")
            for q in range(5):
                ins = turn(pp[:, q * E:(q + 1) * E], selr[:, q, :], ident[0:E, 0:E])
            end(ins, "ixT")

            def turn_tokens(e, k):
                pe.wait_ge(xs_full[k % 2], 16 * (e // 2 + 1) if isinstance(e, int) else 8 * e + (16 if k % 2 == 0 else 8))
                if k > 0:
                    pe.wait_ge(xT_lat, e)
                    pe.wait_ge(xT_ctx, 2 * e)
                for kk in range(KC):
                    ins = turn(xT_ps(kk), xs[:, k % 2, tile(kk)], ident[0:SLOTS, 0:SLOTS])
                ins.then_inc(xTp_done, 1)

            def scatter(base, n):
                t, half = n // 2, n % 2
                kind = vec(t)
                if n >= 3:
                    pe.wait_ge(sc_added, base + n - 2)
                else:
                    pe.wait_ge(sc_added, base)
                oh = oh_l[:, half, tile(t)] if kind == 0 else oh_c[:, half, :]
                mm(sc_banks[n % 3], oh, y_hi[:, kind, half, :], start=True, stop=False)
                mm(sc_banks[n % 3], oh, y_lo[:, kind, half, :], start=False, stop=True).then_inc(sc_done, 1)

            def weights(e, k, u):
                n = 6 * k + u
                slot = n % RING_SLOTS
                count = 16 * (n // RING_SLOTS + 1)
                pe.wait_ge(w_full[slot], count if isinstance(e, int) else 12 * (e - k) + count)
                return ring[slot]

            def expert(e, k):
                q = k % 2
                add = q == 0 and k > 0
                base = 5 * e - SC
                xt = xT[:, k % 2]
                pe.wait_ge(xT_lat, e + 1)
                pe.wait_ge(xT_ctx, 2 * e + 2)
                if k > 0:
                    pe.wait_ge(aT_ready, e)
                    pe.wait_ge(aTc_ready, e)
                for half in range(2):
                    wg, wu = weights(e, k, 2 * half), weights(e, k, 2 * half + 1)
                    for j in range(4):
                        kk = 4 * half + j
                        for ps, w in ((gate_ps, wg), (up_ps, wu)):
                            for n in range(2):
                                ins = mm(ps[64 * n:64 * n + 64, :], xt[:, kk, 0:CAP_L], w[:, j, n * 512:(n + 1) * 512],
                                         start=kk == 0, stop=kk == KC - 1)
                    if half == 1:
                        ins.then_inc(gul_done, 1)
                    if add:
                        if half == 0:
                            pe.wait_ge(ylo_ready, e if isinstance(e, int) else 2 * pair_of[0])
                            pe.wait_ge(oh_ready, base // SC + 1 if isinstance(e, int) else pair_of[0])
                            pe.wait_ge(y_read, 4 * e)
                        for n in ((0, 1, 2), (6, 7))[half]:
                            scatter(base, n)
                    for j in range(4):
                        kk = 4 * half + j
                        for g in range(4):
                            n, w = g % 2, (wg, wu)[g // 2]
                            ins = mm(ctx_ps[32 * g:32 * g + 32, :], xt[:, kk, CAP_L:96], w[:, j, n * 512:(n + 1) * 512],
                                     start=kk == 0, stop=kk == KC - 1)
                        if half == 1 and j == 2:
                            pe.wait_ge(act_l_ready, e + 1)
                            for jl in range(4):
                                turned = turn(gate_ps[:, tile(jl)], act_l[:, tile(jl)], ident[:, :])
                            turned.then_inc(aTp_l, 1)
                    ins.then_inc(gu_used, 1)
                    if add:
                        for n in ((3, 4, 5), (8, 9))[half]:
                            scatter(base, n)
                if k < E - 1:
                    turn_tokens(e + 1, k + 1)
                pe.wait_ge(aT_ready, e + 1)
                if k > 0:
                    pe.wait_ge(y_read, 4 * e)
                if add:
                    pe.wait_ge(sc_added, base + 8)
                for fh in range(2):
                    wd = weights(e, k, 4 + fh)
                    for j in range(4):
                        for n in range(2):
                            r = 64 * (n ^ q)
                            ins = mm(y_ps[0][r:r + 64, :], aT[:, j, 64 * fh:64 * fh + 64], wd[:, j, n * 512:(n + 1) * 512],
                                     start=fh == 0 and j == 0, stop=fh == 1 and j == 3)
                            if fh == 1 and j == 3 and n == 1:
                                ins.then_inc(dl_done, 1)
                        if fh == 0 and j == 1:
                            pe.wait_ge(act_c_ready, e + 1)
                            for jc in range(4):
                                ins = turn(ctx_ps[:, tile(jc)], act_c[:, tile(jc)], ident[:, :])
                            ins.then_inc(aTp_c, 1)
                    if fh == 0:
                        pe.wait_ge(aTc_ready, e + 1)
                        if add:
                            pe.wait_ge(sc_added, base + 9)
                    for j in range(4):
                        for n in range(2):
                            r = 64 * (n ^ q) + 32 * (j % 2)
                            ins = mm(y_ps[1][r:r + 32, :], aTc[:, j, 32 * fh:32 * fh + 32],
                                     wd[:, j, n * 512:(n + 1) * 512], start=fh == 0 and j < 2, stop=fh == 1 and j >= 2)
                    ins.then_inc(d_used, 1)

            pair_of = [0]
            pe.wait_ge(xT_zero, 1)
            turn_tokens(0, 0)
            expert(0, 0)
            expert(1, 1)
            with pe.Fori(0, 3) as i:
                for j in range(2, 6):
                    pair_of[0] = 2 * i + j // 2
                    expert(4 * i + j, j)
            expert(14, 14)
            expert(15, 15)
            pe.wait_ge(ylo_ready, E)
            pe.wait_ge(y_read, 4 * E)
            for n in range(SC):
                scatter(SC * (E // 2 - 1), n)


_INS = ["x_prompt", "x_sample", "state_gla_fwd", "state_gla_bwd", "c", "c_ctx", "w_mod", "b_mod", "g_norm1", "g_norm2",
        "w_in", "w_conv", "b_conv", "w_a_up_f", "b_a_f", "w_a_up_b", "b_a_b", "g_gla_norm", "w_out", "w_router",
        "w_gate", "w_up", "w_down", "g_final"]
_OUTS = [(1, T_CTX, D), (1, T_LAT, D), (1, 1, H, DK, DV), (1, 1, H, DK, DV)]


def kernel(**inputs):
    import numpy as np
    import concourse.bacc as bacc
    from concourse.bass_utils import run_bass_kernel_spmd

    nc = bacc.Bacc("TRN2", target_bir_lowering=False, num_devices=1)
    arrays, args = {}, []
    for name in _INS:
        a = np.ascontiguousarray(inputs[name])
        arrays[f"in_{name}"] = a
        args.append(nc.dram_tensor(f"in_{name}", a.shape, mybir.dt.from_np(a.dtype), kind="ExternalInput").ap())
    for i, shape in enumerate(_OUTS):
        args.append(nc.dram_tensor(f"out_{i}", shape, F32, kind="ExternalOutput").ap())
    build(nc, *args)
    r = run_bass_kernel_spmd(nc, [arrays], core_ids=[0])
    return tuple(r.results[0][f"out_{i}"] for i in range(len(_OUTS)))
```

```python
from contextlib import ExitStack

import concourse.bass as bass
from concourse import mybir

F32 = mybir.dt.float32
F32R = mybir.dt.float32r
U32 = mybir.dt.uint32
I32 = mybir.dt.int32
ALU = mybir.AluOpType
ACT = mybir.ActivationFunctionType
AX = mybir.AxisListType

P = 128
D = 1024
KC = D // P
T_LAT, T_CTX = 512, 128
T = T_LAT + T_CTX
NT = T // P
HALF = T // 2
GRID_W = 64
CH = D // 2 // P
H, DK, DV = 4, 64, 128
C = 64
NCH, NCH_LAT = T // C, T_LAT // C
LR = 16
TAU = 16.0
E = 16
CAP_L, CAP_C = 2 * T_LAT // E, 2 * T_CTX // E
SLOTS = CAP_L + CAP_C
NMOD = 6
EPS = 1e-6
P_TOT = 3 * 512 + 2 * H * DK + 2 * H * DV + 2 * LR

R_BMOD, R_G1, R_G2, R_C, R_CONV, R_BCONV, R_GLA, R_BA = 0, 48, 56, 64, 80, 92, 96, 100
R_ALL = 104

WORK = 16512
RING_SLOTS = 8
SLOT = 4 * D * 4
RING = 229368 // 32 * 32 - RING_SLOTS * SLOT
A_X = WORK
A_CONST = A_X + 20480
A_G2B = A_CONST + 3680
A_GFIN = A_G2B + 8192
A_P2 = A_GFIN + 4096
R_HT = RING
R_HLO = R_HT + 20480
R_U = R_HLO + 20480
R_QD = R_U + 10240
R_KD = R_QD + 10240
R_KST = R_KD + 10240
R_V = RING + 7 * SLOT
R_FIN = R_V + 10240
R_ALOW = R_FIN + 2048
P1_SLOTS = (5, 6, 0, 3)
W_YT = A_P2
W_KS = W_YT + 10240
W_HI = W_YT + 20480
W_XR = W_HI + 16384
B_XS = A_P2
B_XT = B_XS + 8192
B_G = B_XT + 6144
B_GC = B_G + 2048
B_AT = B_GC + 2048
B_ATC = B_AT + 2048
B_Y = B_ATC + 1024
B_YH = B_Y + 8192
B_OH = B_YH + 8192
B_IOTA = B_OH + 5120
assert B_IOTA + 2048 <= RING and W_XR + 8192 <= RING


def first_phase_jobs():
    jobs = ["prm", "mod0", "mod1", "modT0"] + [f"xT{t}" for t in range(NT)]
    jobs += ["mod2", "modT1", "modT2", "mod3", "modT3"]
    jobs += ["q0", "q1", "alow", "k0", "k1", "la0", "la1"]
    jobs += ["v0", "v1", "v2", "mod4", "v3", "v4", "ks0", "ks1", "modT4", "la2"]
    jobs += ["xc0", "xc1", "mod5", "xc2", "modT5", "xc3", "ks2"]
    jobs += ["xv0", "la3", "xv1", "mod6", "xv2", "modT6", "xv3", "ks3"]
    jobs += ["xb0", "xb1", "mod7", "xb2", "modT7", "xb3"]
    jobs += ["og0", "og1", "mod8", "og2", "modT8", "og3"]
    jobs += [f"kv{n}" for n in KV_ORDER]
    jobs += ["g1_0", "g1_1", "att0", "att1", "mod9", "modT9"]
    jobs += ["o0", "att2", "o1", "att3", "oT0", "o2", "att4", "oT1", "o3", "oT2", "o4", "oT3", "oT4"]
    jobs += ["wo0", "wo1", "x2T0", "wo2", "lg0", "x2T1", "mod10", "wo3", "lg1", "modT10", "x2T2", "wo4", "x2T3", "lg2",
             "mod11", "x2T4", "lg3", "lg4", "modT11", "pT", "g2_0", "g2_1", "ixT", "pcT"]
    return jobs


KV_ORDER = [0, 7, 1, 6, 2, 5, 3, 4, 8, 9]
JOBS = first_phase_jobs()
UNITS = ["mod0", "mod1", "mod2", "mod3", "qk", "v", "mod4", "xc", "mod5", "xv", "mod6", "xb", "mod7", "og", "mod8", "wo0",
         "mod9", "wo1", "mod10", "mod11"]
PLACES = [0, 1, 0, 1, 0, 1, 0, 0, 1, 1, 0, 0, 1, 1, 0, 0, 1, 1, 2, 3]
IN_COLS = {"xb": 0, "xc": 512, "xv": 1024, "qk": 1536, "v": 2048, "og": 2560}


CHUNK_UNITS = ["qk", "v", "xc", "xv", "xb", "og"]
SPLITS = [(name, j) for name in CHUNK_UNITS + ["wo0", "wo1"] for j in range(4)]
CHUNK_JOBS = {"qk": ("q0", "q1", "k0", "k1"), "v": ("v4",) * 4,
              **{name: tuple(f"{name}{j}" for j in range(4)) for name in ("xc", "xv", "xb", "og")}}


def unit_place(name):
    n = UNITS.index(name)
    return PLACES[n], PLACES[:n].count(PLACES[n])


def last_job(unit):
    return CHUNK_JOBS[unit][3] if unit in CHUNK_JOBS else "wo4" if unit[:2] == "wo" else unit


def job(name):
    return JOBS.index(name)


def build(nc, x_prompt, x_sample, s_fwd, s_bwd, c, c_ctx, w_mod, b_mod, g_norm1, g_norm2, w_in, w_conv, b_conv,
          w_a_up_f, b_a_f, w_a_up_b, b_a_b, g_gla_norm, w_out, w_router, w_gate, w_up, w_down, g_final,
          y_prompt, y_sample, new_f, new_b):
    ctx = ExitStack()
    with ctx:
        def at(name, offset, shape, dt=F32):
            return nc.alloc_sbuf_tensor_at(name, shape, dt, offset=offset)

        def sem(name):
            return ctx.enter_context(nc.semaphore(name))

        const_next = [A_CONST]

        def small(name, shape, dt=F32):
            n = 4
            for s in shape[1:]:
                n *= s
            t = at(name, const_next[0], shape, dt)
            const_next[0] += (n + 31) // 32 * 32
            assert const_next[0] <= A_G2B
            return t

        x_sb = at("x_sb", A_X, [P, NT, D])
        ident = small("ident", [P, P])
        param = small("param", [P, R_ALL])
        mod = small("mod", [P, NMOD * KC, 2])
        scale1 = small("scale1", [P, KC, 2])
        scale2 = small("scale2", [P, KC, 2])
        eps_col = small("eps_col", [P, 1])
        one_col = small("one_col", [P, 1])
        rms = small("rms", [P, 6, NT])
        hrms = small("hrms", [P, 6, H])
        dec = small("dec", [P, H, NCH])
        smax = small("smax", [P, 3, NT])
        gather_idx = small("gather_idx", [P, E], U32)
        pair_cols = small("pair_cols", [P, 8, E // 2])
        logits = small("logits", [P, NT, E])
        w_router_sb = small("w_router_sb", [P, KC, E])

        gate2b = at("gate2b", A_G2B, [P, 2, D])
        gfin = at("gfin", A_GFIN, [P, D])

        hT = at("hT", R_HLO, [P, KC, T])
        hT_lo = at("hT_lo", R_HLO, [P, KC, T], F32R)
        hT_hi = at("hT_hi", R_HT, [P, KC, T], F32R)
        states = at("states", R_HT, [P, NCH, H, DV])
        u_sb = at("u_sb", R_U, [P, CH, T])
        og_sb = at("og_sb", R_U, [P, H, T])
        qd = at("qd", R_QD, [P, H, T])
        kd = at("kd", R_KD, [P, H, T])
        ksT = at("ksT", R_KST, [P, NT, H, P])
        v_sb = at("v_sb", R_V, [P, NT, H * DV])
        att_sb = [at("att_sb0", R_HLO + 16384, [P, 2, H, P]), at("att_sb1", R_ALOW, [P, 2, H, P])]
        w_hi = at("w_hi", W_HI, [P, KC, 512], F32R)
        wo_hi = [at("wo_hi0", R_HLO, [P, KC, 512], F32R), at("wo_hi1", W_HI, [P, KC, 512], F32R)]
        final_state = at("final_state", R_FIN, [P, H, DV])
        p1w = [at(f"p1w{i}", RING + slot * SLOT, [P, KC, 512]) for i, slot in enumerate(P1_SLOTS)]
        w_lo = [at(f"w_lo{i}", RING + P1_SLOTS[i] * SLOT, [P, KC, 512], F32R) for i in range(2)]
        xn = at("xn", R_QD, [P, NT, D])
        yT = at("yT", W_YT, [P, KC, T])
        yT_lo = at("yT_lo", W_YT, [P, KC, T], F32R)
        yT_hi = at("yT_hi", R_V, [P, 2, KC, P], F32R)
        ks_row = at("ks_row", W_KS, [P, 2, T])
        scan_mask = at("scan_mask", W_KS + 5120, [P, T])
        work_d = at("work_d", W_KS + 7680, [P, T])
        gate1b = at("gate1b", R_KST, [P, 2, D])
        a_lowT = at("a_lowT", R_ALOW, [P, T])
        xr = at("xr", W_XR, [P, 2, D])
        work_a = at("work_a", W_XR, [P, T])
        work_b = at("work_b", W_XR + 2560, [P, T])
        norm_r = at("norm_r", W_XR, [P, H * P])
        norm_sq = at("norm_sq", W_XR + 2048, [P, H * P])
        w_decay = at("w_decay", A_G2B, [P, H, P])
        mod_rows = at("mod_rows", A_G2B + 2048, [P, 2, 512])
        silu_c = at("silu_c", A_G2B + 6144, [P, KC, 32])
        keep_f = at("keep_f", A_G2B + 7168, [P, P])
        keep_b = at("keep_b", A_G2B + 7680, [P, P])
        w_tail = at("w_tail", A_GFIN, [P, KC, 2 * LR])
        param_rows = at("param_rows", A_GFIN + 1024, [R_ALL, P])
        h2T = [at("h2T_0", A_GFIN, [P, KC, P]), at("h2T_1", RING + 4 * SLOT, [P, KC, P])]

        ring = [at(f"ring{i}", RING + i * SLOT, [P, 4, D]) for i in range(RING_SLOTS)]
        xs = at("xs", B_XS, [SLOTS, 2, D])
        xT = at("xT", B_XT, [P, 2, KC, 96])
        act_l = at("act_l", B_G, [P, 512])
        act_c = at("act_c", B_GC, [P, 512])
        aT = at("aT", B_AT, [P, 4, P])
        aTc = at("aTc", B_ATC, [P, 4, 64])
        y_f = at("y_f", B_Y, [P, 2, 2, 512])
        y_lo = at("y_lo", B_Y, [P, 2, 2, 512], F32R)
        y_hi = at("y_hi", B_YH, [P, 2, 2, 512], F32R)
        oh_l = at("oh_l", B_OH, [P, 2, 512], F32R)
        oh_c = at("oh_c", B_OH + 4096, [P, 2, P], F32R)
        iota_f = at("iota_f", B_IOTA, [P, 512])
        RTK = RING + 7 * SLOT
        probs = at("probs", RTK, [P, NT, E])
        probsT = at("probsT", RTK + 512, [E, T])
        topv_l = at("topv_l", RTK + 3072, [E, P])
        topv_c = at("topv_c", RTK + 3584, [E, P])
        topi_l = at("topi_l", RTK + 4096, [E, P], U32)
        topi_c = at("topi_c", RTK + 4608, [E, P], U32)
        selr = at("selr", RTK + 5120, [E, 5, P])

        hn = nc.dram_tensor("hn", [T, D], F32, kind="Internal").ap()

        square_out = at("square_out", RING, [P, 2, D])

        pairs = [ctx.enter_context(nc.psum_tensor(f"pair{i}", [P, 2 * 512], F32)) for i in range(4)]

        names = """job_done prm_in tail_in st_in const_ready mask_ready param_ready silu_ready o_sum o_mean o_root
            silu_zero decay_zero modrow_ready mod_sum mod_ready scale_ready ss_ready mean_ready root_ready
            xr_ready hT_low hT_high raw_even raw_odd hT_hi_ready hT_ready whi_ready wlo_ready yThi_ready
            yTlo_ready alow_ready qk_first qk_second abs_ready min_ready softplus_ready cum_ready exp_b_ready
            exp_mb_ready dec_ready diff_ready exp_d_ready ks_ready ksT_ready v_sb_ready xc_ready u_ready
            conv_mid conv_ready ya_ready og_act og_ready kv_ready state_step att_ready o_sq o_norm yb_ready
            g1_ready g2_ready wo_half wo_read x2_ready h2_low h2_high lg_ready exp_ready smax_ready probs_ready
            probsT_ready selr_ready idx_ready state_out fin_state dve_chain act_chain pool_chain gu_used dl_done
            d_used xTp_done xT_lat xT_ctx xT_zero gul_done silu_lat silu_ctx act_l_ready act_c_ready aTp_l aTp_c
            aT_ready aTc_ready y_read yhi_ready ylo_ready oh_ready sc_done sc_added fss_ready fmean_ready
            froot_ready gfin_in fin_ready fin_out iota_ready""".split()
        (job_done, prm_in, tail_in, st_in, const_ready, mask_ready, param_ready, silu_ready, o_sum, o_mean,
         o_root, silu_zero, decay_zero, modrow_ready, mod_sum, mod_ready, scale_ready, ss_ready, mean_ready,
         root_ready, xr_ready, hT_low, hT_high, raw_even, raw_odd, hT_hi_ready, hT_ready, whi_ready, wlo_ready,
         yThi_ready, yTlo_ready, alow_ready, qk_first, qk_second, abs_ready, min_ready, softplus_ready,
         cum_ready, exp_b_ready, exp_mb_ready, dec_ready, diff_ready, exp_d_ready, ks_ready, ksT_ready,
         v_sb_ready, xc_ready, u_ready, conv_mid, conv_ready, ya_ready, og_act, og_ready, kv_ready, state_step,
         att_ready, o_sq, o_norm, yb_ready, g1_ready, g2_ready, wo_half, wo_read, x2_ready, h2_low, h2_high,
         lg_ready, exp_ready, smax_ready, probs_ready, probsT_ready, selr_ready, idx_ready, state_out, fin_state,
         dve_chain, act_chain, pool_chain, gu_used, dl_done, d_used, xTp_done, xT_lat, xT_ctx, xT_zero, gul_done,
         silu_lat, silu_ctx, act_l_ready, act_c_ready, aTp_l, aTp_c, aT_ready, aTc_ready, y_read, yhi_ready,
         ylo_ready, oh_ready, sc_done, sc_added, fss_ready, fmean_ready, froot_ready, gfin_in, fin_ready,
         fin_out, iota_ready) = [sem(n) for n in names]
        x_in = [sem(f"x_in{t}") for t in range(NT)]
        p1_full = [sem(f"p1_full{i}") for i in range(4)]
        w_full = [sem(f"w_full{i}") for i in range(RING_SLOTS)]
        xs_full = [sem(f"xs_full{i}") for i in range(2)]
        hn_out = [sem(f"hn_out{i}") for i in range(2)]

        read_by = {"prm": [(param_ready, 1)], "alow": [(alow_ready, 1)], "pT": [(probsT_ready, 1)]}
        for u in range(12):
            read_by[f"mod{u}"] = [(modrow_ready, u + 1)]
            read_by[f"modT{u}"] = [(mod_sum, u + 1)]
        for t in range(NT):
            read_by[f"xT{t}"] = [(hT_low, t + 1), (hT_high, t + 1)]
            read_by[f"v{t}"] = [(v_sb_ready, t + 1)]
            read_by[f"att{t}"] = [(att_ready, 2 * (t + 1))]
            read_by[f"o{t}"] = [(o_sq, t + 1), (o_norm, t + 1)]
            read_by[f"oT{t}"] = [(yb_ready, t + 1)]
            read_by[f"wo{t}"] = [(wo_read, 2 * t + 2)]
            read_by[f"x2T{t}"] = [(h2_low, t + 1), (h2_high, t + 1)]
            read_by[f"lg{t}"] = [(lg_ready, t + 1)]
        for i, n in enumerate(("q0", "q1", "k0", "k1")):
            read_by[n] = [(qk_first, i + 1), (qk_second, i + 1)]
        for h in range(H):
            read_by[f"la{h}"] = [(abs_ready, h + 1), (min_ready, h + 1)]
            read_by[f"ks{h}"] = [(ksT_ready, h + 1)]
            read_by[f"og{h}"] = [(og_act, h + 1)]
        for j in range(CH):
            read_by[f"xc{j}"] = [(xc_ready, j + 1)]
            read_by[f"xv{j}"] = [(u_ready, j + 1)]
            read_by[f"xb{j}"] = [(ya_ready, j + 1)]
        for i, n in enumerate(KV_ORDER):
            read_by[f"kv{n}"] = [(kv_ready, i + 1)]
        for v in range(2):
            read_by[f"g1_{v}"] = [(g1_ready, v + 1)]
            read_by[f"g2_{v}"] = [(g2_ready, v + 1)]

        def vec(t):
            return 0 if t < NT - 1 else 1

        def rounded(unit):
            return wo_hi[int(unit[2])] if unit[:2] == "wo" else w_hi

        def tile(t):
            return slice(t * P, (t + 1) * P)

        def claim(pe, name):
            n = job(name)
            if n >= 4:
                for signal, value in read_by[JOBS[n - 4]]:
                    pe.wait_ge(signal, value)
            return pairs[n % 4]

        def result(eng, name):
            eng.wait_ge(job_done, job(name) + 1)
            return pairs[job(name) % 4]

        def halves(ap):
            return ap.rearrange("p (s n) -> p s n", s=2)[:, :, 0:HALF]

        def split(ap):
            return ap.rearrange("p (s n) -> p s n", s=2)

        def body_loop(eng, expert):
            expert(0, 0)
            expert(1, 1)
            with eng.Fori(0, 3) as i:
                for j in range(2, 6):
                    expert(4 * i + j, j)
            expert(14, 14)
            expert(15, 15)

        gate_ps, up_ps = pairs[0][:, 0:512], pairs[0][:, 512:1024]
        ctx_ps, sc_ps = pairs[1][:, 0:512], pairs[1][:, 512:1024]
        y_ps = [pairs[3][:, 0:512], pairs[3][:, 512:1024]]
        sc_banks = [sc_ps, y_ps[0], y_ps[1]]
        SC = 2 * NT

        def xT_ps(kk):
            o = kk // 4 * 512 + kk % 4 * SLOTS
            return pairs[2][:, o:o + SLOTS]

        FINAL_GROUPS = ((0, 3), (3, NT))
        LAST_OF_GROUP = [hi - 1 for _, hi in FINAL_GROUPS]

        block = ctx.enter_context(nc.Block())

        @block.sync
        def _(sp):

            def load_unit(n):
                name = UNITS[n]
                place, turns = unit_place(name)
                if turns:
                    last = max(i for i in range(n) if PLACES[i] == place)
                    sp.wait_ge(job_done, job(last_job(UNITS[last])) + 1)
                if name.startswith("mod"):
                    src = w_mod[0, :, 512 * int(name[3:]):512 * (int(name[3:]) + 1)]
                elif name.startswith("wo"):
                    src = w_out[0, :, 512 * int(name[2:]):512 * (int(name[2:]) + 1)]
                else:
                    src = w_in[0, :, IN_COLS[name]:IN_COLS[name] + 512]
                sp.dma_start(p1w[place][:, :, :], src.rearrange("(k p) n -> p k n", p=P)).then_inc(p1_full[place], 16)

            sp.dma_start(param_rows[R_C:R_C + KC, :], c[0].rearrange("(r p) -> r p", p=P)).then_inc(prm_in, 16)
            sp.dma_start(param_rows[R_C + KC:R_C + 2 * KC, :], c_ctx.rearrange("(r p) -> r p", p=P)).then_inc(prm_in, 16)
            sp.dma_start(param_rows[R_GLA:R_GLA + H, :], g_gla_norm[0]).then_inc(prm_in, 16)
            sp.dma_start(param_rows[R_BA:R_BA + H, 0:DK], b_a_f[0].rearrange("(h d) -> h d", d=DK)).then_inc(prm_in, 16)
            sp.dma_start(param_rows[R_BA:R_BA + H, DK:P], b_a_b[0].rearrange("(h d) -> h d", d=DK)).then_inc(prm_in, 16)
            load_unit(0)
            for t in range(NT):
                src = x_sample[0, tile(t), :] if t < NT - 1 else x_prompt[0]
                sp.dma_start(x_sb[:, t, :], src).then_inc(x_in[t], 16)
            for n in range(1, 4):
                load_unit(n)
            sp.dma_start(w_tail[:, :, :], w_in[0, :, P_TOT - 2 * LR:].rearrange("(k p) n -> p k n", p=P)
                         ).then_inc(tail_in, 16)
            load_unit(4)
            sp.wait_ge(decay_zero, 1)
            for r in range(0, P, 2 * LR):
                sp.dma_start(w_decay[r:r + LR, :, 0:DK], w_a_up_f[0].rearrange("r (h d) -> r h d", d=DK)
                             ).then_inc(tail_in, 16)
                sp.dma_start(w_decay[r + LR:r + 2 * LR, :, DK:P], w_a_up_b[0].rearrange("r (h d) -> r h d", d=DK)
                             ).then_inc(tail_in, 16)
            sp.dma_start(w_router_sb[:, :, :], w_router[0].rearrange("(k p) n -> p k n", p=P)).then_inc(tail_in, 16)
            for n in range(5, UNITS.index("wo0")):
                load_unit(n)
            sp.wait_ge(job_done, job("og3") + 1)
            sp.dma_start(states[0:DK, 0, :, :], s_fwd[0, 0].rearrange("h d v -> d h v")).then_inc(st_in, 16)
            sp.dma_start(states[DK:P, NCH_LAT - 1, :, :], s_bwd[0, 0].rearrange("h d v -> d h v")).then_inc(st_in, 16)
            for n in range(UNITS.index("wo0"), len(UNITS) - 2):
                load_unit(n)
            sp.wait_ge(fin_state, 1)
            sp.dma_start(new_f[0, 0].rearrange("h d v -> d h v"), final_state[0:DK, :, :]).then_inc(state_out, 16)
            sp.dma_start(new_b[0, 0].rearrange("h d v -> d h v"), final_state[DK:P, :, :]).then_inc(state_out, 16)

            def load_expert(e, k):
                for u in range(6):
                    half = u // 2 if u < 4 else u - 4
                    w = (w_gate, w_up)[u % 2] if u < 4 else w_down
                    n = 6 * k + u
                    if n >= RING_SLOTS:
                        if u < 2:
                            sp.wait_ge(d_used, 2 * e - 3 + u)
                        else:
                            sp.wait_ge(gu_used, 2 * e - 1 + (u - 2) // 2)
                    elif n == 0:
                        sp.wait_ge(yb_ready, NT)
                        load_unit(len(UNITS) - 2)
                        load_unit(len(UNITS) - 1)
                        sp.wait_ge(job_done, job("mod10") + 1)
                    elif n == 1:
                        sp.wait_ge(job_done, job("wo4") + 1)
                    elif n == P1_SLOTS[3]:
                        sp.wait_ge(job_done, job("mod11") + 1)
                    elif n == 4:
                        sp.wait_ge(job_done, job("lg3") + 1)
                    elif n == 6:
                        sp.wait_ge(xs_full[0], 16)
                    elif n == 7:
                        sp.wait_ge(state_out, 32)
                        sp.wait_ge(idx_ready, 2)
                    rows = slice(half * 512, (half + 1) * 512)
                    src = w[0, e, rows, :] if isinstance(e, int) else \
                        w[0, bass.ds(e, 1), rows, :].rearrange("o r n -> (o r) n")
                    sp.dma_start(ring[n % RING_SLOTS][:, :, :], src.rearrange("(k p) n -> p k n", p=P)
                                 ).then_inc(w_full[n % RING_SLOTS], 16)

            body_loop(sp, load_expert)
            sp.dma_start(gfin[:, :], g_final.partition_broadcast(P)).then_inc(gfin_in, 16)
            sp.wait_ge(fin_out, 16 * NT)

        @block.gpsimd
        def _(pool):
            g = nc.gpsimd
            steps = [0]

            def link(ins):
                steps[0] += 1
                ins.then_inc(pool_chain, 1)
                pool.wait_ge(pool_chain, steps[0])

            g.memset(silu_c[:, :, :], 0.0).then_inc(silu_zero, 1)
            g.memset(eps_col[:, :], EPS)
            g.memset(one_col[:, :], 1.0)
            link(g.memset(ident[:, :], 0.0))
            g.affine_select(out=ident[:, :], in_=ident[:, :], compare_op=ALU.not_equal, fill=1.0, base=0,
                            pattern=[[-1, P]], channel_multiplier=1).then_inc(const_ready, 1)
            g.memset(w_decay[:, :, :], 0.0).then_inc(decay_zero, 1)
            link(g.memset(scan_mask[:, :], 1.0))
            g.memset(scan_mask[0:DK, 0:T:C], 0.0).then_inc(mask_ready, 1)
            g.memset(scan_mask[DK:P, C - 1:T:C], 0.0).then_inc(mask_ready, 1)
            pool.wait_ge(mask_ready, 2)
            link(g.memset(keep_f[:, :], 1.0))
            link(g.affine_select(out=keep_f[:, :], in_=keep_f[:, :], compare_op=ALU.is_ge, fill=0.0, base=0,
                                 pattern=[[1, P]], channel_multiplier=-1))
            g.memset(keep_f[0:C, C:P], 0.0).then_inc(mask_ready, 1)
            pool.wait_ge(mask_ready, 3)
            link(g.memset(keep_b[:, :], 1.0))
            link(g.affine_select(out=keep_b[:, :], in_=keep_b[:, :], compare_op=ALU.is_ge, fill=0.0, base=0,
                                 pattern=[[-1, P]], channel_multiplier=1))
            g.memset(keep_b[C:P, 0:C], 0.0).then_inc(mask_ready, 1)
            pool.wait_ge(mask_ready, 4)
            pool.wait_ge(job_done, job("og3") + 1)
            for b in range(2):
                g.memset(att_sb[b][:, :, :, :], 0.0).then_inc(mask_ready, 1)

            pool.wait_ge(mask_ready, 6)
            pool.wait_ge(idx_ready, 1)
            pool.wait_ge(hn_out[0], 48)
            pool.wait_ge(hn_out[1], 32)
            for e in range(E):
                if e >= 2:
                    pool.wait_ge(xTp_done, e - 1)
                g.indirect_dma_start(xs[:, e % 2, :], None, hn[:, :],
                                     bass.IndirectOffsetOnAxis(ap=gather_idx[0:SLOTS, e:e + 1], axis=0)
                                     ).then_inc(xs_full[e % 2], 16)
                if e == 1:
                    g.iota(iota_f[:, :], pattern=[[1, 512]], base=0, channel_multiplier=0,
                           allow_small_or_imprecise_dtypes=True).then_inc(iota_ready, 1)

        @block.scalar
        def _(act):
            a = nc.scalar
            steps = [0]

            def link(ins):
                steps[0] += 1
                ins.then_inc(act_chain, 1)
                act.wait_ge(act_chain, steps[0])

            for r0, src in (
                (R_BMOD, b_mod[0].rearrange("(r p) -> r p", p=P)),
                (R_G1, g_norm1[0].rearrange("(r p) -> r p", p=P)),
                (R_G2, g_norm2[0].rearrange("(r p) -> r p", p=P)),
                (R_CONV, w_conv[0].rearrange("w (r p) -> (w r) p", p=P)),
                (R_BCONV, b_conv[0].rearrange("(r p) -> r p", p=P)),
            ):
                act.dma_start(param_rows[r0:r0 + src.shape[0], :], src).then_inc(prm_in, 16)
            act.wait_ge(param_ready, 1)
            act.wait_ge(silu_zero, 1)
            a.activation(silu_c[:, :, 0:2].rearrange("p k v -> p v k"),
                         param[:, R_C:R_C + 2 * KC].rearrange("p (v k) -> p v k", v=2), ACT.Silu
                         ).then_inc(silu_ready, 1)

            def mod_row(u):
                pp = result(act, f"mod{u}")
                if u >= 2:
                    act.wait_ge(job_done, job(f"modT{u - 2}") + 1)
                a.activation(mod_rows[:, u % 2, :], pp[:, 0:512], ACT.Copy).then_inc(modrow_ready, 1)

            def square_sum(t):
                a.activation(xr[:, t % 2, :], x_sb[:, t, :], ACT.Square, accum_out=rms[:, 0, t:t + 1]
                             ).then_inc(ss_ready, 1)

            mod_row(0)
            for t in range(NT):
                act.wait_ge(x_in[t], 16)
                if t >= 2:
                    act.wait_ge(ss_ready, t - 1)
                square_sum(t)
            act.wait_ge(mean_ready, 1)
            a.activation(rms[:, 2, :], rms[:, 1, :], ACT.Sqrt).then_inc(root_ready, 1)
            mod_row(1)
            for t in range(NT):
                pp = result(act, f"xT{t}")
                a.activation(hT[:, 0:KC // 2, tile(t)], pp[:, 0:512].rearrange("p (k n) -> p k n", n=P), ACT.Copy
                             ).then_inc(hT_low, 1)
            mod_row(2)
            mod_row(3)

            def split_hi(name, j):
                place, turns = unit_place(name)
                act.wait_ge(p1_full[place], 16 * (turns + 1))
                if name[:2] == "wo":
                    act.wait_ge(job_done, job("og3") + 1)
                elif name != "qk":
                    act.wait_ge(job_done, job(CHUNK_JOBS[CHUNK_UNITS[CHUNK_UNITS.index(name) - 1]][j]) + 1)
                a.activation(rounded(name)[:, :, tile(j)], p1w[place][:, :, tile(j)], ACT.Copy).then_inc(whi_ready, 1)

            act.wait_ge(scale_ready, 1)
            act.wait_ge(hT_low, NT)
            act.wait_ge(hT_high, NT)

            def modulated(k):
                for v, cols in enumerate((slice(0, T_LAT), slice(T_LAT, T))):
                    ins = a.activation(hT[:, k, cols], hT[:, k, cols], ACT.Identity, bias=mod[:, k, v:v + 1],
                                       scale=scale1[:, k, v:v + 1])
                ins.then_inc(raw_odd, 1)

            def tokens_hi(k):
                act.wait_ge(raw_odd if k % 2 else raw_even, k // 2 + 1)
                a.activation(hT_hi[:, k, :], hT[:, k, :], ACT.Copy).then_inc(hT_hi_ready, 1)

            for k in range(0, KC, 2):
                modulated(k + 1)
                tokens_hi(k)
                tokens_hi(k + 1)
                if k == 0:
                    split_hi("qk", 0)
            for j in range(1, 4):
                split_hi("qk", j)

            def q_k(name, dst):
                pp = result(act, name)
                for d in range(2):
                    ins = a.activation(split(dst[d * DK:(d + 1) * DK, 2 * int(name[1]), :]), halves(pp[0:DK, :]),
                                       ACT.Copy)
                ins.then_inc(qk_first, 1)

            def decay(h):
                pp = result(act, f"la{h}")
                if h:
                    act.wait_ge(ks_ready, h)
                a.activation(split(work_b[:, :]), halves(pp), ACT.Abs, bias=param[:, R_BA + h:R_BA + h + 1]
                             ).then_inc(abs_ready, 1)
                act.wait_ge(abs_ready, h + 1)
                link(a.activation(work_b[:, :], work_b[:, :], ACT.Exp, scale=-1.0))
                a.activation(work_b[:, :], work_b[:, :], ACT.Ln, bias=one_col[:, 0:1]).then_inc(softplus_ready, 1)
                act.wait_ge(cum_ready, 2 * (h + 1))
                a.activation(work_a[:, :], work_b[:, :], ACT.Exp, scale=1.0 / TAU).then_inc(exp_b_ready, 1)
                a.activation(work_d[:, :], work_b[:, :], ACT.Exp, scale=-1.0 / TAU).then_inc(exp_mb_ready, 1)
                a.activation(dec[0:DK, h, :], work_b[0:DK, C - 1:T:C], ACT.Exp, scale=1.0 / TAU)
                a.activation(dec[DK:P, h, :], work_b[DK:P, 0:T:C], ACT.Exp, scale=1.0 / TAU).then_inc(dec_ready, 1)
                act.wait_ge(diff_ready, h + 1)
                a.activation(work_a[:, :], work_a[:, :], ACT.Exp, scale=1.0 / TAU).then_inc(exp_d_ready, 1)

            def ks_turn(h):
                pp = result(act, f"ks{h}")
                a.activation(ksT[:, :, h, :], pp[:, 0:T].rearrange("p (t n) -> p t n", n=P), ACT.Copy
                             ).then_inc(ksT_ready, 1)

            def values(t):
                pp = result(act, f"v{t}")
                a.activation(v_sb[:, t, :], pp[:, 0:512], ACT.Copy).then_inc(v_sb_ready, 1)

            def conv_input(j):
                pp = result(act, f"xc{j}")
                a.activation(split(u_sb[:, j, :]), halves(pp), ACT.Copy).then_inc(xc_ready, 1)

            for j, (name, dst) in enumerate((("q0", qd), ("q1", qd), ("k0", kd), ("k1", kd))):
                q_k(name, dst)
                split_hi("v", j)
            decay(0)
            values(0)
            values(1)
            decay(1)
            values(2)
            mod_row(4)
            values(3)
            values(4)
            split_hi("xc", 0)
            split_hi("xc", 1)
            ks_turn(0)
            ks_turn(1)
            split_hi("xc", 2)
            split_hi("xc", 3)
            decay(2)
            conv_input(0)
            conv_input(1)
            mod_row(5)
            conv_input(2)
            split_hi("xv", 0)
            split_hi("xv", 1)
            conv_input(3)
            split_hi("xv", 2)
            split_hi("xv", 3)
            ks_turn(2)

            def centre_tap(j):
                act.wait_ge(u_ready, j + 1)
                a.activation(yT[:, j, :], u_sb[:, j, :], ACT.Identity,
                             scale=param[:, R_CONV + CH + j:R_CONV + CH + j + 1],
                             bias=param[:, R_BCONV + j:R_BCONV + j + 1]).then_inc(conv_mid, 1)

            decay(3)
            mod_row(6)
            centre_tap(0)
            centre_tap(1)
            centre_tap(2)
            split_hi("xb", 0)
            split_hi("xb", 1)
            split_hi("xb", 2)
            split_hi("xb", 3)
            centre_tap(3)
            ks_turn(3)
            mod_row(7)
            for j in range(H):
                split_hi("og", j)
            act.wait_ge(conv_ready, CH)
            for j in range(H):
                pp = result(act, f"og{j}")
                a.activation(split(og_sb[:, j, :]), halves(pp), ACT.Silu).then_inc(og_act, 1)
                if j == 1:
                    mod_row(8)

            def gate_row(name, v, dst, ready):
                pp = result(act, name)
                a.activation(dst[:, v, :], pp[:, :], ACT.Copy).then_inc(ready, 1)

            for n in KV_ORDER:
                pp = result(act, f"kv{n}")
                f_dst = final_state[0:DK] if n == NCH - 1 else None if n == NCH_LAT - 1 else states[0:DK, n + 1]
                b_dst = final_state[DK:P] if n == NCH_LAT else None if n == 0 else states[DK:P, n - 1]
                src = pp[:, 0:512].rearrange("p (h n) -> p h n", h=H)
                if f_dst is not None:
                    ins = a.activation(f_dst, src[0:DK], ACT.Copy)
                if b_dst is not None:
                    ins = a.activation(b_dst, src[DK:P], ACT.Copy)
                ins.then_inc(kv_ready, 1)

            gate_row("g1_0", 0, gate1b, g1_ready)
            gate_row("g1_1", 1, gate1b, g1_ready)
            mod_row(9)
            for j in range(4):
                split_hi("wo0", j)

            def o_square(t):
                pp = result(act, f"o{t}")
                if t:
                    act.wait_ge(o_sum, t)
                a.activation(norm_sq[:, :], pp[:, 0:512], ACT.Square).then_inc(o_sq, 1)
                act.wait_ge(o_mean, t + 1)
                a.activation(hrms[:, 2, :], hrms[:, 1, :], ACT.Sqrt).then_inc(o_root, 1)

            def mixed_hi(t):
                act.wait_ge(yb_ready, t + 1)
                act.wait_ge(ya_ready, CH)
                act.wait_ge(job_done, job("o4" if t < 2 else f"wo{t - 2}") + 1)
                a.activation(yT_hi[:, t % 2, :, :], yT[:, :, tile(t)], ACT.Copy).then_inc(yThi_ready, 1)

            for t in range(NT - 1):
                o_square(t)
                split_hi("wo1", t)
            mixed_hi(0)
            o_square(NT - 1)
            mixed_hi(1)

            def second_norm(t):
                act.wait_ge(x2_ready, 2 * t + 2)
                square_sum(t)
                act.wait_ge(mean_ready, t + 2)
                a.activation(rms[:, 2, t:t + 1], rms[:, 1, t:t + 1], ACT.Sqrt).then_inc(root_ready, 1)

            def store_rows(t):
                act.wait_ge(xr_ready, NT + t + 1)
                act.dma_start(hn[tile(t), :], xr[:, t % 2, :]).then_inc(hn_out[t % 2], 16)

            def h2_turn(t):
                pp = result(act, f"x2T{t}")
                if t >= 2:
                    act.wait_ge(job_done, job(f"lg{t - 2}") + 1)
                for k in range(KC // 2):
                    ins = a.activation(h2T[t % 2][:, k, :], pp[:, k * P:(k + 1) * P], ACT.Identity,
                                       bias=mod[:, 3 * KC + k, vec(t):vec(t) + 1],
                                       scale=scale2[:, k, vec(t):vec(t) + 1])
                ins.then_inc(h2_low, 1)

            act.wait_ge(scale_ready, 2)
            for t in range(NT - 1):
                if t >= 1:
                    h2_turn(t - 1)
                if t + 2 < NT:
                    mixed_hi(t + 2)
                second_norm(t)
                store_rows(t)
                if t == 2:
                    mod_row(10)
            second_norm(NT - 1)
            h2_turn(NT - 2)
            store_rows(NT - 1)
            mod_row(11)
            h2_turn(NT - 1)
            act.wait_ge(smax_ready, 1)
            a.activation(probs[:, :, :], probs[:, :, :], ACT.Exp).then_inc(exp_ready, 1)
            for v in range(2):
                gate_row(f"g2_{v}", v, gate2b, g2_ready)

            def tokens(e, k):
                act.wait_ge(xTp_done, e + 1)
                for kk in range(KC):
                    ins = a.activation(xT[:, k % 2, kk, 0:CAP_L], xT_ps(kk)[:, 0:CAP_L], ACT.Identity,
                                       bias=mod[:, 3 * KC + kk, 0:1], scale=scale2[:, kk, 0:1])
                ins.then_inc(xT_lat, 1)

            def expert(e, k):
                act.wait_ge(gul_done, e + 1)
                a.activation(act_l[:, :], gate_ps, ACT.Silu).then_inc(silu_lat, 1)
                act.wait_ge(gu_used, 2 * e + 2)
                a.activation(act_c[64:P, :], ctx_ps[0:64, :], ACT.Silu).then_inc(silu_ctx, 1)
                if k < E - 1:
                    tokens(e + 1, k + 1)
                if k % 2 == 1:
                    for kind in range(2):
                        act.wait_ge(y_read, 4 * e + 2 + 2 * kind)
                        a.activation(y_hi[:, kind, :, :], y_f[:, kind, :, :], ACT.Copy).then_inc(yhi_ready, 1)

            tokens(0, 0)
            body_loop(act, expert)

            for t in range(NT):
                act.wait_ge(sc_added, SC * (E // 2 - 1) + 2 * t + 2)
                if t >= 2:
                    act.wait_ge(fss_ready, t - 1)
                a.activation(square_out[:, t % 2, :], x_sb[:, t, :], ACT.Square, accum_out=rms[:, 0, t:t + 1]
                             ).then_inc(fss_ready, 1)
                if t in LAST_OF_GROUP:
                    cols = slice(*FINAL_GROUPS[LAST_OF_GROUP.index(t)])
                    act.wait_ge(fmean_ready, LAST_OF_GROUP.index(t) + 1)
                    a.activation(rms[:, 2, cols], rms[:, 1, cols], ACT.Sqrt).then_inc(froot_ready, 1)
            for t in range(NT):
                act.wait_ge(fin_ready, t + 1)
                dst = y_sample[0, tile(t), :] if t < NT - 1 else y_prompt[0]
                act.dma_start(dst, x_sb[:, t, :]).then_inc(fin_out, 16)

        @block.vector
        def _(dve):
            v = nc.vector
            steps = [0]

            def link(ins):
                steps[0] += 1
                ins.then_inc(dve_chain, 1)
                dve.wait_ge(dve_chain, steps[0])

            pp = result(dve, "prm")
            v.tensor_copy(param[:, :], pp[:, 0:R_ALL]).then_inc(param_ready, 1)

            def mean_square(cols, ready):
                v.tensor_scalar(rms[:, 1, cols], rms[:, 0, cols], 1.0 / D, EPS, ALU.mult, ALU.add).then_inc(ready, 1)

            def inverse_root(r, cols):
                link(v.reciprocal(r[:, 3, cols], r[:, 2, cols]))
                link(v.tensor_tensor(r[:, 4, cols], r[:, 3, cols], r[:, 3, cols], ALU.mult))
                link(v.tensor_tensor(r[:, 4, cols], r[:, 4, cols], r[:, 1, cols], ALU.mult))
                link(v.tensor_scalar(r[:, 4, cols], r[:, 4, cols], -0.5, 1.5, ALU.mult, ALU.add))
                link(v.tensor_tensor(r[:, 5, cols], r[:, 3, cols], r[:, 4, cols], ALU.mult))

            def normalise(t):
                v.tensor_scalar(xr[:, t % 2, :], x_sb[:, t, :], rms[:, 5, t:t + 1], None, ALU.mult
                                ).then_inc(xr_ready, 1)

            def modulation(u):
                pp = result(dve, f"modT{u}")
                src = pp[:, 0:512].rearrange("p (j g r) -> p j r g", j=4, g=4)[:, :, 0:2, :]
                cols = slice(4 * u, 4 * u + 4)
                v.tensor_reduce(mod[:, cols, :], src, AX.X, ALU.add).then_inc(mod_sum, 1)
                dve.wait_ge(mod_sum, u + 1)
                v.tensor_tensor(mod[:, cols, :], mod[:, cols, :],
                                param[:, R_BMOD + 4 * u:R_BMOD + 4 * u + 4].unsqueeze(2).to_broadcast([P, 4, 2]),
                                ALU.add).then_inc(mod_ready, 1)

            def scales(dst, chunk, g_row, u):
                dve.wait_ge(mod_ready, u)
                v.scalar_tensor_tensor(out=dst[:, :, :], in0=mod[:, chunk:chunk + KC, :], scalar=1.0,
                                       in1=param[:, g_row:g_row + KC].unsqueeze(2).to_broadcast([P, KC, 2]),
                                       op0=ALU.add, op1=ALU.mult).then_inc(scale_ready, 1)

            dve.wait_ge(ss_ready, NT)
            mean_square(slice(0, NT), mean_ready)
            dve.wait_ge(root_ready, 1)
            inverse_root(rms, slice(0, NT))
            for t in range(NT):
                v.tensor_scalar(xn[:, t, :], x_sb[:, t, :], rms[:, 5, t:t + 1], None, ALU.mult).then_inc(xr_ready, 1)
            dve.wait_ge(param_ready, 1)
            modulation(0)
            for t in range(NT):
                pp = result(dve, f"xT{t}")
                v.tensor_copy(hT[:, KC // 2:KC, tile(t)], pp[:, 512:1024].rearrange("p (k n) -> p k n", n=P)
                              ).then_inc(hT_high, 1)
            for u in range(1, 4):
                modulation(u)

            splits = [0]

            def split_lo(name, j):
                assert SPLITS[splits[0]] == (name, j)
                splits[0] += 1
                place = unit_place(name)[0]
                dve.wait_ge(whi_ready, splits[0])
                v.tensor_tensor(w_lo[place][:, :, tile(j)], p1w[place][:, :, tile(j)],
                                rounded(name)[:, :, tile(j)].bitcast(F32), ALU.subtract).then_inc(wlo_ready, 1)

            scales(scale1, KC, R_G1, 4)
            dve.wait_ge(scale_ready, 1)
            dve.wait_ge(hT_low, NT)
            dve.wait_ge(hT_high, NT)

            def modulated(k):
                for i, cols in enumerate((slice(0, T_LAT), slice(T_LAT, T))):
                    ins = v.tensor_scalar(hT[:, k, cols], hT[:, k, cols], scale1[:, k, i:i + 1], mod[:, k, i:i + 1],
                                          ALU.mult, ALU.add)
                ins.then_inc(raw_even, 1)

            def tokens_lo(k):
                dve.wait_ge(hT_hi_ready, k + 1)
                v.tensor_tensor(hT_lo[:, k, :], hT[:, k, :], hT_hi[:, k, :].bitcast(F32), ALU.subtract
                                ).then_inc(hT_ready, 1)

            modulated(0)
            for k in range(0, KC, 2):
                if k + 2 < KC:
                    modulated(k + 2)
                tokens_lo(k)
                tokens_lo(k + 1)
                if k == 0:
                    split_lo("qk", 0)
            for j in range(1, 4):
                split_lo("qk", j)

            def q_k(name, dst):
                pp = result(dve, name)
                for d in range(2):
                    ins = v.tensor_copy(split(dst[d * DK:(d + 1) * DK, 2 * int(name[1]) + 1, :]), halves(pp[DK:P, :]))
                ins.then_inc(qk_second, 1)

            def decay(h):
                pp = result(dve, f"la{h}")
                dve.wait_ge(abs_ready, h + 1)
                v.tensor_scalar(split(work_a[:, :]), halves(pp), param[:, R_BA + h:R_BA + h + 1], 0.0,
                                ALU.add, ALU.min).then_inc(min_ready, 1)
                dve.wait_ge(min_ready, h + 1)
                dve.wait_ge(softplus_ready, h + 1)
                link(v.tensor_tensor(work_a[:, :], work_a[:, :], work_b[:, :], ALU.subtract))
                v.tensor_tensor_scan(work_b[0:DK, :], scan_mask[0:DK, :], work_a[0:DK, :], 0.0,
                                     ALU.mult, ALU.add).then_inc(cum_ready, 1)
                v.tensor_tensor_scan(work_b[DK:P, ::-1], scan_mask[DK:P, ::-1], work_a[DK:P, ::-1], 0.0,
                                     ALU.mult, ALU.add).then_inc(cum_ready, 1)
                dve.wait_ge(exp_b_ready, h + 1)
                dve.wait_ge(qk_first, 4)
                dve.wait_ge(qk_second, 4)
                link(v.scalar_tensor_tensor(out=qd[:, h, :], in0=qd[:, h, :], scalar=float(DK) ** -0.5,
                                            in1=work_a[:, :], op0=ALU.mult, op1=ALU.mult))
                chunks = lambda ap: ap.rearrange("p (n c) -> p n c", c=C)
                v.tensor_tensor(chunks(work_a[0:DK, :]),
                                work_b[0:DK, C - 1:T:C].unsqueeze(2).to_broadcast([DK, NCH, C]),
                                chunks(work_b[0:DK, :]), ALU.subtract)
                v.tensor_tensor(chunks(work_a[DK:P, :]),
                                work_b[DK:P, 0:T:C].unsqueeze(2).to_broadcast([DK, NCH, C]),
                                chunks(work_b[DK:P, :]), ALU.subtract).then_inc(diff_ready, 1)
                if h >= 2:
                    dve.wait_ge(job_done, job(f"ks{h - 2}") + 1)
                dve.wait_ge(exp_d_ready, h + 1)
                v.tensor_tensor(ks_row[:, h % 2, :], kd[:, h, :], work_a[:, :], ALU.mult)
                dve.wait_ge(exp_mb_ready, h + 1)
                v.tensor_tensor(kd[:, h, :], kd[:, h, :], work_d[:, :], ALU.mult).then_inc(ks_ready, 1)

            q_k("q0", qd)
            split_lo("v", 0)
            q_k("q1", qd)
            split_lo("v", 1)
            pp = result(dve, "alow")
            v.tensor_copy(split(a_lowT[:, :]), halves(pp)).then_inc(alow_ready, 1)
            q_k("k0", kd)
            split_lo("v", 2)
            q_k("k1", kd)
            split_lo("v", 3)
            dve.wait_ge(mask_ready, 4)
            decay(0)
            decay(1)
            for j in range(3):
                split_lo("xc", j)
            modulation(4)
            split_lo("xc", 3)
            decay(2)
            split_lo("xv", 0)
            split_lo("xv", 1)
            modulation(5)
            split_lo("xv", 2)
            split_lo("xv", 3)

            def gated_input(j):
                pp = result(dve, f"xv{j}")
                dve.wait_ge(xc_ready, j + 1)
                v.tensor_tensor(split(u_sb[:, j, :]), split(u_sb[:, j, :]), halves(pp), ALU.mult
                                ).then_inc(u_ready, 1)

            def side_taps(j):
                dve.wait_ge(conv_mid, j + 1)
                w0 = param[:, R_CONV + j:R_CONV + j + 1]
                w2 = param[:, R_CONV + 2 * CH + j:R_CONV + 2 * CH + j + 1]
                for lo, hi, width in ((0, T_LAT, GRID_W), (T_LAT, T, T_CTX)):
                    y = yT[:, j, lo:hi].rearrange("p (r w) -> p r w", w=width)
                    x = u_sb[:, j, lo:hi].rearrange("p (r w) -> p r w", w=width)
                    link(v.scalar_tensor_tensor(out=y[:, :, 1:], in0=x[:, :, :width - 1], scalar=w0,
                                                in1=y[:, :, 1:], op0=ALU.mult, op1=ALU.add))
                    ins = v.scalar_tensor_tensor(out=y[:, :, :width - 1], in0=x[:, :, 1:], scalar=w2,
                                                 in1=y[:, :, :width - 1], op0=ALU.mult, op1=ALU.add)
                ins.then_inc(conv_ready, 1)

            gated_input(0)
            decay(3)
            gated_input(1)
            side_taps(0)
            gated_input(2)
            modulation(6)
            split_lo("xb", 0)
            split_lo("xb", 1)
            side_taps(1)
            gated_input(3)
            split_lo("xb", 2)
            split_lo("xb", 3)
            side_taps(2)
            side_taps(3)

            def gated_conv(j):
                pp = result(dve, f"xb{j}")
                dve.wait_ge(conv_ready, j + 1)
                v.tensor_tensor(split(yT[:, j, :]), split(yT[:, j, :]), halves(pp), ALU.mult).then_inc(ya_ready, 1)

            for j in range(3):
                gated_conv(j)
            modulation(7)
            split_lo("og", 0)
            split_lo("og", 1)
            gated_conv(3)
            split_lo("og", 2)
            split_lo("og", 3)
            for j in range(H):
                dve.wait_ge(og_act, j + 1)
                v.tensor_scalar(og_sb[:, j, :], og_sb[:, j, :], param[:, R_GLA + j:R_GLA + j + 1], None, ALU.mult
                                ).then_inc(og_ready, 1)
                if j == 2:
                    modulation(8)

            dve.wait_ge(job_done, job("og3") + 1)
            v.memset(states[0:DK, NCH_LAT, :, :], 0.0).then_inc(state_step, 1)
            v.memset(states[DK:P, NCH - 1, :, :], 0.0).then_inc(state_step, 1)

            def state(n, d):
                rows = slice(0, DK) if d == 0 else slice(DK, P)
                m = n + 1 if d == 0 else n - 1
                last = (n == NCH - 1 and d == 0) or (n == NCH_LAT and d == 1)
                dst = final_state[rows] if last else states[rows, m]
                for h in range(H):
                    ins = v.scalar_tensor_tensor(out=dst[:, h, :], in0=states[rows, n, h, :],
                                                 scalar=dec[rows, h, n:n + 1], in1=dst[:, h, :],
                                                 op0=ALU.mult, op1=ALU.add)
                return ins

            dve.wait_ge(st_in, 32)
            dve.wait_ge(dec_ready, H)
            for i in range(NCH_LAT - 1):
                for d in range(2):
                    n = i if d == 0 else NCH_LAT - 1 - i
                    dve.wait_ge(kv_ready, KV_ORDER.index(n) + 1)
                    if i:
                        dve.wait_ge(state_step, 2 * i + d + 1)
                    state(n, d).then_inc(state_step, 1)
            def att_mask(t):
                pp = result(dve, f"att{t}")
                if t >= 2:
                    dve.wait_ge(job_done, job(f"o{t - 2}") + 1)
                for d, keep in enumerate((keep_f, keep_b)):
                    v.copy_predicated(att_sb[t % 2][:, d, :, :],
                                      keep[:, :].bitcast(I32).unsqueeze(1).to_broadcast([P, H, P]),
                                      pp[:, d * 512:(d + 1) * 512].rearrange("p (h n) -> p h n", h=H)
                                      ).then_inc(att_ready, 1)

            dve.wait_ge(mask_ready, 6)
            att_mask(0)
            att_mask(1)
            STEPS = 2 * NCH_LAT
            dve.wait_ge(kv_ready, len(KV_ORDER))
            dve.wait_ge(state_step, 2)
            state(NCH_LAT, 0).then_inc(state_step, 1)
            state(NCH - 1, 1).then_inc(state_step, 1)
            dve.wait_ge(state_step, STEPS + 2)
            state(NCH - 1, 0)
            state(NCH_LAT, 1).then_inc(fin_state, 1)
            modulation(9)
            scales(scale2, 4 * KC, R_G2, 10)
            heads = lambda ap: ap.rearrange("p (h n) -> p h n", h=H)

            def head_norm(t):
                dve.wait_ge(o_sq, t + 1)
                v.tensor_reduce(hrms[:, 0, :], heads(norm_sq[:, :]), AX.X, ALU.add).then_inc(o_sum, 1)
                dve.wait_ge(o_sum, t + 1)
                v.tensor_scalar(hrms[:, 1, :], hrms[:, 0, :], 1.0 / DV, EPS, ALU.mult, ALU.add).then_inc(o_mean, 1)
                dve.wait_ge(o_root, t + 1)
                inverse_root(hrms, slice(0, H))
                pp = result(dve, f"o{t}")
                if t:
                    dve.wait_ge(job_done, job(f"oT{t - 1}") + 1)
                v.tensor_tensor(heads(norm_r[:, :]), heads(pp[:, 0:512]),
                                hrms[:, 5, :].unsqueeze(2).to_broadcast([P, H, DV]), ALU.mult).then_inc(o_norm, 1)

            def gated(t):
                pp = result(dve, f"oT{t}")
                dve.wait_ge(og_ready, H)
                v.tensor_tensor(yT[:, CH:KC, tile(t)], heads(pp[:, 0:512]), og_sb[:, :, tile(t)], ALU.mult
                                ).then_inc(yb_ready, 1)

            def mixed_lo(t):
                dve.wait_ge(yThi_ready, t + 1)
                v.tensor_tensor(yT_lo[:, :, tile(t)], yT[:, :, tile(t)], yT_hi[:, t % 2, :, :].bitcast(F32),
                                ALU.subtract).then_inc(yTlo_ready, 1)

            for t in range(NT - 1):
                head_norm(t)
                if t + 2 < NT:
                    att_mask(t + 2)
                split_lo("wo0", t)
                if t == NT - 2:
                    mixed_lo(0)
                gated(t)
            head_norm(NT - 1)
            mixed_lo(1)
            gated(NT - 1)
            for j in range(4):
                split_lo("wo1", j)

            dve.wait_ge(g1_ready, 2)

            def high_chunks(t):
                pp = result(dve, f"x2T{t}")
                if t >= 2:
                    dve.wait_ge(job_done, job(f"lg{t - 2}") + 1)
                for k in range(KC // 2, KC):
                    ins = v.tensor_scalar(h2T[t % 2][:, k, :], pp[:, k * P:(k + 1) * P],
                                          scale2[:, k, vec(t):vec(t) + 1], mod[:, 3 * KC + k, vec(t):vec(t) + 1],
                                          ALU.mult, ALU.add)
                ins.then_inc(h2_high, 1)

            def router_row(t):
                pp = result(dve, f"lg{t}")
                v.tensor_copy(logits[:, t, :], pp[:, 0:E]).then_inc(lg_ready, 1)

            dve.wait_ge(scale_ready, 2)
            for t in range(NT):
                if t >= 2:
                    dve.wait_ge(hn_out[t % 2], 16 * (t // 2))
                    dve.wait_ge(job_done, job(f"x2T{t - 2}") + 1)
                pp = pairs[job(f"wo{t}") % 4]
                for half in range(2):
                    cols = slice(512 * half, 512 * half + 512)
                    if half == 0:
                        dve.wait_ge(wo_half, t + 1)
                    else:
                        dve.wait_ge(job_done, job(f"wo{t}") + 1)
                    v.tensor_tensor(xr[:, t % 2, cols], pp[:, cols], gate1b[:, vec(t), cols], ALU.mult
                                    ).then_inc(wo_read, 1)
                    dve.wait_ge(wo_read, 2 * t + half + 1)
                    v.tensor_tensor(x_sb[:, t, cols], x_sb[:, t, cols], xr[:, t % 2, cols], ALU.add).then_inc(x2_ready, 1)
                if 1 <= t < NT - 1:
                    high_chunks(t - 1)
                if t + 2 < NT:
                    mixed_lo(t + 2)
                dve.wait_ge(ss_ready, NT + t + 1)
                mean_square(slice(t, t + 1), mean_ready)
                dve.wait_ge(root_ready, t + 2)
                inverse_root(rms, slice(t, t + 1))
                normalise(t)
                if t >= 2:
                    router_row(t - 2)
                if t == 3:
                    modulation(10)
            high_chunks(NT - 2)
            high_chunks(NT - 1)
            router_row(NT - 2)
            router_row(NT - 1)

            dve.wait_ge(lg_ready, NT)
            dve.wait_ge(job_done, job("wo4") + 1)
            link(v.tensor_reduce(smax[:, 0, :], logits[:, :, :], AX.X, ALU.max))
            v.tensor_tensor(probs[:, :, :], logits[:, :, :], smax[:, 0, :].unsqueeze(2).to_broadcast([P, NT, E]),
                            ALU.subtract).then_inc(smax_ready, 1)
            dve.wait_ge(exp_ready, 1)
            link(v.tensor_reduce(smax[:, 1, :], probs[:, :, :], AX.X, ALU.add))
            link(v.reciprocal(smax[:, 2, :], smax[:, 1, :]))
            v.tensor_tensor(probs[:, :, :], probs[:, :, :], smax[:, 2, :].unsqueeze(2).to_broadcast([P, NT, E]),
                            ALU.mult).then_inc(probs_ready, 1)
            modulation(11)
            pp = result(dve, "pT")
            v.tensor_copy(probsT[:, :], pp[0:E, 0:T]).then_inc(probsT_ready, 1)
            dve.wait_ge(probsT_ready, 1)

            for lo, hi, cap, top_v, top_i in ((0, T_LAT, CAP_L, topv_l, topi_l), (T_LAT, T, CAP_C, topv_c, topi_c)):
                for r in range(cap // 8):
                    eight = slice(8 * r, 8 * r + 8)
                    link(v.max(top_v[:, eight], probsT[:, lo:hi]))
                    v.max_index(top_i[:, eight], top_v[:, eight], probsT[:, lo:hi])
                    if r < cap // 8 - 1:
                        link(v.match_replace(probsT[:, lo:hi], top_v[:, eight], probsT[:, lo:hi], -1.0))

            link(v.memset(selr[:, 4, SLOTS:], 0.0))
            v.tensor_copy(selr[:, 4, 0:CAP_L], topi_l[:, 0:CAP_L])
            v.tensor_scalar(selr[:, 4, CAP_L:SLOTS], topi_c[:, 0:CAP_C], float(T_LAT), None, ALU.add
                            ).then_inc(selr_ready, 1)
            four = lambda ap: ap.rearrange("e (b s) -> e b s", s=32)
            v.memset(selr[:, 0:2, :], 0.0)
            v.memset(selr[:, 2, :], -1.0)
            link(v.memset(selr[:, 3, :], 0.0))
            pp = result(dve, "ixT")
            v.tensor_copy(gather_idx[0:SLOTS, :], pp[0:SLOTS, 0:E]).then_inc(idx_ready, 1)
            for b in range(2):
                v.tensor_copy(selr[:, 0, b * CAP_L:(b + 1) * CAP_L], topi_l[:, 0:CAP_L])
                v.tensor_copy(selr[:, 1, b * CAP_L:(b + 1) * CAP_L], topv_l[:, 0:CAP_L])
            v.tensor_copy(four(selr[:, 2, :])[:, :, 0:CAP_C],
                          topi_c[:, 0:CAP_C].unsqueeze(1).to_broadcast([E, 4, CAP_C]))
            v.tensor_copy(four(selr[:, 3, :])[:, :, 0:CAP_C],
                          topv_c[:, 0:CAP_C].unsqueeze(1).to_broadcast([E, 4, CAP_C])).then_inc(selr_ready, 1)
            pp = result(dve, "pcT")
            src = pp[:, 0:4 * E].rearrange("p (q n two) -> p q n two", q=4, two=2)
            dst = pair_cols[:, :, :].rearrange("p (q o) n -> p q o n", o=2)
            v.tensor_copy(dst[0:64, :, 0, :], src[0:64, :, :, 0])
            v.tensor_copy(dst[0:64, :, 1, :], src[0:64, :, :, 1])
            v.tensor_copy(dst[64:P, :, 0, :], src[64:P, :, :, 1])
            v.tensor_copy(dst[64:P, :, 1, :], src[64:P, :, :, 0]).then_inc(idx_ready, 1)

            def col(q, o, pair):
                return pair_cols[:, 2 * q + o, pair:pair + 1] if isinstance(pair, int) else \
                    pair_cols[:, 2 * q + o, bass.ds(pair, 1)]

            def tokens(e, k):
                dve.wait_ge(xT_lat, e + 1)
                src = pairs[2][:, :].rearrange("p (b n) -> p b n", b=2)[:, :, 0:4 * SLOTS].rearrange(
                    "p b (k s) -> p b k s", s=SLOTS)[:, :, :, CAP_L:SLOTS]
                dst = xT[:, k % 2, :, CAP_L:SLOTS].rearrange("p (b k) s -> p b k s", b=2)
                by = lambda ap: ap.rearrange("p (b k) v -> p b k v", b=2).to_broadcast([P, 2, 4, CAP_C])
                v.tensor_tensor(dst, src, by(scale2[:, :, 1:2]), ALU.mult).then_inc(xT_ctx, 1)
                dve.wait_ge(xT_ctx, 2 * e + 1)
                v.tensor_tensor(dst, dst, by(mod[:, 3 * KC:4 * KC, 1:2]), ALU.add).then_inc(xT_ctx, 1)

            def add_back(base, n):
                t, half = n // 2, n % 2
                cols = slice(half * 512, (half + 1) * 512)
                dve.wait_ge(sc_done, base + n + 1)
                v.tensor_tensor(x_sb[:, t, cols], x_sb[:, t, cols], sc_banks[n % 3], ALU.add).then_inc(sc_added, 1)

            def expert(e, k):
                q = k % 2
                if q == 0 and k > 0:
                    for n in range(6):
                        add_back(5 * e - SC, n)
                dve.wait_ge(silu_lat, e + 1)
                v.tensor_tensor(act_l[:, :], act_l[:, :], up_ps, ALU.mult).then_inc(act_l_ready, 1)
                if q == 0 and k > 0:
                    for n in range(6, 8):
                        add_back(5 * e - SC, n)
                dve.wait_ge(aTp_l, e + 1)
                v.tensor_copy(aT[:, :, :], gate_ps.rearrange("p (j n) -> p j n", j=4)).then_inc(aT_ready, 1)
                dve.wait_ge(silu_ctx, e + 1)
                v.tensor_tensor(act_c[0:64, :], act_c[64:P, :], ctx_ps[64:P, :], ALU.mult).then_inc(act_c_ready, 1)
                if q == 0 and k > 0:
                    for n in range(8, SC):
                        add_back(5 * e - SC, n)
                dve.wait_ge(aTp_c, e + 1)
                v.tensor_copy(aTc[:, :, :], ctx_ps.rearrange("p (j n) -> p j n", j=4)[:, :, 0:64]).then_inc(aTc_ready, 1)
                if k < E - 1:
                    tokens(e + 1, k + 1)
                pair = k // 2 if isinstance(e, int) else pair_of[0]
                if q == 0:
                    dve.wait_ge(iota_ready, 1)
                    for o in range(2):
                        v.tensor_scalar(oh_l[:, o, :], iota_f[:, :], col(0, o, pair), None, ALU.is_equal)
                        ins = v.tensor_scalar(oh_c[:, o, :], iota_f[:, 0:P], col(2, o, pair), None, ALU.is_equal)
                    ins.then_inc(oh_ready, 1)
                for kind in range(2):
                    if kind == 0:
                        dve.wait_ge(dl_done, e + 1)
                    else:
                        dve.wait_ge(d_used, 2 * e + 2)
                    for half in range(2):
                        r = 64 * (half ^ q)
                        v.scalar_tensor_tensor(out=y_f[r:r + 64, kind, half, :], in0=y_ps[kind][r:r + 64, :],
                                               scalar=col(2 * kind + 1, half, pair)[r:r + 64],
                                               in1=gate2b[r:r + 64, kind, half * 512:(half + 1) * 512],
                                               op0=ALU.mult, op1=ALU.mult).then_inc(y_read, 1)
                    if q == 1:
                        dve.wait_ge(yhi_ready, 2 * pair + kind + 1)
                        v.tensor_tensor(y_lo[:, kind, :, :], y_f[:, kind, :, :], y_hi[:, kind, :, :].bitcast(F32),
                                        ALU.subtract).then_inc(ylo_ready, 1)

            pair_of = [0]

            def dve_loop():
                expert(0, 0)
                expert(1, 1)
                with dve.Fori(0, 3) as i:
                    for j in range(2, 6):
                        pair_of[0] = 2 * i + j // 2
                        expert(4 * i + j, j)
                expert(14, 14)
                expert(15, 15)

            dve.wait_ge(g2_ready, 2)
            v.memset(xT[:, :, :, SLOTS:96], 0.0).then_inc(xT_zero, 1)
            tokens(0, 0)
            dve_loop()
            for n in range(SC):
                add_back(SC * (E // 2 - 1), n)
            dve.wait_ge(gfin_in, 16)
            for i, (lo, hi) in enumerate(FINAL_GROUPS):
                dve.wait_ge(fss_ready, hi)
                mean_square(slice(lo, hi), fmean_ready)
                dve.wait_ge(froot_ready, i + 1)
                inverse_root(rms, slice(lo, hi))
                for t in range(lo, hi):
                    v.scalar_tensor_tensor(out=x_sb[:, t, :], in0=x_sb[:, t, :], scalar=rms[:, 5, t:t + 1],
                                           in1=gfin[:, :], op0=ALU.mult, op1=ALU.mult).then_inc(fin_ready, 1)

        @block.tensor
        def _(pe):
            mm, turn = nc.tensor.matmul, nc.tensor.transpose

            def unit_wait(name):
                place, turns = unit_place(name)
                pe.wait_ge(p1_full[place], 16 * (turns + 1))
                return p1w[place]

            done = [0]

            def end(ins, name):
                assert JOBS[done[0]] == name, (JOBS[done[0]], name)
                done[0] += 1
                ins.then_inc(job_done, 1)

            def turn_params():
                pe.wait_ge(prm_in, 160)
                pe.wait_ge(const_ready, 1)
                pp = claim(pe, "prm")
                end(turn(pp[:, 0:R_ALL], param_rows[:, :], ident[0:R_ALL, 0:R_ALL]), "prm")

            def mod_products(u):
                w = unit_wait(f"mod{u}")
                pe.wait_ge(silu_ready, 1)
                pp = claim(pe, f"mod{u}")
                for k in range(KC):
                    g = 32 * (k % 4)
                    ins = mm(pp[g:g + 32, 0:512], silu_c[:, k, :], w[:, k, :], start=k < 4, stop=k >= 4)
                end(ins, f"mod{u}")

            def mod_turn(u):
                pe.wait_ge(modrow_ready, u + 1)
                pp = claim(pe, f"modT{u}")
                for j in range(4):
                    ins = turn(pp[:, tile(j)], mod_rows[:, u % 2, tile(j)], ident[:, :])
                end(ins, f"modT{u}")

            def turn_rows(name, ready, rows):
                pe.wait_ge(xr_ready, ready)
                pp = claim(pe, name)
                for k in range(KC):
                    ins = turn(pp[:, tile(k)], rows[:, tile(k)], ident[:, :])
                end(ins, name)

            def passes(w_hi_part, w_lo_part, tokens_hi_part, tokens_lo_part):
                return ((w_hi_part, tokens_hi_part), (w_hi_part, tokens_lo_part), (w_lo_part, tokens_hi_part))

            def project(name, unit, j):
                pe.wait_ge(wlo_ready, SPLITS.index((unit, j)) + 1)
                lo = w_lo[unit_place(unit)[0]]
                pp = claim(pe, name)
                for k in range(KC):
                    if name == "q0":
                        pe.wait_ge(hT_ready, k + 1)
                    for i, (w, h) in enumerate(passes(w_hi[:, k, tile(j)], lo[:, k, tile(j)], hT_hi[:, k, :],
                                                      hT_lo[:, k, :])):
                        for s in range(2):
                            ins = mm(pp[:, s * 512:s * 512 + HALF], w, h[:, s * HALF:(s + 1) * HALF],
                                     start=k == 0 and i == 0, stop=k == KC - 1 and i == 2)
                end(ins, name)

            def low_rank():
                pe.wait_ge(tail_in, 16)
                pp = claim(pe, "alow")
                for s in range(2):
                    tok = slice(s * HALF, (s + 1) * HALF)
                    for k in range(KC):
                        g = 32 * (k % 4)
                        for i, h in enumerate((hT_hi, hT_lo)):
                            ins = mm(pp[g:g + 32, s * 512:s * 512 + HALF], w_tail[:, k, :],
                                     h[:, k, tok].bitcast(F32), start=k < 4 and i == 0, stop=k >= 4 and i == 1)
                end(ins, "alow")

            def log_decay(h):
                pe.wait_ge(alow_ready, 1)
                pe.wait_ge(tail_in, 144)
                pp = claim(pe, f"la{h}")
                for s in range(2):
                    ins = mm(pp[:, s * 512:s * 512 + HALF], w_decay[:, h, :], a_lowT[:, s * HALF:(s + 1) * HALF],
                             start=True, stop=True)
                end(ins, f"la{h}")

            def values(t):
                lo = w_lo[unit_place("v")[0]]
                pp = claim(pe, f"v{t}")
                for s in range(2):
                    pe.wait_ge(wlo_ready, SPLITS.index(("v", 2 * s + 1)) + 1)
                    cols = slice(256 * s, 256 * s + 256)
                    for k in range(KC):
                        for i, (w, h) in enumerate(passes(w_hi[:, k, cols], lo[:, k, cols],
                                                          hT_hi[:, k, tile(t)], hT_lo[:, k, tile(t)])):
                            ins = mm(pp[:, cols], h, w, start=k == 0 and i == 0, stop=k == KC - 1 and i == 2)
                end(ins, f"v{t}")

            def turn_ks(h):
                pe.wait_ge(ks_ready, h + 1)
                pp = claim(pe, f"ks{h}")
                for t in range(NT):
                    ins = turn(pp[:, tile(t)], ks_row[:, h % 2, tile(t)], ident[:, :])
                end(ins, f"ks{h}")

            turn_params()
            mod_products(0)
            mod_products(1)
            mod_turn(0)
            for t in range(NT):
                turn_rows(f"xT{t}", t + 1, xn[:, t])
            mod_products(2)
            mod_turn(1)
            mod_turn(2)
            mod_products(3)
            mod_turn(3)
            project("q0", "qk", 0)
            project("q1", "qk", 1)
            low_rank()
            project("k0", "qk", 2)
            project("k1", "qk", 3)
            log_decay(0)
            log_decay(1)
            values(0)
            values(1)
            values(2)
            mod_products(4)
            values(3)
            values(4)
            turn_ks(0)
            turn_ks(1)
            mod_turn(4)
            log_decay(2)
            for name, u in (("xc", 5), ("xv", 6), ("xb", 7), ("og", 8)):
                project(f"{name}0", name, 0)
                if name == "xv":
                    log_decay(3)
                project(f"{name}1", name, 1)
                mod_products(u)
                project(f"{name}2", name, 2)
                mod_turn(u)
                project(f"{name}3", name, 3)
                if name == "xc":
                    turn_ks(2)
                elif name == "xv":
                    turn_ks(3)

            pe.wait_ge(ksT_ready, H)
            pe.wait_ge(v_sb_ready, NT)
            for n in KV_ORDER:
                pp = claim(pe, f"kv{n}")
                r = slice(n % 2 * C, n % 2 * C + C)
                for h in range(H):
                    ins = mm(pp[:, tile(h)], ksT[r, n // 2, h, :], v_sb[r, n // 2, tile(h)], start=True, stop=True)
                end(ins, f"kv{n}")

            def attention(t):
                pp = claim(pe, f"att{t}")
                for d in range(2):
                    r = slice(d * DK, (d + 1) * DK)
                    for h in range(H):
                        ins = mm(pp[:, d * 512 + h * P:d * 512 + (h + 1) * P], kd[r, h, tile(t)], qd[r, h, tile(t)],
                                 start=True, stop=True)
                end(ins, f"att{t}")

            def head_outputs(t):
                pe.wait_ge(att_ready, 2 * (t + 1))
                pp = claim(pe, f"o{t}")
                for h in range(H):
                    for d in range(2):
                        mm(pp[:, tile(h)], att_sb[t % 2][:, d, h, :], v_sb[:, t, tile(h)], start=d == 0, stop=False)
                    for j in range(2):
                        n = 2 * t + j
                        ins = mm(pp[j * C:(j + 1) * C, tile(h)], qd[:, h, n * C:(n + 1) * C], states[:, n, h, :],
                                 start=False, stop=True)
                end(ins, f"o{t}")

            def turn_heads(t):
                pe.wait_ge(o_norm, t + 1)
                pp = claim(pe, f"oT{t}")
                for h in range(H):
                    ins = turn(pp[:, tile(h)], norm_r[:, tile(h)], ident[:, :])
                end(ins, f"oT{t}")

            def gate_rows(which, chunk, v):
                pp = claim(pe, f"g{which}_{v}")
                for k in range(KC):
                    ins = mm(pp[:, tile(k)], mod[:, chunk + k, v:v + 1].to_broadcast([P, P]), ident[:, :],
                             start=True, stop=True)
                end(ins, f"g{which}_{v}")

            gate_rows(1, 2 * KC, 0)
            gate_rows(1, 2 * KC, 1)
            attention(0)
            attention(1)
            mod_products(9)
            mod_turn(9)
            pe.wait_ge(state_step, 2 * NCH_LAT)
            head_outputs(0)
            attention(2)
            head_outputs(1)
            attention(3)
            turn_heads(0)
            head_outputs(2)
            attention(4)
            turn_heads(1)
            head_outputs(3)
            turn_heads(2)
            pe.wait_ge(state_step, 2 * NCH_LAT + 2)
            head_outputs(4)
            turn_heads(3)

            def output_projection(t, half):
                pe.wait_ge(yTlo_ready, t + 1)
                pe.wait_ge(wlo_ready, SPLITS.index((f"wo{half}", 3)) + 1)
                pp = claim(pe, f"wo{t}") if half == 0 else pairs[job(f"wo{t}") % 4]
                for k in range(KC):
                    for i, (w, y) in enumerate(passes(wo_hi[half][:, k, :], w_lo[half][:, k, :],
                                                      yT_hi[:, t % 2, k, :], yT_lo[:, k, tile(t)])):
                        ins = mm(pp[:, half * 512:(half + 1) * 512], y, w, start=k == 0 and i == 0,
                                 stop=k == KC - 1 and i == 2)
                if half == 1:
                    end(ins, f"wo{t}")
                else:
                    ins.then_inc(wo_half, 1)

            def router(t):
                pe.wait_ge(h2_low, t + 1)
                pe.wait_ge(h2_high, t + 1)
                pp = claim(pe, f"lg{t}")
                for k in range(KC):
                    ins = mm(pp[:, 0:E], h2T[t % 2][:, k, :], w_router_sb[:, k, :], start=k == 0, stop=k == KC - 1)
                end(ins, f"lg{t}")

            output_projection(0, 0)
            turn_heads(4)
            output_projection(1, 0)
            output_projection(0, 1)
            output_projection(1, 1)
            output_projection(2, 0)
            turn_rows("x2T0", NT + 1, xr[:, 0])
            output_projection(2, 1)
            router(0)
            turn_rows("x2T1", NT + 2, xr[:, 1])
            mod_products(10)
            output_projection(3, 0)
            output_projection(3, 1)
            router(1)
            mod_turn(10)
            turn_rows("x2T2", NT + 3, xr[:, 0])
            output_projection(4, 0)
            output_projection(4, 1)
            turn_rows("x2T3", NT + 4, xr[:, 1])
            router(2)
            mod_products(11)
            turn_rows("x2T4", NT + 5, xr[:, 0])
            router(3)
            router(4)
            mod_turn(11)

            pe.wait_ge(probs_ready, 1)
            pp = claim(pe, "pT")
            for t in range(NT):
                ins = turn(pp[0:E, tile(t)], probs[:, t, :], ident[:, :])
            end(ins, "pT")
            pe.wait_ge(mod_ready, 12)
            gate_rows(2, 5 * KC, 0)
            gate_rows(2, 5 * KC, 1)
            pe.wait_ge(selr_ready, 1)
            pp = claim(pe, "ixT")
            end(turn(pp[:, 0:E], selr[:, 4, :], ident[0:E, 0:E]), "ixT")
            pe.wait_ge(selr_ready, 2)
            pp = claim(pe, "pcT")
            for q in range(4):
                ins = turn(pp[:, q * E:(q + 1) * E], selr[:, q, :], ident[0:E, 0:E])
            end(ins, "pcT")

            def turn_tokens(e, k):
                pe.wait_ge(xs_full[k % 2], 16 * (e // 2 + 1) if isinstance(e, int) else 8 * e + (16 if k % 2 == 0 else 8))
                if k > 0:
                    pe.wait_ge(xT_lat, e)
                    pe.wait_ge(xT_ctx, 2 * e)
                for kk in range(KC):
                    ins = turn(xT_ps(kk), xs[:, k % 2, tile(kk)], ident[0:SLOTS, 0:SLOTS])
                ins.then_inc(xTp_done, 1)

            def scatter(base, n):
                t, half = n // 2, n % 2
                kind = vec(t)
                if n >= 3:
                    pe.wait_ge(sc_added, base + n - 2)
                oh = oh_l[:, half, tile(t)] if kind == 0 else oh_c[:, half, :]
                mm(sc_banks[n % 3], oh, y_hi[:, kind, half, :], start=True, stop=False)
                mm(sc_banks[n % 3], oh, y_lo[:, kind, half, :], start=False, stop=True).then_inc(sc_done, 1)

            def weights(e, k, u):
                n = 6 * k + u
                slot = n % RING_SLOTS
                count = 16 * (n // RING_SLOTS + 1)
                pe.wait_ge(w_full[slot], count if isinstance(e, int) else 12 * (e - k) + count)
                return ring[slot]

            def expert(e, k):
                q = k % 2
                add = q == 0 and k > 0
                base = 5 * e - SC
                xt = xT[:, k % 2]
                pe.wait_ge(xT_lat, e + 1)
                if k > 0:
                    pe.wait_ge(aT_ready, e)
                    pe.wait_ge(aTc_ready, e)
                for half in range(2):
                    wg, wu = weights(e, k, 2 * half), weights(e, k, 2 * half + 1)
                    for j in range(4):
                        kk = 4 * half + j
                        for ps, w in ((gate_ps, wg), (up_ps, wu)):
                            for n in range(2):
                                ins = mm(ps[64 * n:64 * n + 64, :], xt[:, kk, 0:CAP_L], w[:, j, n * 512:(n + 1) * 512],
                                         start=kk == 0, stop=kk == KC - 1)
                    if half == 1:
                        ins.then_inc(gul_done, 1)
                    if add:
                        if half == 0:
                            pe.wait_ge(ylo_ready, e if isinstance(e, int) else 2 * pair_of[0])
                            pe.wait_ge(oh_ready, base // SC + 1 if isinstance(e, int) else pair_of[0])
                            pe.wait_ge(y_read, 4 * e)
                        for n in ((0, 1, 2), (6, 7))[half]:
                            scatter(base, n)
                    if half == 0:
                        pe.wait_ge(xT_ctx, 2 * e + 2)
                    for j in range(4):
                        kk = 4 * half + j
                        for g in range(4):
                            n, w = g % 2, (wg, wu)[g // 2]
                            ins = mm(ctx_ps[32 * g:32 * g + 32, :], xt[:, kk, CAP_L:96], w[:, j, n * 512:(n + 1) * 512],
                                     start=kk == 0, stop=kk == KC - 1)
                        if half == 1 and j == 2:
                            pe.wait_ge(act_l_ready, e + 1)
                            for jl in range(4):
                                turned = turn(gate_ps[:, tile(jl)], act_l[:, tile(jl)], ident[:, :])
                            turned.then_inc(aTp_l, 1)
                    ins.then_inc(gu_used, 1)
                    if add:
                        for n in ((3, 4, 5), (8, 9))[half]:
                            scatter(base, n)
                if k < E - 1:
                    turn_tokens(e + 1, k + 1)
                pe.wait_ge(aT_ready, e + 1)
                if k > 0:
                    pe.wait_ge(y_read, 4 * e)
                if add:
                    pe.wait_ge(sc_added, base + 8)
                for fh in range(2):
                    wd = weights(e, k, 4 + fh)
                    for j in range(4):
                        for n in range(2):
                            r = 64 * (n ^ q)
                            ins = mm(y_ps[0][r:r + 64, :], aT[:, j, 64 * fh:64 * fh + 64],
                                     wd[:, j, n * 512:(n + 1) * 512],
                                     start=fh == 0 and j == 0, stop=fh == 1 and j == 3)
                            if fh == 1 and j == 3 and n == 1:
                                ins.then_inc(dl_done, 1)
                        if fh == 0 and j == 1:
                            pe.wait_ge(act_c_ready, e + 1)
                            for jc in range(4):
                                ins = turn(ctx_ps[:, tile(jc)], act_c[:, tile(jc)], ident[:, :])
                            ins.then_inc(aTp_c, 1)
                    if fh == 0:
                        pe.wait_ge(aTc_ready, e + 1)
                        if add:
                            pe.wait_ge(sc_added, base + SC)
                    for j in range(4):
                        for n in range(2):
                            r = 64 * (n ^ q) + 32 * (j % 2)
                            ins = mm(y_ps[1][r:r + 32, :], aTc[:, j, 32 * fh:32 * fh + 32],
                                     wd[:, j, n * 512:(n + 1) * 512], start=fh == 0 and j < 2, stop=fh == 1 and j >= 2)
                    ins.then_inc(d_used, 1)

            pair_of = [0]
            pe.wait_ge(xT_zero, 1)
            turn_tokens(0, 0)
            expert(0, 0)
            expert(1, 1)
            with pe.Fori(0, 3) as i:
                for j in range(2, 6):
                    pair_of[0] = 2 * i + j // 2
                    expert(4 * i + j, j)
            expert(14, 14)
            expert(15, 15)
            pe.wait_ge(ylo_ready, E - 1)
            for n in range(SC):
                if n == 2:
                    pe.wait_ge(y_read, 4 * E)
                if n == 8:
                    pe.wait_ge(ylo_ready, E)
                scatter(SC * (E // 2 - 1), n)


_INS = ["x_prompt", "x_sample", "state_gla_fwd", "state_gla_bwd", "c", "c_ctx", "w_mod", "b_mod", "g_norm1", "g_norm2",
        "w_in", "w_conv", "b_conv", "w_a_up_f", "b_a_f", "w_a_up_b", "b_a_b", "g_gla_norm", "w_out", "w_router",
        "w_gate", "w_up", "w_down", "g_final"]
_OUTS = [(1, T_CTX, D), (1, T_LAT, D), (1, 1, H, DK, DV), (1, 1, H, DK, DV)]


def kernel(**inputs):
    import numpy as np
    import concourse.bacc as bacc
    from concourse.bass_utils import run_bass_kernel_spmd

    nc = bacc.Bacc("TRN2", target_bir_lowering=False, num_devices=1)
    arrays, args = {}, []
    for name in _INS:
        a = np.ascontiguousarray(inputs[name])
        arrays[f"in_{name}"] = a
        args.append(nc.dram_tensor(f"in_{name}", a.shape, mybir.dt.from_np(a.dtype), kind="ExternalInput").ap())
    for i, shape in enumerate(_OUTS):
        args.append(nc.dram_tensor(f"out_{i}", shape, F32, kind="ExternalOutput").ap())
    build(nc, *args)
    r = run_bass_kernel_spmd(nc, [arrays], core_ids=[0])
    return tuple(r.results[0][f"out_{i}"] for i in range(len(_OUTS)))
```
